# Optimizing a Trainium2 kernel written in Bass

```python
import jax, jax.numpy as jnp
from jax import lax
import numpy as np

D_MODEL = 1024
BATCH = 1
SEQ = 256
DEPTH = 1
DEC_BATCH = 1
DEC_SEQ = 1024
PAST_LEN = 512

GRID_W = 64
D_MIX = D_MODEL
GLA_HEADS = 4
GLA_DV = D_MIX // 2
GLA_DK = GLA_DV // 2
GLA_HK = GLA_DK // GLA_HEADS
GLA_HV = GLA_DV // GLA_HEADS
GLA_RANK = 16
GLA_NORMALIZER = 16.0
CHUNK = 64
CONV_CH = D_MIX - GLA_DV
CONV_K = 31
CONV_PAD = CONV_K // 2
PEER_HEADS = 8
PEER_NKEYS = 128
PEER_N = PEER_NKEYS * PEER_NKEYS
PEER_DQ = 256
PEER_TOPK = 16
PEER_BLOCK = 128
EPS = 1e-6
COL_SIZES = (GLA_DK, GLA_DK, GLA_DV, GLA_DV, GLA_RANK, GLA_RANK, CONV_CH, CONV_CH)
D_IN = sum(COL_SIZES)

kernel_name = "hybrid_gla_conformer_peer_diffusion_step"

def _rmsnorm(x, g):
    xf = x.astype(jnp.float32)
    y = xf * lax.rsqrt(jnp.mean(xf * xf, axis=-1, keepdims=True) + EPS)
    return (y * g.astype(jnp.float32)).astype(x.dtype)

def _layernorm(x, g, b):
    xf = x.astype(jnp.float32)
    mu = jnp.mean(xf, axis=-1, keepdims=True)
    var = jnp.mean(jnp.square(xf - mu), axis=-1, keepdims=True)
    y = (xf - mu) * lax.rsqrt(var + EPS)
    return (y * g.astype(jnp.float32) + b.astype(jnp.float32)).astype(x.dtype)

def _gla_scan(q, k, v, gk, s0):
    B, L, H, _ = q.shape
    n = L // CHUNK
    def to_chunks(t):
        return jnp.moveaxis(t.astype(jnp.float32).reshape(B, n, CHUNK, H, t.shape[-1]), 1, 0)
    mask = jnp.tril(jnp.ones((CHUNK, CHUNK), bool))[None, :, :, None, None]
    def step(S, inp):
        qc, kc, vc, gc = inp
        b = jnp.cumsum(gc, axis=1)
        diff = b[:, :, None] - b[:, None, :]
        decay = jnp.exp(jnp.where(mask, diff, -jnp.inf))
        scores = jnp.einsum('bihk,bijhk,bjhk->bhij', qc, decay, kc)
        o_intra = jnp.einsum('bhij,bjhv->bihv', scores, vc)
        o_inter = jnp.einsum('bihk,bhkv->bihv', qc * jnp.exp(b), S)
        k_dec = kc * jnp.exp(b[:, -1:] - b)
        S_new = jnp.exp(b[:, -1])[..., None] * S + jnp.einsum('bjhk,bjhv->bhkv', k_dec, vc)
        return S_new, o_intra + o_inter
    S_fin, o = lax.scan(step, s0.astype(jnp.float32), (to_chunks(q), to_chunks(k), to_chunks(v), to_chunks(gk)))
    o = jnp.moveaxis(o, 0, 1).reshape(B, L, H, v.shape[-1])
    return o, S_fin

def _gla_bidir(q, k, v, gf, gb, sf0, sb0):
    of, sf = _gla_scan(q, k, v, gf, sf0)
    fl = lambda t: jnp.flip(t, axis=1)
    ob, sb = _gla_scan(fl(q), fl(k), fl(v), fl(gb), sb0)
    return of + fl(ob), sf, sb

def _dwconv_seq(x, w):
    C = x.shape[-1]
    return lax.conv_general_dilated(x, w[:, None, :].astype(x.dtype), (1,), [(CONV_PAD, CONV_PAD)],
                                    dimension_numbers=('NWC', 'WIO', 'NWC'), feature_group_count=C)

def _dwconv_grid(x, w):
    B, L, C = x.shape
    rows = L // GRID_W
    xg = x.reshape(B, rows, GRID_W, C)
    h = C // 2
    wd = w.astype(x.dtype)
    dn = ('NHWC', 'HWIO', 'NHWC')
    xh = lax.conv_general_dilated(xg[..., :h], wd[None, :, None, :h], (1, 1), [(0, 0), (CONV_PAD, CONV_PAD)],
                                  dimension_numbers=dn, feature_group_count=h)
    xv = lax.conv_general_dilated(xg[..., h:], wd[:, None, None, h:], (1, 1), [(CONV_PAD, CONV_PAD), (0, 0)],
                                  dimension_numbers=dn, feature_group_count=C - h)
    return jnp.concatenate([xh, xv], axis=-1).reshape(B, L, C)

def _mixer(h, latent, sf0, sb0, w_in, w_af_up, b_af, w_ab_up, b_ab, gla_norm_g,
           conv_dw_w, conv_dw_b, conv_ln_g, conv_ln_b, conv_pw2, w_out):
    B, L, _ = h.shape
    offs = np.cumsum(COL_SIZES)[:-1].tolist()
    q, k, v, g, af, ab, ca, cb = jnp.split(h @ w_in, offs, axis=-1)
    heads = lambda t, d: t.reshape(B, L, GLA_HEADS, d)
    gf = jax.nn.log_sigmoid((af @ w_af_up + b_af).astype(jnp.float32)) / GLA_NORMALIZER
    gb = jax.nn.log_sigmoid((ab @ w_ab_up + b_ab).astype(jnp.float32)) / GLA_NORMALIZER
    o, sf, sb = _gla_bidir(heads(q * (GLA_HK ** -0.5), GLA_HK), heads(k, GLA_HK), heads(v, GLA_HV),
                           heads(gf, GLA_HK), heads(gb, GLA_HK), sf0, sb0)
    o = o * lax.rsqrt(jnp.mean(o * o, axis=-1, keepdims=True) + EPS)
    o = (o.reshape(B, L, GLA_DV) * gla_norm_g.astype(jnp.float32)).astype(h.dtype) * jax.nn.silu(g)
    u = ca * jax.nn.sigmoid(cb)
    u = (_dwconv_grid(u, conv_dw_w) if latent else _dwconv_seq(u, conv_dw_w)) + conv_dw_b
    u = jax.nn.silu(_layernorm(u, conv_ln_g, conv_ln_b)) @ conv_pw2
    out = jnp.concatenate([o, u], axis=-1) @ w_out
    return out, sf.astype(h.dtype), sb.astype(h.dtype)

def _peer(h, w_q, sub_keys, u_tab, v_tab):
    B, L, D = h.shape
    T = B * L
    xt = h.reshape(T, D)
    qf = (xt @ w_q).astype(jnp.float32).reshape(T, PEER_HEADS, 2, PEER_DQ // 2)
    s = jnp.einsum('thpd,hpnd->thpn', qf, sub_keys.astype(jnp.float32))
    sv, si = lax.top_k(s, PEER_TOPK)
    cand = (sv[:, :, 0, :, None] + sv[:, :, 1, None, :]).reshape(T, PEER_HEADS, PEER_TOPK * PEER_TOPK)
    cidx = (si[:, :, 0, :, None] * PEER_NKEYS + si[:, :, 1, None, :]).reshape(T, PEER_HEADS, PEER_TOPK * PEER_TOPK)
    top_s, pos = lax.top_k(cand, PEER_TOPK)
    idx = jnp.take_along_axis(cidx, pos, axis=-1)
    gate = jax.nn.softmax(top_s, axis=-1).astype(h.dtype)
    nb = T // PEER_BLOCK
    def block(args):
        xb, ib, gb = args
        act = jax.nn.gelu(jnp.einsum('td,thkd->thk', xb, u_tab[ib]), approximate=False)
        return jnp.einsum('thk,thkd->td', gb * act, v_tab[ib])
    out = lax.map(block, (xt.reshape(nb, PEER_BLOCK, D),
                          idx.reshape(nb, PEER_BLOCK, PEER_HEADS, PEER_TOPK),
                          gate.reshape(nb, PEER_BLOCK, PEER_HEADS, PEER_TOPK)))
    return out.reshape(B, L, D)

def _layer(x, mod, latent, sf0, sb0, norm1_g, norm2_g, mw, pw):
    shift1, scale1, gate1, shift2, scale2, gate2 = jnp.split(mod, 6, axis=-1)
    h = _rmsnorm(x, norm1_g) * (1.0 + scale1) + shift1
    m, sf, sb = _mixer(h, latent, sf0, sb0, *mw)
    x = x + gate1 * m
    h = _rmsnorm(x, norm2_g) * (1.0 + scale2) + shift2
    x = x + gate2 * _peer(h, *pw)
    return x, sf, sb

def setup_inputs(seed: int = 0) -> dict:
    key = jax.random.key(seed)
    ks = jax.random.split(key, 32)
    nrm = lambda i, shape, s: jax.random.normal(ks[i], shape, jnp.float32) * s
    D = D_MODEL
    st_shape = (DEC_BATCH, DEPTH, GLA_HEADS, GLA_HK, GLA_HV)
    return {
        'x_prompt': nrm(0, (BATCH, SEQ, D), 1.0),
        'x_sample': nrm(1, (DEC_BATCH, DEC_SEQ, D), 1.0),
        'c': nrm(2, (DEC_BATCH, D), 1.0),
        'state_gla_fwd': nrm(3, st_shape, 0.5),
        'state_gla_bwd': nrm(4, st_shape, 0.5),
        'c_ctx': nrm(5, (D,), 1.0),
        'norm1_g': 1.0 + nrm(6, (DEPTH, D), 0.02),
        'w_mod': nrm(7, (DEPTH, D, 6 * D), 0.5 * D ** -0.5),
        'b_mod': nrm(8, (DEPTH, 6 * D), 0.02),
        'w_in': nrm(9, (DEPTH, D, D_IN), D ** -0.5),
        'w_af_up': nrm(10, (DEPTH, GLA_RANK, GLA_DK), GLA_RANK ** -0.5),
        'b_af': nrm(11, (DEPTH, GLA_DK), 0.1) + 1.0,
        'w_ab_up': nrm(12, (DEPTH, GLA_RANK, GLA_DK), GLA_RANK ** -0.5),
        'b_ab': nrm(13, (DEPTH, GLA_DK), 0.1) + 1.0,
        'gla_norm_g': 1.0 + nrm(14, (DEPTH, GLA_DV), 0.02),
        'conv_dw_w': nrm(15, (DEPTH, CONV_K, CONV_CH), CONV_K ** -0.5),
        'conv_dw_b': nrm(16, (DEPTH, CONV_CH), 0.02),
        'conv_ln_g': 1.0 + nrm(17, (DEPTH, CONV_CH), 0.02),
        'conv_ln_b': nrm(18, (DEPTH, CONV_CH), 0.02),
        'conv_pw2': nrm(19, (DEPTH, CONV_CH, CONV_CH), CONV_CH ** -0.5),
        'w_out': nrm(20, (DEPTH, D_MIX, D), D_MIX ** -0.5),
        'norm2_g': 1.0 + nrm(21, (DEPTH, D), 0.02),
        'peer_wq': nrm(22, (DEPTH, D, PEER_HEADS * PEER_DQ), D ** -0.5),
        'peer_subkeys': nrm(23, (DEPTH, PEER_HEADS, 2, PEER_NKEYS, PEER_DQ // 2), (PEER_DQ // 2) ** -0.5),
        'peer_u': nrm(24, (DEPTH, PEER_N, D), D ** -0.5),
        'peer_v': nrm(25, (DEPTH, PEER_N, D), PEER_HEADS ** -0.5),
        'final_norm_g': 1.0 + nrm(26, (D,), 0.02),
    }

def reference(x_prompt, x_sample, c, state_gla_fwd, state_gla_bwd, c_ctx, norm1_g, w_mod, b_mod,
              w_in, w_af_up, b_af, w_ab_up, b_ab, gla_norm_g, conv_dw_w, conv_dw_b, conv_ln_g,
              conv_ln_b, conv_pw2, w_out, norm2_g, peer_wq, peer_subkeys, peer_u, peer_v, final_norm_g):
    yp, ys = x_prompt, x_sample
    zero_state = jnp.zeros((x_prompt.shape[0], GLA_HEADS, GLA_HK, GLA_HV), jnp.float32)
    new_f, new_b = [], []
    for l in range(DEPTH):
        mw = (w_in[l], w_af_up[l], b_af[l], w_ab_up[l], b_ab[l], gla_norm_g[l], conv_dw_w[l], conv_dw_b[l],
              conv_ln_g[l], conv_ln_b[l], conv_pw2[l], w_out[l])
        pw = (peer_wq[l], peer_subkeys[l], peer_u[l], peer_v[l])
        mod_ctx = jax.nn.silu(c_ctx) @ w_mod[l] + b_mod[l]
        mod_lat = (jax.nn.silu(c) @ w_mod[l] + b_mod[l])[:, None, :]
        yp, sf, sb = _layer(yp, mod_ctx, False, zero_state, zero_state, norm1_g[l], norm2_g[l], mw, pw)
        new_f.append(sf)
        new_b.append(sb)
        ys, _, _ = _layer(ys, mod_lat, True, state_gla_fwd[:, l], state_gla_bwd[:, l],
                          norm1_g[l], norm2_g[l], mw, pw)
    y_prompt = _rmsnorm(yp, final_norm_g)
    y_sample = _rmsnorm(ys, final_norm_g)
    new_state_gla_fwd = jnp.stack(new_f, axis=1)
    new_state_gla_bwd = jnp.stack(new_b, axis=1)
    return (y_prompt, y_sample, new_state_gla_fwd, new_state_gla_bwd)


_drawn_inputs = setup_inputs


def setup_inputs(seed=0):
    import zlib

    import numpy as np

    out = dict(_drawn_inputs(seed))
    spreads = {}
    factors = {'state_gla_fwd': 8.0,
     'state_gla_bwd': 8.0,
     'gla_norm_g': 8.0,
     'conv_dw_b': 7.85,
     'conv_ln_g': 8.0,
     'conv_ln_b': 8.0,
     'norm2_g': 6.366,
     'final_norm_g': 2.798}
    for name, (base, spread) in spreads.items():
        noise = np.random.default_rng([zlib.crc32(name.encode()), seed]).standard_normal(out[name].shape)
        drawn = base * np.exp(spread * noise) if base else spread * noise
        out[name] = __import__('jax').numpy.asarray(drawn.astype(out[name].dtype))
    for name, factor in factors.items():
        out[name] = (out[name] * factor).astype(out[name].dtype)
    return out
```

```python
from contextlib import ExitStack

import concourse.bass as bass
from concourse import mybir

F32 = mybir.dt.float32
U32 = mybir.dt.uint32
ALU = mybir.AluOpType
ACT = mybir.ActivationFunctionType
AX = mybir.AxisListType

P = 128
D = 1024
KD = D // P
EPS = 1e-6
HEADS, HK, HV = 4, 64, 128
PAIRS = HEADS // 2
DK, DV = HEADS * HK, HEADS * HV
RANK = 16
CH = 512
CM = CH // P
TAPS = 31
PAD = TAPS // 2
GRID = 64
PH, NKEYS, TOPK = 8, 128, 16
HP = 2 * PH
SLOTS = PH * TOPK
NEG = -3.0e38
STREAMS = ((0, 2), (2, 10))
NT = STREAMS[1][1]
MAXL = P * (STREAMS[1][1] - STREAMS[1][0])
WSLOTS = 8
RING = 8
GROUP = 4


class Signal:

    def __init__(self, sem, counts):
        self.sem, self.counts, self.n = sem, counts, 0
        self.known = bool(counts)

    def mark(self, key, by=1):
        self.n += by
        self.counts[key] = self.n
        return self.sem, by

    def at(self, key):
        return self.sem, self.counts[key] if self.known else 1


def stream_blocks(s):
    t0, t1 = STREAMS[s]
    n = min(4, t1 - t0)
    return [(s + i, t0 + i * n, n) for i in range((t1 - t0) // n)]


def build(nc, a, counts):
    with ExitStack() as ctx:
        def sb(name, shape, dt=F32):
            return ctx.enter_context(nc.sbuf_tensor(name, shape, dt))

        def scratch(name, shape):
            return nc.dram_tensor(name, shape, F32, kind="Internal").ap()

        def signal(name):
            return Signal(ctx.enter_context(nc.semaphore(name)), counts.setdefault(name, {}))

        mod_d = scratch("mod_d", (2, 6 * D))
        gate2_d = scratch("gate2_d", (NT // 2, D))
        x1_d = scratch("x1_d", (NT * P, D))
        h2_d = scratch("h2_d", (NT * P, D))
        sc_d = scratch("sc_d", ((NT + 1) * P, HP * NKEYS))

        ident = sb("ident", [P, P])
        ones = sb("ones", [P, P])
        keep_f = sb("keep_f", [P, HEADS, P], U32)
        twice_d = sb("twice_d", [P, HEADS, P])
        restart = sb("restart", [P, MAXL])
        iota16 = sb("iota16", [P, TOPK])
        eps = sb("eps", [P, 1])
        cvec = sb("cvec", [P, KD, 2])
        csil = sb("csil", [P, KD, 2])
        modT = sb("modT", [P, 2, KD, 2])
        wup = sb("wup", [2 * RANK, 2, DK])
        bup = sb("bup", [P, 2, PAIRS])
        cw = sb("cw", [P, CM, TAPS])
        cvv = sb("cvv", [P, 3, CM])
        gnb = sb("gnb", [P, DV])
        ss = sb("ss", [P, 2, NT])
        rs = sb("rs", [P, 2, NT])
        oss = sb("oss", [P, NT, HEADS])
        ors = sb("ors", [P, NT, HEADS])
        colsin = sb("colsin", [P, 4, 3, MAXL // P])
        cols = sb("cols", [P, 4, 3, MAXL // P])
        WORDS = 43 * 1024
        arena = sb("arena", [P, WORDS])
        top = [0]

        def take(words):
            top[0] += words
            assert top[0] <= WORDS, top[0]
            return arena[:, top[0] - words:top[0]]

        xb = [take(D) for _ in range(2)]
        junk = take(D)
        hreg = take(KD * MAXL)
        hT = hreg.rearrange("p (k n) -> p k n", k=KD)
        ureg = take(CM * MAXL)
        U = ureg.rearrange("p (m n) -> p m n", m=CM)
        creg = take(CM * MAXL)
        C = creg.rearrange("p (m n) -> p m n", m=CM)
        qkreg = take(4 * MAXL)
        QK = qkreg.rearrange("p (m n) -> p m n", m=4)
        vreg = take(8 * DV)
        V = vreg.rearrange("p (t n) -> p t n", n=DV)
        greg = take(8 * DV)
        SG = greg.rearrange("p (t n) -> p t n", n=DV)
        W = [take(D) for _ in range(WSLOTS)]
        gate1b, a2b, shift2b = take(D), take(D), take(D)
        afT = take(MAXL)
        QF = hreg[:, 0:2 * MAXL].rearrange("p (m n) -> p m n", m=PAIRS)
        KF = hreg[:, 2 * MAXL:4 * MAXL].rearrange("p (m n) -> p m n", m=PAIRS)
        ST = [r.rearrange("p (c d n) -> p c d n", d=PAIRS, n=2 * HV) for r in (hreg[:, 4 * MAXL:8 * MAXL], creg)]
        X1 = hreg.rearrange("p (t n) -> p t n", n=D)
        TMP = creg.rearrange("p (b n) -> p b n", b=4)
        sgt = [junk[:, 0:512], junk[:, 512:1024]]
        rsb = xb[0][:, 0:512]
        kT = [xb[0][:, i * P:(i + 1) * P] for i in range(4)]
        Scur = [xb[1][:, i * P:(i + 1) * P] for i in range(4)]
        Stmp = [xb[1][:, (4 + i) * P:(5 + i) * P] for i in range(4)]
        H2T = greg.rearrange("p (k n) -> p k n", k=KD)
        qfT = [vreg[:, 0:512], vreg[:, 512:1024]]
        skT = vreg[:, 2048:4096].rearrange("p (h n) -> p h n", h=HP)
        scb = [creg[:, i * 2048:(i + 1) * 2048].rearrange("p (t h n) -> p t h n", t=4, h=4) for i in range(2)]
        wmod = [hreg[:, i * 4096:(i + 1) * 4096].rearrange("p (k n) -> p k n", k=KD) for i in range(2)]
        modrow = arena[0:2, 3 * D + 8 * MAXL + 8 * MAXL + 4 * MAXL:3 * D + 20 * MAXL + 6 * D]
        assert 6 * D <= 16 * DV
        bmod = arena[0:2, 3 * D + 8 * MAXL:3 * D + 8 * MAXL + 6 * D]
        grow = arena[0:2, 3 * D + 14 * MAXL:3 * D + 16 * MAXL].rearrange("p (a n) -> p a n", a=2)

        top[0] = 0
        ring = [take(2 * D) for _ in range(RING)]
        h2b = [take(D) for _ in range(2)]
        x1b = [take(D) for _ in range(2)]
        gate2b = [take(D) for _ in range(2)]
        finalb = take(D)
        scr = take(HP * NKEYS)
        oneh = take(SLOTS * TOPK)
        cand = [take(TOPK * TOPK) for _ in range(2)]
        sv = take(HP * TOPK)
        sf = take(HP * TOPK)
        si = take(HP * TOPK).bitcast(U32)
        ts = take(SLOTS)
        pos = take(SLOTS).bitcast(U32)
        pab = [take(SLOTS).bitcast(U32) for _ in range(2)]
        pf = [take(SLOTS) for _ in range(2)]
        pi = [take(SLOTS) for _ in range(2)]
        gsum = take(PH)
        ge = take(SLOTS)
        gate = [take(SLOTS) for _ in range(2)]
        diag = [take(P) for _ in range(RING)]
        dots, gel, wts = take(RING), take(RING), take(RING)
        fss, frs = take(2), take(2)
        idx = [sb(f"idx{i}", [P, SLOTS], U32) for i in range(2)]

        banks = [ctx.enter_context(nc.psum_tensor(f"bank{i}", [P, 512], F32)) for i in range(4)]
        wide = [ctx.enter_context(nc.psum_tensor(f"wide{i}", [P, 2 * 512], F32)) for i in range(2)]

        S = {n: signal(n) for n in (
            "consts", "small_in", "cs_ready", "wmod_in0", "wmod_in1", "mod_rows", "mod_cols", "mod_out", "modT_ready",
            "x_in0", "x_in1", "sumsq", "std_ready", "rstd", "xn_ready", "xT_done", "hT_act", "hT_dve",
            "bank_full", "bank_act", "bank_dve", "tap_done", "centred", "squared", "ln_rstd", "ln_scaled",
            "conv_act", "afT_ready", "az", "softplus", "g_ready", "scan", "span", "cols_in", "exps", "cols_ready",
            "qk_scaled", "kT_done", "st_zero", "st_tmp", "st_kept", "st_next", "state_in", "state_out", "sc_sel", "scT",
            "osum", "ostd", "orstd", "og", "sg_ready", "x1_in", "x1_tmp", "x1_ready", "sumsq2", "std2", "rstd2",
            "h2_pre", "h2_ready", "h2_out0", "h2_out1", "h2T_done", "h2T_act", "h2T_dve", "qf_ready", "sc_out0", "sc_out1",
            "bc_in", "sk_in", "front_done", "scr_in", "tile_in0", "tile_in1", "pick", "gexp_in", "gexp", "idx_ready", "slot_ok",
            "dot", "gelu", "weight", "diag_ready", "slot_used", "y_pre", "y_sum", "y_std", "y_ready", "y_out0", "y_out1", "x_pace", "sp_pace", "act_pace")}
        w_in = [signal(f"w_in{i}") for i in range(WSLOTS)]
        landed = [ctx.enter_context(nc.semaphore(f"landed{i}")) for i in range(RING)]

        def chunks(s):
            for m in range(CM):
                yield ("cb", m)
                yield ("ca", m)
            for m in range(4):
                yield ("qk", m)
            yield ("af", 0)
            for name in ("v", "g"):
                for c in range(4):
                    yield (name, c)
            for c in range(2):
                yield ("pw2", c)
            for half in range(2):
                for c in range(4):
                    yield ("out", 4 * half + c)
            for b, _, _ in stream_blocks(s):
                for hp in range(HP):
                    yield ("wq", (b, hp))

        order = [(s, *c) for s in range(2) for c in chunks(s)]
        at_slot = {c: (n % WSLOTS, n) for n, c in enumerate(order)}

        def last_unit(s, name, part):
            b, _, _ = stream_blocks(s)[-1]
            t = STREAMS[s][1] - 1
            return {"cb": ("cb", part, b), "ca": ("ca", part, b), "qk": ("qk", part, b), "af": ("af", b),
                    "v": ("v", t), "g": ("g", t), "pw2": ("pw2", CM - 1, b),
                    "out": ("out", part // 4 if name == "out" else 0, t),
                    "wq": ("qf", *part) if name == "wq" else None}[name]

        def chunk_source(name, part):
            if name in ("cb", "ca", "qk"):
                m = {"qk": 0, "ca": 4, "cb": 8}[name] + part
                return a["w_cols"][m], D
            if name == "af":
                return a["w_af"], KD * 2 * RANK
            if name in ("v", "g"):
                return a["w_vg"][4 * (name == "g") + part], D
            if name == "pw2":
                return a["w_pw2"][part], D
            if name == "out":
                return a["w_out"][part], D
            return a["w_q"][part[1]], D

        def weights_ready(pe, s, name, part):
            slot, _ = at_slot[(s, name, part)]
            pe.wait_ge(*w_in[slot].at((s, name, part)))
            return W[slot]

        BY_DVE = {"ca", "ln1", "scf", "out", "sc", "mod"}

        def emptied(key):
            if key[0] == "st":
                return S["st_next"].at(key[1:])
            if key[0] == "o":
                return S["og"].at(key[1])
            return S["bank_dve" if key[0] in BY_DVE else "bank_act"].at(key)

        def sct(c):
            return junk[:, (c % 2) * 512:(c % 2 + 1) * 512]

        def by_head(r, odd):
            return r.rearrange("p (a o n) -> p a o n", o=2, n=P)[:, :, odd, :]

        def unit_banks():
            keys = counts["bank_full"]
            return {k: banks[(v - 1) % 4] for k, v in keys.items()}

        def former(d, pair):
            n = PAIRS * d + pair - 1
            return n // PAIRS, n % PAIRS

        block = ctx.enter_context(nc.Block())

        def store_scores(sp, b, tb, n, quad):
            sp.wait_ge(*S["bank_dve"].at(("sc", b, 4 * quad + 3)))
            for j in range(n):
                out = sc_d[(tb + j) * P:(tb + j + 1) * P, quad * 512:(quad + 1) * 512]
                src = scb[quad % 2][:, j, :, :].rearrange("p h n -> p (h n)")
                sp.dma_start(out, src).then_inc(*S[f"sc_out{quad % 2}"].mark((b, quad), 16))
                if tb + j == 0:
                    sp.dma_start(sc_d[NT * P:, quad * 512:(quad + 1) * 512], src
                                 ).then_inc(*S[f"sc_out{quad % 2}"].mark((b, quad), 16))

        @block.sync
        def _(sp):
            n_small = 0
            sp.dma_start(cvec[:], a["c2"]).then_inc(*S["small_in"].mark("c", 16))
            sp.wait_ge(*S["small_in"].at("c"))
            for i in range(2):
                sp.dma_start(bmod[i:i + 1, :], a["b_mod"]).then_inc(*S["small_in"].mark(("b", i), 16))
                sp.dma_start(grow[i:i + 1, 0, :], a["norm1_g"]).then_inc(*S["small_in"].mark(("g1", i), 16))
                sp.dma_start(grow[i:i + 1, 1, :], a["norm2_g"]).then_inc(*S["small_in"].mark(("g2", i), 16))
            for dst, name in ((wup[:], "w_up"), (bup[:], "b_up"), (cw[:], "conv_w"), (cvv[:], "conv_v"),
                              (gnb[:], "gla_g")):
                src = a[name].partition_broadcast(P) if name == "gla_g" else a[name]
                sp.dma_start(dst, src).then_inc(*S["small_in"].mark("all", 16))
            for n in range(12):
                if n >= 2:
                    sp.wait_ge(*S["bank_full"].at(("mod", n - 2)))
                sp.dma_start(wmod[n % 2], a["w_mod"][n]).then_inc(*S[f"wmod_in{n % 2}"].mark(n, 16))
            sp.wait_ge(*S["mod_rows"].at("a2"))
            sp.dma_start(mod_d, modrow).then_inc(*S["mod_out"].mark("rows", 16))
            sp.wait_ge(*S["mod_out"].at("rows"))
            sp.dma_start(gate2_d[0:1, :], mod_d[0:1, 5 * D:6 * D]).then_inc(*S["mod_out"].mark("gate2", 16))
            sp.dma_start(gate2_d[1:NT // 2, :], mod_d[1, 5 * D:6 * D].partition_broadcast(NT // 2 - 1)
                         ).then_inc(*S["mod_out"].mark("gate2", 16))

            for s, (t0, t1) in enumerate(STREAMS):
                queue = [c for c in order if c[0] == s]

                def load_weights(upto):
                    while queue:
                        c = queue.pop(0)
                        slot, n = at_slot[c]
                        if n >= WSLOTS:
                            sp.wait_ge(*S["bank_full"].at(last_unit(*order[n - WSLOTS])))
                        src, words = chunk_source(*c[1:])
                        sp.dma_start(W[slot][:, 0:words], src).then_inc(*w_in[slot].mark(c, 16))
                        if c[1:] == upto:
                            return

                if s == 0:
                    sp.wait_ge(*S["modT_ready"].at(0))
                for t in range(t0, t1):
                    if t >= 2:
                        sp.wait_ge(*(S["xT_done"].at(t - 2) if t >= t0 + 2 else S["h2_out0" if t % 2 == 0 else "h2_out1"].at(t - 2)))
                        if t < t0 + 2:
                            sp.wait_ge(*S["h2T_done"].at(t - 2))
                    sp.dma_start(xb[t % 2], a["x"][t * P:(t + 1) * P, :]).then_inc(*S[f"x_in{t % 2}"].mark(t, 16))
                    if t == t0 + 1:
                        load_weights(("cb", 1))
                for n, (dst, row) in enumerate(((gate1b, 2), (shift2b, 3), (a2b, 4))):
                    if s == 1:
                        sp.wait_ge(*S["h2_ready"].at(t0 - 1))
                    sp.dma_start(dst, mod_d[s, row * D:(row + 1) * D].partition_broadcast(P)
                                 ).then_inc(*S["bc_in"].mark(s, 16))
                load_weights(("pw2", 1))
                if s == 1:
                    sp.wait_ge(*S["xT_done"].at(t1 - 1))
                    for d, name in enumerate(("state_f", "state_b")):
                        for pair in range(PAIRS):
                            sp.dma_start(Scur[2 * d + pair], a[name][pair * P:(pair + 1) * P, :]
                                         ).then_inc(*S["state_in"].mark(s, 16))
                load_weights(("out", 0))
                if s == 0:
                    for d, name in enumerate(("new_f", "new_b")):
                        for pair in range(PAIRS):
                            sp.wait_ge(*S["st_next"].at((s, t1 - t0 - 1, 2 * d + pair)))
                            sp.dma_start(a[name][pair * P:(pair + 1) * P, :], Scur[2 * d + pair]
                                         ).then_inc(*S["state_out"].mark(s, 16))
                load_weights(("out", 3))
                for t in range(t0, t1):
                    sp.wait_ge(*S["bank_full"].at(("o", t1 - 1)))
                    sp.dma_start(X1[:, t - t0, :], a["x"][t * P:(t + 1) * P, :]).then_inc(*S["x1_in"].mark(s, 16))
                load_weights(("out", 7))
                sp.wait_ge(*S["bank_full"].at(("out", 1, t1 - 1)))
                sp.dma_start(skT, a["sk"]).then_inc(*S["sk_in"].mark(s, 16))
                for b, tb, n in stream_blocks(s):
                    load_weights(("wq", (b, 0)))
                    for t in range(tb, tb + n):
                        sp.wait_ge(*S["x1_ready"].at((1, t)))
                        sp.dma_start(x1_d[t * P:(t + 1) * P, :], X1[:, t - t0, :]).then_inc(*S["front_done"].mark("x1", 16))
                        sp.wait_ge(*S["h2_ready"].at(t))
                        sp.dma_start(h2_d[t * P:(t + 1) * P, :], xb[t % 2]).then_inc(*S[f"h2_out{t % 2}"].mark(t, 16))
                    for hp in range(HP):
                        if hp:
                            load_weights(("wq", (b, hp)))
                        if hp >= 4 and hp % 4 == 1:
                            store_scores(sp, b, tb, n, hp // 4 - 1)
                    store_scores(sp, b, tb, n, 3)

            for i in range(2):
                sp.wait_ge(*S[f"h2_out{i}"].at(NT - 2 + i))
                sp.wait_ge(*S[f"sc_out{i}"].at((2, i + 2)))
            sp.wait_ge(*S["front_done"].at("x1"))
            sp.wait_ge(*S["mod_out"].at("gate2"))
            sp.wait_ge(*S["bank_dve"].at(("sc", 2, HP - 1)))
            sp.dma_start(finalb, a["final_g"].partition_broadcast(P)).then_inc(*S["scr_in"].mark("f", 16))
            sp.dma_start(scr, sc_d[0:P, :]).then_inc(*S["scr_in"].mark("0", 16))
            for p in range(2):
                sp.sem_inc(S[f"y_out{p}"].sem, Y_BASE)
            with sp.Fori(0, NT // 2) as i:
                for p in range(2):
                    sp.wait_ge(S[f"y_out{p}"].sem, i * 16 + Y_BASE)
                    sp.sem_inc(S["sp_pace"].sem)
                    row = i * (2 * P) + p * P
                    sp.dma_start(h2b[p], h2_d[bass.ds(row, P), :]).then_inc(S[f"tile_in{p}"].sem, 16)
                    sp.dma_start(x1b[p], x1_d[bass.ds(row, P), :]).then_inc(S[f"tile_in{p}"].sem, 16)
                    sp.dma_start(gate2b[p], gate2_d[bass.ds(i, 1), :].rearrange("a n -> (a n)").partition_broadcast(P)
                                 ).then_inc(S[f"tile_in{p}"].sem, 16)
                    sp.wait_ge(S["idx_ready"].sem, i * 2 + p + 1)
                    sp.sem_inc(S["sp_pace"].sem)
                    sp.dma_start(scr, sc_d[bass.ds(row + P, P), :]).then_inc(S["scr_in"].sem, 16)
            for p in range(2):
                sp.wait_ge(S[f"y_out{p}"].sem, Y_BASE + 16 * NT // 2)
            sp.wait_ge(*S["state_out"].at(0))

        @block.gpsimd
        def _(pool):
            consts = S["consts"]
            pool.memset(ident[:], 0.0).then_inc(*consts.mark("z"))
            pool.memset(twice_d[:], 1.0).then_inc(*consts.mark("z"))
            pool.memset(keep_f[:], 1).then_inc(*consts.mark("z"))
            pool.memset(restart[:], 1.0).then_inc(*consts.mark("z"))
            pool.memset(ones[:], 1.0 / CH).then_inc(*consts.mark("z"))
            pool.memset(eps[:], EPS).then_inc(*consts.mark("z"))
            pool.iota(iota16[:], [[1, TOPK]], base=0, channel_multiplier=0,
                      allow_small_or_imprecise_dtypes=True).then_inc(*consts.mark("z"))
            pool.wait_ge(*consts.at("z"))
            pool.affine_select(out=ident[:], in_=ident[:], compare_op=ALU.not_equal, fill=1.0, base=0,
                               pattern=[[-1, P]], channel_multiplier=1).then_inc(*consts.mark("all"))
            pool.affine_select(out=twice_d[:], in_=twice_d[:], compare_op=ALU.not_equal, fill=2.0, base=0,
                               pattern=[[0, HEADS], [-1, P]], channel_multiplier=1).then_inc(*consts.mark("all"))
            kf = keep_f[:].bitcast(mybir.dt.int32)
            pool.affine_select(out=kf, in_=kf, compare_op=ALU.is_ge, fill=0, base=0,
                               pattern=[[0, HEADS], [1, P]], channel_multiplier=-1).then_inc(*consts.mark("all"))
            pool.affine_select(out=restart[:], in_=restart[:], compare_op=ALU.not_equal, fill=0.0, base=0,
                               pattern=[[0, MAXL // P], [1, P]], channel_multiplier=0).then_inc(*consts.mark("all"))

            with pool.Fori(0, NT // 2) as i:
                for p in range(2):
                    pool.wait_ge(S["idx_ready"].sem, i * 2 + p + 1)
                    pool.sem_inc(S["slot_ok"].sem)
                    for k in range(SLOTS):
                        used = p * SLOTS + k - RING + 1
                        if used > 0:
                            pool.wait_ge(S["slot_used"].sem, i * (2 * SLOTS) + used + 1)
                            pool.sem_inc(S["slot_ok"].sem)
                        elif k == 0:
                            pool.wait_ge(S["slot_used"].sem, i * (2 * SLOTS) + 1)
                            pool.sem_inc(S["slot_ok"].sem)
                        pool.indirect_dma_start(
                            out=ring[k % RING], out_offset=None, in_=a["uv"],
                            in_offset=bass.IndirectOffsetOnAxis(ap=idx[p][:, k:k + 1], axis=0)
                        ).then_inc(landed[k % RING], 16)

        @block.tensor
        def _(pe):
            units = []

            def bank(key):
                n = len(units)
                if n >= 4:
                    pe.wait_ge(*emptied(units[n - 4]))
                units.append(key)
                return banks[n % 4]

            def full(ins, key):
                ins.then_inc(*S["bank_full"].mark(key))

            pe.wait_ge(*S["consts"].at("all"))
            pe.wait_ge(*S["cs_ready"].at(0))
            for n in range(12):
                bk = bank(("mod", n))
                pe.wait_ge(*S[f"wmod_in{n % 2}"].at(n))
                for k in range(KD):
                    ins = pe.matmul(bk[0:2, :], lhsT=csil[:, k, :], rhs=wmod[n % 2][:, k, :],
                                    start=(k == 0), stop=(k == KD - 1))
                full(ins, ("mod", n))
            pe.wait_ge(*S["mod_rows"].at("a2"))
            for which in range(2):
                for k in range(KD):
                    ins = pe.transpose(wide[0][:, (which * KD + k) * 2:(which * KD + k) * 2 + 2],
                                       modrow[:, which * D + k * P:which * D + (k + 1) * P], ident[0:2, 0:2])
            ins.then_inc(*S["mod_cols"].mark(0))
            pe.wait_ge(*S["modT_ready"].at(0))

            for s, (t0, t1) in enumerate(STREAMS):
                blocks = stream_blocks(s)
                for t in range(t0, t1):
                    pe.wait_ge(*S["xn_ready"].at(t))
                    if t >= 2:
                        for e in ("act", "dve"):
                            pe.wait_ge(*S[("hT_" if t >= t0 + 2 else "h2T_") + e].at(t - 2))
                    for k in range(KD):
                        ins = pe.transpose(wide[t % 2][:, k * P:(k + 1) * P], xb[t % 2][:, k * P:(k + 1) * P], ident[:])
                    ins.then_inc(*S["xT_done"].mark(t))
                for e in ("act", "dve"):
                    pe.wait_ge(*S["hT_" + e].at(t1 - 1))

                def project(name, m, b, tb, n):
                    w = weights_ready(pe, s, name, m)
                    cols_ = slice((tb - t0) * P, (tb - t0 + n) * P)
                    key = (name, m, b) if name != "af" else ("af", b)
                    bk = bank(key)
                    M = P if name != "af" else 2 * RANK
                    for k in range(KD):
                        ins = pe.matmul(bk[0:M, 0:n * P], lhsT=w[:, k * M:(k + 1) * M], rhs=hT[:, k, cols_],
                                        start=(k == 0), stop=(k == KD - 1))
                    full(ins, key)

                for m in range(CM):
                    for blk in blocks:
                        project("cb", m, *blk)
                        project("ca", m, *blk)
                for m in range(4):
                    for blk in blocks:
                        project("qk", m, *blk)
                for blk in blocks:
                    project("af", 0, *blk)
                for name in ("v", "g"):
                    for t in range(t0, t1):
                        bk = bank((name, t))
                        for k in range(KD):
                            w = weights_ready(pe, s, name, k // 2)
                            ins = pe.matmul(bk[:], lhsT=hT[:, k, (t - t0) * P:(t - t0 + 1) * P],
                                            rhs=w[:, (k % 2) * 512:(k % 2 + 1) * 512], start=(k == 0), stop=(k == KD - 1))
                        full(ins, (name, t))
                for b, tb, n in blocks:
                    cols_ = slice((tb - t0) * P, (tb - t0 + n) * P)
                    if b == blocks[0][0]:
                        for m in range(CM):
                            pe.wait_ge(*S["tap_done"].at((s, m, TAPS - 1)))
                    bk = bank(("ln1", b))
                    for m in range(CM):
                        ins = pe.matmul(bk[:, 0:n * P], lhsT=ones[:], rhs=C[:, m, cols_], start=(m == 0), stop=(m == CM - 1))
                    full(ins, ("ln1", b))
                    pe.wait_ge(*S["squared"].at(b))
                    bk = bank(("ln2", b))
                    for m in range(CM):
                        ins = pe.matmul(bk[:, 0:n * P], lhsT=ones[:], rhs=U[:, m, cols_], start=(m == 0), stop=(m == CM - 1))
                    full(ins, ("ln2", b))
                    pe.wait_ge(*S["conv_act"].at(b))
                    for m in range(CM):
                        bk = bank(("pw2", m, b))
                        for k in range(CM):
                            w = weights_ready(pe, s, "pw2", k // 2)
                            c0 = (k % 2) * 512 + m * P
                            ins = pe.matmul(bk[:, 0:n * P], lhsT=w[:, c0:c0 + P], rhs=C[:, k, cols_],
                                            start=(k == 0), stop=(k == CM - 1))
                        full(ins, ("pw2", m, b))
                pe.wait_ge(*S["bank_act"].at(("af", blocks[-1][0])))
                for d in range(2):
                    for pair in range(PAIRS):
                        for b, tb, n in blocks:
                            bk = bank(("gz", d, pair, b))
                            ins = pe.matmul(bk[:, 0:n * P], lhsT=wup[:, d, pair * P:(pair + 1) * P],
                                            rhs=afT[0:2 * RANK, (tb - t0) * P:(tb - t0 + n) * P], start=True, stop=True)
                            full(ins, ("gz", d, pair, b))
                pe.wait_ge(*S["qk_scaled"].at((s, 1, PAIRS - 1, 1)))
                steps = t1 - t0
                last = steps if s == 0 else steps - 1
                for i in range(last):
                    for dp in range(4):
                        d, pair = dp // 2, dp % 2
                        c = i if d == 0 else steps - 1 - i
                        K_ = KF[:, pair, :] if d == 0 else QK[:, 2 + pair, :]
                        bk = bank(("kt", s, i, dp))
                        full(pe.transpose(bk[:, 0:P], K_[:, c * P:(c + 1) * P], ident[:]), ("kt", s, i, dp))
                    for dp in range(4):
                        d, pair = dp // 2, dp % 2
                        c = i if d == 0 else steps - 1 - i
                        pe.wait_ge(*S["bank_act"].at(("kt", s, i, dp)))
                        bk = bank(("st", s, i, dp))
                        full(pe.matmul(bk[:, 0:2 * HV], lhsT=kT[dp], rhs=V[:, c, pair * 2 * HV:(pair + 1) * 2 * HV],
                                       start=True, stop=True), ("st", s, i, dp))
                pe.wait_ge(*S["st_kept"].at((s, steps - 1, 3)))

                def out_chunk(c):
                    t = t0 + c
                    pe.wait_ge(*S["scT"].at(t))
                    bk = bank(("o", t))
                    cc = slice(c * P, (c + 1) * P)
                    for h in range(HEADS):
                        pe.matmul(bk[:, h * HV:(h + 1) * HV], lhsT=sct(c)[:, h * P:(h + 1) * P],
                                  rhs=V[:, c, h * HV:(h + 1) * HV], start=(h == 0), stop=False, skip_group_check=True)
                    for pair in range(PAIRS):
                        o = bk[:, pair * 2 * HV:(pair + 1) * 2 * HV]
                        pe.matmul(o, lhsT=QF[:, pair, cc], rhs=ST[0][:, c, pair, :], start=False, stop=False,
                                  skip_group_check=True)
                        ins = pe.matmul(o, lhsT=QK[:, pair, cc], rhs=ST[1][:, c, pair, :], start=False, stop=True,
                                        skip_group_check=True)
                    full(ins, ("o", t))

                def turn_chunk(c):
                    t = t0 + c
                    pe.wait_ge(*S["og"].at(t))
                    bk = bank(("ot", t))
                    for h in range(HEADS):
                        ins = pe.transpose(bk[:, h * P:(h + 1) * P], SG[:, c, h * P:(h + 1) * P], ident[:])
                    full(ins, ("ot", t))

                for c in range(steps + 2):
                    if c < steps:
                        cc = slice(c * P, (c + 1) * P)
                        for name, k_, q_, o_ in (("scb", QK, QK, 2), ("scf", KF, QF, 0)):
                            for odd in range(2):
                                bk = bank((name, odd, t0 + c))
                                rows = slice(odd * HK, (odd + 1) * HK)
                                for pair in range(PAIRS):
                                    ins = pe.matmul(bk[:, pair * P:(pair + 1) * P], lhsT=k_[rows, o_ + pair, cc],
                                                    rhs=q_[rows, pair, cc], start=True, stop=True)
                                full(ins, (name, odd, t0 + c))
                    if 1 <= c <= steps:
                        out_chunk(c - 1)
                    if c >= 2:
                        turn_chunk(c - 2)
                pe.wait_ge(*S["bank_act"].at(("ot", t1 - 1)))
                for half in range(2):
                    for t in range(t0, t1):
                        bk = bank(("out", half, t))
                        c = t - t0
                        for k in range(KD):
                            w = weights_ready(pe, s, "out", 4 * half + k // 2)
                            l = V[:, c, k * P:(k + 1) * P] if k < 4 else U[:, k - 4, c * P:(c + 1) * P]
                            ins = pe.matmul(bk[:], lhsT=l, rhs=w[:, (k % 2) * 512:(k % 2 + 1) * 512],
                                            start=(k == 0), stop=(k == KD - 1))
                        full(ins, ("out", half, t))
                for b, tb, n in blocks:
                    for t in range(tb, tb + n):
                        pe.wait_ge(*S["h2_ready"].at(t))
                        if t >= t0 + 2:
                            for e in ("act", "dve"):
                                pe.wait_ge(*S["h2T_" + e].at(t - 2))
                        for k in range(KD):
                            ins = pe.transpose(wide[t % 2][:, k * P:(k + 1) * P], xb[t % 2][:, k * P:(k + 1) * P], ident[:])
                        ins.then_inc(*S["h2T_done"].mark(t))
                    for e in ("act", "dve"):
                        pe.wait_ge(*S["h2T_" + e].at(tb + n - 1))
                    pe.wait_ge(*S["sk_in"].at(s))
                    for hp in range(HP + 1):
                        if hp < HP:
                            w = weights_ready(pe, s, "wq", (b, hp))
                            bk = bank(("qf", b, hp))
                            for k in range(KD):
                                ins = pe.matmul(bk[:, 0:n * P], lhsT=w[:, k * P:(k + 1) * P], rhs=H2T[:, k, 0:n * P],
                                                start=(k == 0), stop=(k == KD - 1))
                            full(ins, ("qf", b, hp))
                        if hp:
                            pe.wait_ge(*S["bank_act"].at(("qf", b, hp - 1)))
                            bk = bank(("sc", b, hp - 1))
                            for j in range(n):
                                ins = pe.matmul(bk[:, j * P:(j + 1) * P], lhsT=qfT[(hp - 1) % 2][:, j * P:(j + 1) * P],
                                                rhs=skT[:, hp - 1, :], start=True, stop=True)
                            full(ins, ("sc", b, hp - 1))

            for e in ("act", "dve"):
                pe.wait_ge(*S["h2T_" + e].at(NT - 1))

            def add_rows(i, p, g, first):
                for r in range(RING):
                    pe.wait_ge(S["diag_ready"].sem, i * (2 * SLOTS) + p * SLOTS + g * RING + r + 1)
                    for c in range(2):
                        ins = pe.matmul(wide[p][:, c * 512:(c + 1) * 512], lhsT=diag[r],
                                        rhs=ring[r][:, D + c * 512:D + (c + 1) * 512],
                                        start=(first and r == 0), stop=(r == RING - 1), skip_group_check=True)
                    ins.then_inc(S["slot_used"].sem, 1)

            pe.sem_inc(S["slot_used"].sem)
            with pe.Fori(0, NT // 2) as i:
                for p in range(2):
                    if p == 0:
                        pe.wait_ge(S["y_ready"].sem, i * 2 + 1)
                    add_rows(i, p, 0, True)
                    with pe.Fori(1, SLOTS // RING) as g:
                        add_rows(i, p, g, False)

        @block.scalar
        def _(act):
            def drained(ins, key):
                ins.then_inc(*S["bank_act"].mark(key))

            bank_of = unit_banks()

            def wait_full(key):
                act.wait_ge(*S["bank_full"].at(key))
                return bank_of[key]

            act.wait_ge(*S["small_in"].at("c"))
            act.activation(csil[:], cvec[:], ACT.Silu).then_inc(*S["cs_ready"].mark(0))
            act.wait_ge(*S["consts"].at("all"))

            def mean_square(src, sqname, t, col, stdname):
                act.activation(junk, src, ACT.Square, accum_out=ss[:, col, t:t + 1]).then_inc(*S[sqname].mark(t))
                act.wait_ge(*S[sqname].at(t))
                act.activation(rs[:, col, t:t + 1], ss[:, col, t:t + 1], ACT.Sqrt, bias=eps[:], scale=1.0 / D
                               ).then_inc(*S[stdname].mark(t))

            for s, (t0, t1) in enumerate(STREAMS):
                blocks = stream_blocks(s)
                if s == 0:
                    act.wait_ge(*S["modT_ready"].at(0))
                for t in range(t0, t1 + 1):
                    if t < t1:
                        act.wait_ge(*S[f"x_in{t % 2}"].at(t))
                        mean_square(xb[t % 2], "sumsq", t, 0, "std_ready")
                    if t > t0:
                        u = t - 1
                        act.wait_ge(*S["xT_done"].at(u))
                        for k in range(KD // 2):
                            ins = act.activation(hT[:, k, (u - t0) * P:(u - t0 + 1) * P], wide[u % 2][:, k * P:(k + 1) * P],
                                                 ACT.Identity, bias=modT[:, 0, k, s:s + 1], scale=modT[:, 1, k, s:s + 1])
                        ins.then_inc(*S["hT_act"].mark(u))
                n_, before = 0, []
                for m in range(CM):
                    for b, tb, n in blocks:
                        bk = wait_full(("cb", m, b))
                        if n_ >= 2:
                            act.wait_ge(*S["bank_dve"].at(before[n_ - 2]))
                        before.append(("ca", m, b))
                        drained(act.activation(sgt[n_ % 2][:, 0:n * P], bk[:, 0:n * P], ACT.Sigmoid), ("cb", m, b))
                        n_ += 1
                for m in range(4):
                    for b, tb, n in blocks:
                        bk = wait_full(("qk", m, b))
                        drained(act.activation(QK[:, m, (tb - t0) * P:(tb - t0 + n) * P], bk[:, 0:n * P], ACT.Copy,
                                               scale=HK ** -0.5 if m < 2 else 1.0), ("qk", m, b))
                for b, tb, n in blocks:
                    bk = wait_full(("af", b))
                    drained(act.activation(afT[0:2 * RANK, (tb - t0) * P:(tb - t0 + n) * P], bk[0:2 * RANK, 0:n * P],
                                           ACT.Copy), ("af", b))
                for t in range(t0, t1):
                    bk = wait_full(("v", t))
                    drained(act.activation(V[:, t - t0, :], bk[:], ACT.Copy), ("v", t))
                for t in range(t0, t1):
                    bk = wait_full(("g", t))
                    drained(act.activation(SG[:, t - t0, :], bk[:], ACT.Silu), ("g", t))
                for b, tb, n in blocks:
                    cols_ = slice((tb - t0) * P, (tb - t0 + n) * P)
                    act.wait_ge(*S["bank_dve"].at(("ln1", b)))
                    for m in range(CM):
                        ins = act.activation(U[:, m, cols_], C[:, m, cols_], ACT.Square)
                    ins.then_inc(*S["squared"].mark(b))
                    bk = wait_full(("ln2", b))
                    drained(act.activation(rsb[:, 0:n * P], bk[:, 0:n * P], ACT.Sqrt, bias=eps[:]), ("ln2", b))
                    act.wait_ge(*S["ln_scaled"].at(b))
                    for m in range(CM):
                        ins = act.activation(C[:, m, cols_], C[:, m, cols_], ACT.Silu, bias=cvv[:, 2, m:m + 1],
                                             scale=cvv[:, 1, m:m + 1])
                    ins.then_inc(*S["conv_act"].mark(b))
                    for m in range(CM):
                        bk = wait_full(("pw2", m, b))
                        drained(act.activation(U[:, m, cols_], bk[:, 0:n * P], ACT.Copy), ("pw2", m, b))
                for d in range(2):
                    for pair in range(PAIRS):
                        key = (s, d, pair)
                        L = (t1 - t0) * P
                        for b, tb, n in blocks:
                            cols_ = slice((tb - t0) * P, (tb - t0 + n) * P)
                            bk = wait_full(("gz", d, pair, b))
                            if (d, pair) == (0, 0):
                                act.wait_ge(*S["bank_full"].at(("pw2", CM - 1, blocks[-1][0])))
                            else:
                                act.wait_ge(*S["qk_scaled"].at((s, *former(d, pair), 1)))
                            act.activation(TMP[:, 1, cols_], bk[:, 0:n * P], ACT.Abs, bias=bup[:, d, pair:pair + 1]
                                           ).then_inc(*S["az"].mark((*key, b)))
                            drained(act.activation(TMP[:, 0, cols_], bk[:, 0:n * P], ACT.Identity,
                                                   bias=bup[:, d, pair:pair + 1]), ("gz", d, pair, b))
                        act.wait_ge(*S["az"].at((*key, blocks[-1][0])))
                        act.activation(TMP[:, 1, 0:L], TMP[:, 1, 0:L], ACT.Exp, scale=-1.0).then_inc(*S["softplus"].mark((*key, 0)))
                        act.wait_ge(*S["softplus"].at((*key, 0)))
                        act.activation(TMP[:, 1, 0:L], TMP[:, 1, 0:L], ACT.Ln, bias=1.0).then_inc(*S["softplus"].mark((*key, 1)))
                        act.wait_ge(*S["cols_in"].at(key))
                        dp = 2 * d + pair
                        act.activation(cols[:, dp, :, 0:t1 - t0], colsin[:, dp, :, 0:t1 - t0], ACT.Exp, scale=1.0 / RANK
                                       ).then_inc(*S["cols_ready"].mark(key))
                        act.activation(TMP[:, 3, 0:L], TMP[:, 2, 0:L], ACT.Exp, scale=-1.0 / RANK).then_inc(*S["exps"].mark((*key, 0)))
                        act.activation(TMP[:, 2, 0:L], TMP[:, 2, 0:L], ACT.Exp, scale=1.0 / RANK).then_inc(*S["exps"].mark((*key, 1)))
                steps = t1 - t0
                last = steps if s == 0 else steps - 1
                act.wait_ge(*S["ln_scaled"].at(blocks[-1][0]))
                for i in range(last):
                    for dp in range(4):
                        bk = wait_full(("kt", s, i, dp))
                        if i:
                            act.wait_ge(*S["bank_full"].at(("st", s, i - 1, dp)))
                        drained(act.activation(kT[dp], bk[:, 0:P], ACT.Copy), ("kt", s, i, dp))
                def o_stats(c):
                    t = t0 + c
                    bk = wait_full(("o", t))
                    for h in range(HEADS):
                        if h or c:
                            act.wait_ge(*S["osum"].at((t, h - 1) if h else (t - 1, HEADS - 1)))
                        act.activation(xb[0][:, 512:640], bk[:, h * HV:(h + 1) * HV], ACT.Square,
                                       accum_out=oss[:, t, h:h + 1]).then_inc(*S["osum"].mark((t, h)))
                    act.wait_ge(*S["osum"].at((t, HEADS - 1)))
                    act.activation(ors[:, t, :], oss[:, t, :], ACT.Sqrt, bias=eps[:], scale=1.0 / HV
                                   ).then_inc(*S["ostd"].mark(t))

                def turn_out(c):
                    t = t0 + c
                    bk = wait_full(("ot", t))
                    drained(act.activation(V[:, c, :], bk[:], ACT.Copy), ("ot", t))

                for c in range(steps + 2):
                    if c < steps:
                        if c >= 2:
                            act.wait_ge(*S["bank_full"].at(("o", t0 + c - 2)))
                        for odd in range(2):
                            bk = wait_full(("scb", odd, t0 + c))
                            drained(act.activation(by_head(sct(c), odd), bk[:, 0:2 * P].rearrange("p (a n) -> p a n", n=P),
                                                   ACT.Copy), ("scb", odd, t0 + c))
                    if 1 <= c <= steps:
                        o_stats(c - 1)
                    if c >= 2:
                        turn_out(c - 2)
                for b, tb, n in blocks:
                    for t in range(tb, tb + n + 1):
                        if t < tb + n:
                            act.wait_ge(*S["x1_ready"].at((1, t)))
                            mean_square(X1[:, t - t0, :], "sumsq2", t, 1, "std2")
                        if t > tb:
                            u = t - 1
                            act.wait_ge(*S["h2T_done"].at(u))
                            if b > blocks[0][0]:
                                act.wait_ge(*S["bank_full"].at(("qf", b - 1, HP - 1)))
                            cc = slice((u - tb) * P, (u - tb + 1) * P)
                            ins = act.activation(H2T[:, 0:4, cc], wide[u % 2][:, 0:512].rearrange("p (k n) -> p k n", k=4), ACT.Copy)
                            ins.then_inc(*S["h2T_act"].mark(u))
                    for hp in range(HP):
                        bk = wait_full(("qf", b, hp))
                        if hp >= 2:
                            act.wait_ge(*S["bank_full"].at(("sc", b, hp - 2)))
                        elif b > blocks[0][0]:
                            act.wait_ge(*S["bank_full"].at(("sc", b - 1, HP - 2 + hp)))
                        drained(act.activation(qfT[hp % 2][:, 0:n * P], bk[:, 0:n * P], ACT.Copy), ("qf", b, hp))

            def softmax_exp():
                act.activation(ge, ge, ACT.Exp).then_inc(S["gexp"].sem, 1)

            def group(i, p, g):
                for half in range(RING // GROUP):
                    j = half * GROUP
                    act.wait_ge(S["dot"].sem, i * (2 * SLOTS) + p * SLOTS + g * RING + j + GROUP)
                    act.activation(gel[:, j:j + GROUP], dots[:, j:j + GROUP], ACT.Gelu).then_inc(S["gelu"].sem, 1)
                    act.wait_ge(S["weight"].sem, i * (2 * SLOTS // GROUP) + p * (SLOTS // GROUP) + g * (RING // GROUP) + half + 1)
                    for r in range(j, j + GROUP):
                        act.activation(diag[r], ident[:], ACT.Copy, scale=wts[:, r:r + 1]).then_inc(S["diag_ready"].sem, 1)

            act.wait_ge(S["gexp_in"].sem, 1)
            softmax_exp()
            with act.Fori(0, NT // 2) as i:
                for p in range(2):
                    with act.Fori(0, PICK_DONE) as g:
                        group(i, p, g)
                    act.wait_ge(S["gexp_in"].sem, i * 2 + p + 2)
                    softmax_exp()
                    with act.Fori(PICK_DONE, SLOTS // RING) as g:
                        group(i, p, g)
                    act.wait_ge(S["y_pre"].sem, i * 4 + 2 * p + 2)
                    act.activation(oneh[:, 0:D], x1b[p], ACT.Square, accum_out=fss[:, p:p + 1]).then_inc(S["y_sum"].sem, 1)
                    act.wait_ge(S["y_sum"].sem, i * 2 + p + 1)
                    act.activation(frs[:, p:p + 1], fss[:, p:p + 1], ACT.Sqrt, bias=eps[:], scale=1.0 / D
                                   ).then_inc(S["y_std"].sem, 1)
                    act.wait_ge(S["y_ready"].sem, i * 2 + p + 2)
                    act.sem_inc(S["act_pace"].sem)
                    act.dma_start(a["y"][bass.ds(i * (2 * P) + p * P, P), :], x1b[p]).then_inc(S[f"y_out{p}"].sem, 16)

        @block.vector
        def _(dve):
            def drained(ins, key):
                ins.then_inc(*S["bank_dve"].mark(key))

            bank_of = unit_banks()

            def wait_full(key):
                dve.wait_ge(*S["bank_full"].at(key))
                return bank_of[key]

            dve.wait_ge(*S["consts"].at("all"))
            dve.wait_ge(*S["small_in"].at("all"))
            for n in range(12):
                bk = wait_full(("mod", n))
                drained(dve.tensor_tensor(modrow[:, n * 512:(n + 1) * 512], bk[0:2, :], bmod[:, n * 512:(n + 1) * 512],
                                          ALU.add), ("mod", n))
            dve.wait_ge(*S["bank_dve"].at(("mod", 11)))
            for name, at, g in (("a1", 1, 0), ("a2", 4, 1)):
                r = modrow[:, at * D:(at + 1) * D]
                dve.scalar_tensor_tensor(out=r, in0=r, scalar=1.0, in1=grow[:, g, :], op0=ALU.add, op1=ALU.mult
                                         ).then_inc(*S["mod_rows"].mark(name))
            dve.wait_ge(*S["mod_cols"].at(0))
            dve.tensor_copy(modT[:].rearrange("p a k s -> p (a k s)"), wide[0][:, 0:4 * KD]).then_inc(*S["modT_ready"].mark(0))

            for s, (t0, t1) in enumerate(STREAMS):
                blocks = stream_blocks(s)
                L = (t1 - t0) * P
                for t in range(t0, t1 + 1):
                    if t < t1:
                        dve.wait_ge(*S["std_ready"].at(t))
                        dve.reciprocal(rs[:, 0, t:t + 1], rs[:, 0, t:t + 1]).then_inc(*S["rstd"].mark(t))
                        dve.wait_ge(*S["rstd"].at(t))
                        dve.tensor_scalar(xb[t % 2], xb[t % 2], rs[:, 0, t:t + 1], None, ALU.mult).then_inc(*S["xn_ready"].mark(t))
                    if t > t0:
                        u = t - 1
                        dve.wait_ge(*S["xT_done"].at(u))
                        if u == 0:
                            dve.wait_ge(*S["modT_ready"].at(0))
                        for k in range(KD // 2, KD):
                            ins = dve.tensor_scalar(hT[:, k, (u - t0) * P:(u - t0 + 1) * P], wide[u % 2][:, k * P:(k + 1) * P],
                                                    modT[:, 1, k, s:s + 1], modT[:, 0, k, s:s + 1], ALU.mult, ALU.add)
                        ins.then_inc(*S["hT_dve"].mark(u))
                n_ = 0
                for m in range(CM):
                    for b, tb, n in blocks:
                        bk = wait_full(("ca", m, b))
                        dve.wait_ge(*S["bank_act"].at(("cb", m, b)))
                        drained(dve.tensor_tensor(U[:, m, (tb - t0) * P:(tb - t0 + n) * P], bk[:, 0:n * P],
                                                  sgt[n_ % 2][:, 0:n * P], ALU.mult), ("ca", m, b))
                        n_ += 1
                dve.wait_ge(*S["bank_dve"].at(("ca", CM - 1, blocks[-1][0])))
                offsets = [0] + [d for k in range(1, PAD + 1) for d in (-k, k)]
                for j, d in enumerate(offsets):
                    for m in range(CM):
                        w = cw[:, m, d + PAD:d + PAD + 1]
                        if j:
                            dve.wait_ge(*S["tap_done"].at((s, m, j - 1)))
                        if s == 0:
                            lo, hi = max(0, -d), min(L, L - d)
                            o, x = C[:, m, lo:hi], U[:, m, lo + d:hi + d]
                        elif m < CM // 2:
                            lo, hi = max(0, -d), min(GRID, GRID - d)
                            g_ = lambda r: r[:, m, 0:L].rearrange("p (r c) -> p r c", c=GRID)
                            o, x = g_(C)[:, :, lo:hi], g_(U)[:, :, lo + d:hi + d]
                        else:
                            lo, hi = max(0, -d) * GRID, min(L, L - d * GRID)
                            o, x = C[:, m, lo:hi], U[:, m, lo + d * GRID:hi + d * GRID]
                        if j == 0:
                            dve.tensor_scalar(o, x, w, cvv[:, 0, m:m + 1], ALU.mult, ALU.add
                                              ).then_inc(*S["tap_done"].mark((s, m, j)))
                        else:
                            dve.scalar_tensor_tensor(out=o, in0=x, scalar=w, in1=o, op0=ALU.mult, op1=ALU.add
                                                     ).then_inc(*S["tap_done"].mark((s, m, j)))
                for t in range(t0, t1):
                    dve.wait_ge(*S["bank_act"].at(("g", t)))
                    dve.tensor_tensor(SG[:, t - t0, :], SG[:, t - t0, :], gnb[:], ALU.mult).then_inc(*S["sg_ready"].mark(t))
                for b, tb, n in blocks:
                    cols_ = slice((tb - t0) * P, (tb - t0 + n) * P)
                    bk = wait_full(("ln1", b))
                    for m in range(CM):
                        ins = dve.tensor_tensor(C[:, m, cols_], C[:, m, cols_], bk[:, 0:n * P], ALU.subtract)
                    drained(ins, ("ln1", b))
                    dve.wait_ge(*S["bank_act"].at(("ln2", b)))
                    dve.reciprocal(rsb[:, 0:n * P], rsb[:, 0:n * P]).then_inc(*S["ln_rstd"].mark(b))
                    dve.wait_ge(*S["ln_rstd"].at(b))
                    for m in range(CM):
                        ins = dve.tensor_tensor(C[:, m, cols_], C[:, m, cols_], rsb[:, 0:n * P], ALU.mult)
                    ins.then_inc(*S["ln_scaled"].mark(b))
                nt = t1 - t0
                for d in range(2):
                    for pair in range(PAIRS):
                        key, dp = (s, d, pair), 2 * d + pair
                        z, l, x = TMP[:, 0, 0:L], TMP[:, 1, 0:L], TMP[:, 2, 0:L]
                        xc, lc = (r.rearrange("p (c n) -> p c n", n=P) for r in (x, l))
                        ci = colsin[:, dp, :, 0:nt]
                        dve.wait_ge(*S["softplus"].at((*key, 1)))
                        dve.scalar_tensor_tensor(out=z, in0=z, scalar=0.0, in1=l, op0=ALU.min, op1=ALU.subtract
                                                 ).then_inc(*S["g_ready"].mark(key))
                        dve.wait_ge(*S["g_ready"].at(key))
                        dve.tensor_tensor_scan(l, restart[:, 0:L], z, 0.0, ALU.mult, ALU.add).then_inc(*S["scan"].mark(key))
                        dve.wait_ge(*S["scan"].at(key))
                        if d == 0:
                            mid = lc[:, :, P // 2 - 1:P // 2]
                            end = lc[:, :, P - 1]
                            dve.tensor_copy(ci[:, 0, :], mid.rearrange("p c n -> p (c n)"))
                            dve.tensor_copy(ci[:, 1, :], end)
                            dve.tensor_tensor(ci[:, 2, :], end, mid.rearrange("p c n -> p (c n)"), ALU.subtract)
                            dve.tensor_tensor(xc, lc, mid.to_broadcast([P, nt, P]), ALU.subtract
                                              ).then_inc(*S["cols_in"].mark(key))
                        else:
                            dve.tensor_tensor(z, z, l, ALU.subtract).then_inc(*S["span"].mark(key))
                            dve.wait_ge(*S["span"].at(key))
                            zc = z.rearrange("p (c n) -> p c n", n=P)
                            mid = zc[:, :, P // 2:P // 2 + 1]
                            end = lc[:, :, P - 1]
                            dve.tensor_tensor(ci[:, 0, :], end, mid.rearrange("p c n -> p (c n)"), ALU.add)
                            dve.tensor_copy(ci[:, 1, :], end)
                            dve.tensor_scalar(ci[:, 2, :], mid.rearrange("p c n -> p (c n)"), -1.0, None, ALU.mult)
                            dve.tensor_tensor(xc, zc, mid.to_broadcast([P, nt, P]), ALU.subtract
                                              ).then_inc(*S["cols_in"].mark(key))
                        Q_, K_ = (QF, KF) if d == 0 else (QK, QK[:, 2:4, :])
                        dve.wait_ge(*S["exps"].at((*key, 0)))
                        if d == 0:
                            dve.wait_ge(*S["bank_full"].at(("g", t1 - 1)))
                        dve.tensor_tensor(K_[:, pair, 0:L], QK[:, 2 + pair, 0:L], TMP[:, 3, 0:L], ALU.mult
                                          ).then_inc(*S["qk_scaled"].mark((*key, 0)))
                        dve.wait_ge(*S["exps"].at((*key, 1)))
                        dve.tensor_tensor(Q_[:, pair, 0:L], QK[:, pair, 0:L], TMP[:, 2, 0:L], ALU.mult
                                          ).then_inc(*S["qk_scaled"].mark((*key, 1)))
                if s == 0:
                    dve.wait_ge(*S["xT_done"].at(t1 - 1))
                    for dp in range(4):
                        dve.memset(Scur[dp], 0.0).then_inc(*S["st_next"].mark((s, -1, dp)))
                else:
                    dve.wait_ge(*S["state_in"].at(s))
                last = nt if s == 0 else nt - 1
                dve.wait_ge(*S["cols_ready"].at((s, 1, 1)))
                dve.wait_ge(*S["qk_scaled"].at((s, 1, PAIRS - 1, 1)))
                for d in range(2):
                    dve.memset(ST[d][:, 0:nt].rearrange("p c d n -> p (c d n)"), 0.0).then_inc(*S["st_zero"].mark(s))
                dve.wait_ge(*S["st_zero"].at(s))
                for i in range(nt):
                    for dp in range(4):
                        c = i if dp < 2 else nt - 1 - i
                        T_ = cols[:, dp, 1, c:c + 1]
                        if i or s == 0:
                            dve.wait_ge(*S["st_next"].at((s, i - 1, dp)))
                        for r in range(2):
                            h = slice(r * HK, (r + 1) * HK)
                            ins = dve.tensor_scalar(ST[dp // 2][h, c, dp % 2, r * HV:(r + 1) * HV], Scur[dp][h, :],
                                                    cols[h, dp, 0, c:c + 1], None, ALU.mult)
                        ins.then_inc(*S["st_kept"].mark((s, i, dp)))
                        if i < last:
                            dve.tensor_scalar(Stmp[dp], Scur[dp], T_, None, ALU.mult).then_inc(*S["st_tmp"].mark((s, i, dp)))
                    if i < last:
                        for dp in range(4):
                            c = i if dp < 2 else nt - 1 - i
                            bk = wait_full(("st", s, i, dp))
                            dve.wait_ge(*S["st_tmp"].at((s, i, dp)))
                            dve.wait_ge(*S["st_kept"].at((s, i, dp)))
                            for r in range(2):
                                h = slice(r * HK, (r + 1) * HK)
                                ins = dve.scalar_tensor_tensor(out=Scur[dp][h, :], in0=bk[h, r * HV:(r + 1) * HV],
                                                               scalar=cols[h, dp, 2, c:c + 1], in1=Stmp[dp][h, :],
                                                               op0=ALU.mult, op1=ALU.add)
                                if r == 0:
                                    ins.then_inc(*S["st_next"].mark((s, i, dp, "half")))
                                else:
                                    ins.then_inc(*S["st_next"].mark((s, i, dp)))
                def normalise(c):
                    t = t0 + c
                    dve.wait_ge(*S["ostd"].at(t))
                    dve.reciprocal(ors[:, t, :], ors[:, t, :]).then_inc(*S["orstd"].mark(t))
                    dve.wait_ge(*S["orstd"].at(t))
                    dve.wait_ge(*S["sg_ready"].at(t))
                    bk = bank_of[("o", t)]
                    for h in range(HEADS):
                        hc = slice(h * HV, (h + 1) * HV)
                        ins = dve.scalar_tensor_tensor(out=SG[:, c, hc], in0=bk[:, hc], scalar=ors[:, t, h:h + 1],
                                                       in1=SG[:, c, hc], op0=ALU.mult, op1=ALU.mult)
                    ins.then_inc(*S["og"].mark(t))

                for c in range(nt + 1):
                    if c < nt:
                        for odd in range(2):
                            bk = wait_full(("scf", odd, t0 + c))
                            dve.wait_ge(*S["bank_act"].at(("scb", odd, t0 + c)))
                            drained(dve.copy_predicated(by_head(sct(c), odd), keep_f[:, 0:2, :],
                                                        bk[:, 0:2 * P].rearrange("p (a n) -> p a n", n=P)),
                                    ("scf", odd, t0 + c))
                        dve.wait_ge(*S["bank_dve"].at(("scf", 1, t0 + c)))
                        dve.tensor_tensor(sct(c), sct(c), twice_d[:].rearrange("p h n -> p (h n)"), ALU.mult
                                          ).then_inc(*S["scT"].mark(t0 + c))
                    if c:
                        normalise(c - 1)
                dve.wait_ge(*S["bc_in"].at(s))
                dve.wait_ge(*S["x1_in"].at(s))
                n_ = 0
                for half in range(2):
                    hc = slice(half * 512, (half + 1) * 512)
                    for t in range(t0, t1):
                        bk = wait_full(("out", half, t))
                        tmp = TMP[:, n_ % 2, 0:512]
                        drained(dve.tensor_tensor(tmp, bk[:], gate1b[:, hc], ALU.mult), ("out", half, t))
                        dve.wait_ge(*S["bank_dve"].at(("out", half, t)))
                        dve.tensor_tensor(X1[:, t - t0, hc], X1[:, t - t0, hc], tmp, ALU.add).then_inc(*S["x1_ready"].mark((half, t)))
                        n_ += 1
                for b, tb, n in blocks:
                    for t in range(tb, tb + n + 1):
                        if t < tb + n:
                            dve.wait_ge(*S["std2"].at(t))
                            dve.reciprocal(rs[:, 1, t:t + 1], rs[:, 1, t:t + 1]).then_inc(*S["rstd2"].mark(t))
                            dve.wait_ge(*S["rstd2"].at(t))
                            if t >= t0 + 2:
                                dve.wait_ge(*S["h2T_done"].at(t - 2))
                                dve.wait_ge(*S[f"h2_out{t % 2}"].at(t - 2))
                            elif s == 0:
                                dve.wait_ge(*S["state_out"].at(s))
                            dve.scalar_tensor_tensor(out=xb[t % 2], in0=X1[:, t - t0, :], scalar=rs[:, 1, t:t + 1],
                                                     in1=a2b, op0=ALU.mult, op1=ALU.mult).then_inc(*S["h2_pre"].mark(t))
                            dve.wait_ge(*S["h2_pre"].at(t))
                            dve.tensor_tensor(xb[t % 2], xb[t % 2], shift2b, ALU.add).then_inc(*S["h2_ready"].mark(t))
                        if t > tb:
                            u = t - 1
                            dve.wait_ge(*S["h2T_done"].at(u))
                            if b > blocks[0][0]:
                                dve.wait_ge(*S["bank_full"].at(("qf", b - 1, HP - 1)))
                            cc = slice((u - tb) * P, (u - tb + 1) * P)
                            dve.tensor_copy(H2T[:, 4:8, cc], wide[u % 2][:, 512:1024].rearrange("p (k n) -> p k n", k=4)
                                            ).then_inc(*S["h2T_dve"].mark(u))
                    for hp in range(HP):
                        bk = wait_full(("sc", b, hp))
                        quad = hp // 4
                        if hp % 4 == 0:
                            if quad >= 2:
                                dve.wait_ge(*S[f"sc_out{quad % 2}"].at((b, quad - 2)))
                            elif b > 0:
                                dve.wait_ge(*S[f"sc_out{quad % 2}"].at((b - 1, quad + 2)))
                        drained(dve.tensor_copy(scb[quad % 2][:, 0:n, hp % 4, :],
                                                bk[:, 0:n * P].rearrange("p (t n) -> p t n", n=NKEYS)), ("sc", b, hp))

            chain = S["pick"]

            def picks(tile, p):
                count = [0]

                def after(scan=False):
                    if count[0]:
                        dve.wait_ge(chain.sem, tile * CHAIN + count[0])
                        if scan:
                            dve.sem_inc(S["x_pace"].sem)

                def done(ins):
                    count[0] += 1
                    ins.then_inc(chain.sem, 1)

                def top16(src, vals, places):
                    done(dve.max(vals[:, 0:8], src))
                    after(scan=True)
                    done(dve.max_index(places[:, 0:8], vals[:, 0:8], src))
                    after(scan=True)
                    done(dve.match_replace(src, vals[:, 0:8], src, NEG))
                    after(scan=True)
                    done(dve.max(vals[:, 8:16], src))
                    after(scan=True)
                    done(dve.max_index(places[:, 8:16], vals[:, 8:16], src))

                def keys(hp):
                    if hp == 0:
                        dve.wait_ge(S["scr_in"].sem, tile * 16 + 32)
                        dve.sem_inc(S["x_pace"].sem)
                    top16(scr[:, hp * NKEYS:(hp + 1) * NKEYS], sv[:, hp * TOPK:(hp + 1) * TOPK],
                          si[:, hp * TOPK:(hp + 1) * TOPK])

                def head(h):
                    after()
                    va, vb = (sv[:, (2 * h + r) * TOPK:(2 * h + r + 1) * TOPK] for r in range(2))
                    cd = cand[h % 2]
                    done(dve.tensor_tensor(cd.rearrange("p (a b) -> p a b", b=TOPK),
                                           va.unsqueeze(2).to_broadcast([P, TOPK, TOPK]),
                                           vb.unsqueeze(1).to_broadcast([P, TOPK, TOPK]), ALU.add))
                    after(scan=True)
                    top16(cd, ts[:, h * TOPK:(h + 1) * TOPK], pos[:, h * TOPK:(h + 1) * TOPK])

                def finish():
                    after()
                    t3 = ts.rearrange("p (h k) -> p h k", k=TOPK)
                    g3 = ge.rearrange("p (h k) -> p h k", k=TOPK)
                    dve.tensor_tensor(g3, t3, t3[:, :, 0:1].to_broadcast([P, PH, TOPK]), ALU.subtract
                                      ).then_inc(S["gexp_in"].sem, 1)
                    done(dve.tensor_copy(sf, si))
                    after()
                    done(dve.tensor_scalar(pab[0], pos, 4, None, ALU.logical_shift_right))
                    done(dve.tensor_scalar(pab[1], pos, 15, None, ALU.bitwise_and))
                    for r in range(2):
                        after()
                        done(dve.tensor_copy(pf[r], pab[r]))
                        after()
                        o3 = oneh.rearrange("p (j a) -> p j a", a=TOPK)
                        done(dve.tensor_tensor(o3, pf[r].unsqueeze(2).to_broadcast([P, SLOTS, TOPK]),
                                               iota16[:].unsqueeze(1).to_broadcast([P, SLOTS, TOPK]), ALU.is_equal))
                        after()
                        o4 = oneh.rearrange("p (h k a) -> p h k a", k=TOPK, a=TOPK)
                        s4 = sf.rearrange("p (h r a) -> p h r a", r=2, a=TOPK)[:, :, r:r + 1, :]
                        done(dve.tensor_tensor(o4, o4, s4.to_broadcast([P, PH, TOPK, TOPK]), ALU.mult))
                        after()
                        done(dve.tensor_reduce(pi[r], o3, AX.X, ALU.add))
                    after()
                    done(dve.scalar_tensor_tensor(out=idx[p][:], in0=pi[0], scalar=float(NKEYS), in1=pi[1],
                                                  op0=ALU.mult, op1=ALU.add))
                    after()
                    dve.wait_ge(S["gexp"].sem, tile + 1)
                    done(dve.tensor_reduce(gsum, g3, AX.X, ALU.add))
                    after()
                    done(dve.reciprocal(gsum, gsum))
                    after()
                    done(dve.tensor_tensor(gate[p].rearrange("p (h k) -> p h k", k=TOPK), g3,
                                           gsum.unsqueeze(2).to_broadcast([P, PH, TOPK]), ALU.mult))
                    after()
                    dve.sem_inc(S["idx_ready"].sem)
                    assert count[0] == CHAIN, count[0]

                return ([lambda hp=hp: keys(hp) for hp in range(HP)], [lambda h=h: head(h) for h in range(PH)], finish)

            keys_, heads_, finish_ = picks(0, 0)
            dve.wait_ge(*S["front_done"].at("x1"))
            for f in (*keys_, *heads_, finish_):
                f()
            dve.sem_inc(S["y_ready"].sem)
            with dve.Fori(0, NT // 2) as i:
                for p in range(2):
                    keys_, heads_, finish_ = picks(i * 2 + p + 1, 1 - p)
                    dve.wait_ge(S[f"tile_in{p}"].sem, i * 48 + 48)
                    dve.sem_inc(S["x_pace"].sem)
                    for g in range(SLOTS // RING):
                        for half in range(RING // GROUP):
                            for r in range(half * GROUP, (half + 1) * GROUP):
                                dve.wait_ge(landed[r], i * (32 * SLOTS // RING) + (p * SLOTS // RING + g + 1) * 16)
                                dve.tensor_tensor_reduce(out=ring[r][:, 0:D], in0=ring[r][:, 0:D], in1=h2b[p], scale=1.0,
                                                         scalar=0.0, op0=ALU.mult, op1=ALU.add, accum_out=dots[:, r:r + 1]
                                                         ).then_inc(S["dot"].sem, 1)
                            if half == 0:
                                if g < 6:
                                    for f in keys_[3 * g:3 * g + 3]:
                                        f()
                                elif g < 14:
                                    heads_[g - 6]()
                                elif g == 14:
                                    finish_()
                            n = p * (SLOTS // GROUP) + g * (RING // GROUP) + half + 1
                            j = half * GROUP
                            dve.wait_ge(S["gelu"].sem, i * (2 * SLOTS // GROUP) + n)
                            dve.tensor_tensor(wts[:, j:j + GROUP], gel[:, j:j + GROUP],
                                              gate[p][:, g * RING + j:g * RING + j + GROUP], ALU.mult
                                              ).then_inc(S["weight"].sem, 1)
                    dve.wait_ge(S["slot_used"].sem, i * (2 * SLOTS) + (p + 1) * SLOTS + 1)
                    dve.tensor_tensor(h2b[p], wide[p][:], gate2b[p], ALU.mult).then_inc(S["y_pre"].sem, 1)
                    dve.wait_ge(S["y_pre"].sem, i * 4 + 2 * p + 1)
                    dve.tensor_tensor(x1b[p], x1b[p], h2b[p], ALU.add).then_inc(S["y_pre"].sem, 1)
                    dve.wait_ge(S["y_std"].sem, i * 2 + p + 1)
                    dve.reciprocal(frs[:, p:p + 1], frs[:, p:p + 1]).then_inc(S["rstd"].sem, 1)
                    dve.wait_ge(S["rstd"].sem, i * 2 + p + 1 + NT)
                    dve.scalar_tensor_tensor(out=x1b[p], in0=x1b[p], scalar=frs[:, p:p + 1], in1=finalb,
                                             op0=ALU.mult, op1=ALU.mult).then_inc(S["y_ready"].sem, 1)


CHAIN = 5 * HP + 6 * PH + 15
PICK_DONE = 14
Y_BASE = 16


def kernel(**inputs):
    import numpy as np
    import concourse.bacc as _bacc
    from concourse.bass_utils import run_bass_kernel_spmd as _run

    f = {k: np.asarray(v) for k, v in inputs.items()}

    def by_partition(w, parts):
        return w.reshape(parts, P, -1).transpose(1, 0, 2)

    w_in = by_partition(f["w_in"][0], KD)
    col_at = [0, DK, 2 * DK, 2 * DK + DV, 2 * DK + 2 * DV, 2 * DK + 2 * DV + 2 * RANK]
    ca0 = col_at[5]
    cb0 = ca0 + CH
    starts = [0, P, DK, DK + P] + [ca0 + m * P for m in range(CM)] + [cb0 + m * P for m in range(CM)]
    w_vg = []
    for c0 in (2 * DK, 2 * DK + DV):
        for c in range(4):
            w_vg.append(w_in[:, 2 * c:2 * c + 2, c0:c0 + DV].reshape(P, D))
    w_up = np.zeros((2 * RANK, 2, DK), np.float32)
    w_up[0:RANK, 0] = f["w_af_up"][0]
    w_up[RANK:, 1] = f["w_ab_up"][0]
    pw2 = by_partition(f["conv_pw2"][0], CM)
    w_out = by_partition(f["w_out"][0], KD)
    wq = by_partition(f["peer_wq"][0], KD)
    ins = {
        "x": np.concatenate([f["x_prompt"][0], f["x_sample"][0]], axis=0),
        "c2": np.stack([f["c_ctx"], f["c"][0]], axis=1).reshape(KD, P, 2).transpose(1, 0, 2),
        "w_mod": by_partition(f["w_mod"][0], KD).reshape(P, KD, 12, 512).transpose(2, 0, 1, 3),
        "b_mod": f["b_mod"],
        "norm1_g": f["norm1_g"], "norm2_g": f["norm2_g"],
        "w_cols": np.stack([w_in[:, :, c:c + P].reshape(P, D) for c in starts]),
        "w_af": w_in[:, :, col_at[4]:col_at[4] + 2 * RANK].reshape(P, KD * 2 * RANK),
        "w_vg": np.stack(w_vg),
        "w_up": w_up,
        "b_up": np.stack([f["b_af"][0], f["b_ab"][0]]).reshape(2, PAIRS, P).transpose(2, 0, 1),
        "gla_g": f["gla_norm_g"][0],
        "conv_w": f["conv_dw_w"][0].T.reshape(CM, P, TAPS).transpose(1, 0, 2),
        "conv_v": np.stack([f["conv_dw_b"][0], f["conv_ln_g"][0], f["conv_ln_b"][0]]).reshape(3, CM, P).transpose(2, 0, 1),
        "w_pw2": np.stack([pw2[:, 2 * c:2 * c + 2].reshape(P, D) for c in range(2)]),
        "w_out": np.stack([w_out[:, 2 * c:2 * c + 2, h * 512:(h + 1) * 512].reshape(P, D) for h in range(2) for c in range(4)]),
        "w_q": np.stack([wq[:, :, m * P:(m + 1) * P].reshape(P, D) for m in range(HP)]),
        "sk": f["peer_subkeys"][0].reshape(HP, NKEYS, P).transpose(2, 0, 1),
        "uv": np.concatenate([f["peer_u"][0], f["peer_v"][0]], axis=1),
        "final_g": f["final_norm_g"],
        "state_f": f["state_gla_fwd"].reshape(DK, HV),
        "state_b": f["state_gla_bwd"].reshape(DK, HV),
    }
    ins = {k: np.ascontiguousarray(v) for k, v in ins.items()}

    def program(counts):
        nc = _bacc.Bacc("TRN2", target_bir_lowering=False, num_devices=1)
        a = {k: nc.dram_tensor(f"in_{k}", v.shape, F32, kind="ExternalInput").ap() for k, v in ins.items()}
        for k, shape in (("y", (NT * P, D)), ("new_f", (DK, HV)), ("new_b", (DK, HV))):
            a[k] = nc.dram_tensor(f"out_{k}", shape, F32, kind="ExternalOutput").ap()
        build(nc, a, counts)
        return nc

    counts = {}
    program(counts)
    nc = program(counts)
    r = _run(nc, [{f"in_{k}": v for k, v in ins.items()}], core_ids=[0]).results[0]
    y = r["out_y"]
    state = (1, 1, HEADS, HK, HV)
    n0 = STREAMS[0][1] * P
    return (y[None, :n0], y[None, n0:], r["out_new_f"].reshape(state), r["out_new_b"].reshape(state))
```

```python
from contextlib import ExitStack

import concourse.bass as bass
from concourse import mybir

F32 = mybir.dt.float32
U32 = mybir.dt.uint32
ALU = mybir.AluOpType
ACT = mybir.ActivationFunctionType
AX = mybir.AxisListType

P = 128
D = 1024
KD = D // P
EPS = 1e-6
HEADS, HK, HV = 4, 64, 128
PAIRS = HEADS // 2
DK, DV = HEADS * HK, HEADS * HV
RANK = 16
CH = 512
CM = CH // P
TAPS = 31
PAD = TAPS // 2
GRID = 64
PH, NKEYS, TOPK = 8, 128, 16
HP = 2 * PH
SLOTS = PH * TOPK
NEG = -3.0e38
STREAMS = ((0, 2), (2, 10))
NT = STREAMS[1][1]
MAXL = P * (STREAMS[1][1] - STREAMS[1][0])
WSLOTS = 4
RING = 8
GROUP = 4
ERING = 4
EC = 2
EARLY = 2 * SLOTS // EC


class Signal:

    def __init__(self, sem, counts):
        self.sem, self.counts, self.n = sem, counts, 0
        self.known = bool(counts)

    def mark(self, key, by=1):
        self.n += by
        self.counts[key] = self.n
        return self.sem, by

    def at(self, key):
        return self.sem, self.counts[key] if self.known else 1


def stream_blocks(s):
    t0, t1 = STREAMS[s]
    n = min(4, t1 - t0)
    return [(s + i, t0 + i * n, n) for i in range((t1 - t0) // n)]


def build(nc, a, counts):
    with ExitStack() as ctx:
        def sb(name, shape, dt=F32):
            return ctx.enter_context(nc.sbuf_tensor(name, shape, dt))

        def scratch(name, shape):
            return nc.dram_tensor(name, shape, F32, kind="Internal").ap()

        def signal(name):
            return Signal(ctx.enter_context(nc.semaphore(name)), counts.setdefault(name, {}))

        mod_d = scratch("mod_d", (2, 6 * D))
        gate2_d = scratch("gate2_d", (NT // 2, D))
        x1_d = scratch("x1_d", (NT * P, D))
        h2_d = scratch("h2_d", (NT * P, D))
        sc_d = scratch("sc_d", ((NT + 1) * P, HP * NKEYS))

        ident = sb("ident", [P, P])
        ones = sb("ones", [P, P])
        keep_f = sb("keep_f", [P, PAIRS, P], U32)
        twice_d = sb("twice_d", [P, HEADS, P])
        one = sb("one", [P, P])
        iota16 = sb("iota16", [P, TOPK])
        eps = sb("eps", [P, 1])
        cvec = sb("cvec", [P, KD, 2])
        csil = sb("csil", [P, KD, 2])
        modT = sb("modT", [P, 2, KD, 2])
        wup = sb("wup", [2 * RANK, 2, DK])
        bup = sb("bup", [P, 2, PAIRS])
        cw = sb("cw", [P, CM, TAPS])
        cvv = sb("cvv", [P, 3, CM])
        gnb = sb("gnb", [P, DV])
        ss = sb("ss", [P, 2, NT])
        rs = sb("rs", [P, 2, NT])
        oss = sb("oss", [P, NT, HEADS])
        ors = sb("ors", [P, NT, HEADS])
        colsin = sb("colsin", [P, 4, 3, MAXL // P])
        cols = sb("cols", [P, 4, 3, MAXL // P])
        WORDS = 35 * 1024
        arena = sb("arena", [P, WORDS])
        top = [0]

        def take(words):
            top[0] += words
            assert top[0] <= WORDS, top[0]
            return arena[:, top[0] - words:top[0]]

        xb = [take(D) for _ in range(2)]
        junk = take(D)
        hreg = take(KD * MAXL)
        hT = hreg.rearrange("p (k n) -> p k n", k=KD)
        ureg = take(CM * MAXL)
        U = ureg.rearrange("p (m n) -> p m n", m=CM)
        creg = take(CM * MAXL)
        C = creg.rearrange("p (m n) -> p m n", m=CM)
        qkreg = take(4 * MAXL)
        QK = qkreg.rearrange("p (m n) -> p m n", m=4)
        vreg = take(8 * DV)
        V = vreg.rearrange("p (t n) -> p t n", n=DV)
        greg = take(8 * DV)
        SG = greg.rearrange("p (t n) -> p t n", n=DV)
        W = [take(D) for _ in range(WSLOTS)]
        QF = hreg[:, 0:2 * MAXL].rearrange("p (m n) -> p m n", m=PAIRS)
        KF = hreg[:, 2 * MAXL:4 * MAXL].rearrange("p (m n) -> p m n", m=PAIRS)
        ST = [r.rearrange("p (c d n) -> p c d n", d=PAIRS, n=2 * HV) for r in (hreg[:, 4 * MAXL:8 * MAXL], creg)]
        X1 = hreg.rearrange("p (t n) -> p t n", n=D)
        TMP = creg.rearrange("p (b n) -> p b n", b=4)
        gate1b, a2b, shift2b = (qkreg[:, i * D:(i + 1) * D] for i in range(3))
        afT = junk
        sgt = [junk[:, 0:512], junk[:, 512:1024]]
        rsb = xb[0][:, 0:512]
        kT = [xb[0][:, i * P:(i + 1) * P] for i in range(4)]
        Scur = [xb[1][:, i * P:(i + 1) * P] for i in range(4)]
        Stmp = [xb[1][:, (4 + i) * P:(5 + i) * P] for i in range(4)]
        H2T = greg.rearrange("p (k n) -> p k n", k=KD)
        qfT = [vreg[:, 0:512], vreg[:, 512:1024]]
        skT = vreg[:, 2048:4096].rearrange("p (h n) -> p h n", h=HP)
        scb = [creg[:, i * 2048:(i + 1) * 2048].rearrange("p (t h n) -> p t h n", t=4, h=4) for i in range(2)]
        wmod = [hreg[:, i * 4096:(i + 1) * 4096].rearrange("p (k n) -> p k n", k=KD) for i in range(2)]
        modrow = arena[0:2, 3 * D + 8 * MAXL + 8 * MAXL + 4 * MAXL:3 * D + 20 * MAXL + 6 * D]
        assert 6 * D <= 16 * DV
        bmod = arena[0:2, 3 * D + 8 * MAXL:3 * D + 8 * MAXL + 6 * D]
        grow = arena[0:2, 3 * D + 14 * MAXL:3 * D + 16 * MAXL].rearrange("p (a n) -> p a n", a=2)

        top[0] = 0
        ring = [take(2 * D) for _ in range(RING)]
        h2b = [take(D) for _ in range(2)]
        x1b = [take(D) for _ in range(2)]
        gate2b = [take(D) for _ in range(2)]
        finalb = take(D)
        diag = [take(P) for _ in range(RING)]
        pick_at = [(r[:, 0:2048], r[:, 2048:4096]) for r in (vreg, ureg, take(4096))]
        small = sb("small", [P, 4 * RING + 4 + PH])
        dots, gel, wts, fss, frs, gsum = (small[:, a:b] for a, b in ((0, 8), (8, 16), (16, 24), (24, 26), (26, 28), (28, 36)))
        cand = [sb(f"cand{i}", [P, TOPK * TOPK])[:] for i in range(2)]
        sv, sf = (sb(n, [P, HP * TOPK])[:] for n in ("sv", "sf"))
        si = sb("si", [P, HP * TOPK], U32)[:]
        ts, ge = (sb(n, [P, SLOTS])[:] for n in ("ts", "ge"))
        pos = sb("pos", [P, SLOTS], U32)[:]
        pab = [sb(f"pab{i}", [P, SLOTS], U32)[:] for i in range(2)]
        pf = [sb(f"pf{i}", [P, SLOTS])[:] for i in range(2)]
        pi = [sb(f"pi{i}", [P, SLOTS])[:] for i in range(2)]
        gate = [sb(f"gate{i}", [P, SLOTS])[:] for i in range(2)]
        idx = [sb(f"idx{i}", [P, SLOTS], U32) for i in range(2)]
        ring_e = [sb(f"ring_e{i}", [P, 2 * D])[:] for i in range(ERING)]
        h2e = [sb(f"h2e{i}", [P, D])[:] for i in range(2)]
        diag_e = [sb(f"diag_e{i}", [P, P])[:] for i in range(ERING)]
        dots_e, gel_e, wts_e = (sb(n, [P, ERING])[:] for n in ("dots_e", "gel_e", "wts_e"))

        banks = [ctx.enter_context(nc.psum_tensor(f"bank{i}", [P, 512], F32)) for i in range(4)]
        wide = [ctx.enter_context(nc.psum_tensor(f"wide{i}", [P, 2 * 512], F32)) for i in range(2)]

        S = {n: signal(n) for n in (
            "consts", "small_in", "cs_ready", "wmod_in0", "wmod_in1", "mod_rows", "mod_cols", "mod_out", "modT_ready",
            "x_in0", "x_in1", "sumsq", "std_ready", "rstd", "xn_ready", 
            "bank_full", "bank_act", "bank_dve", "tap_done", "centred", "squared", "ln_rstd", "ln_scaled",
            "conv_act", "afT_ready", "az", "softplus", "g_ready", "scan", "span", "cols_in", "exps", "cols_ready",
            "qk_scaled", "kT_done", "st_zero", "st_tmp", "st_kept", "st_next", "state_in", "state_out", "sc_sel", "scT",
            "osum", "ostd", "orstd", "og", "sg_ready", "x1_in", "x1_tmp", "x1_ready", "sumsq2", "std2", "rstd2",
            "h2_pre", "h2_ready", "h2_out0", "h2_out1", "sc_out0", "sc_out1",
            "bc_in", "sk_in", "front_done", "scr_in", "scr1_in", "final_in", "tile_in0", "tile_in1", "h2e_in", "dot_e", "gelu_e", "weight_e", "diag_e", "used_e", "y_std_done", "pick", "gexp_in", "gexp", "idx_ready", "slot_ok",
            "dot", "gelu", "weight", "diag_ready", "slot_used", "y_pre", "y_sum", "y_std", "y_ready", "y_out0", "y_out1", "x_pace", "sp_pace", "act_pace")}
        w_in = [signal(f"w_in{i}") for i in range(WSLOTS)]
        landed_e = [signal(f"landed_e{i}") for i in range(ERING)]
        landed = [ctx.enter_context(nc.semaphore(f"landed{i}")) for i in range(RING)]

        def chunks(s):
            for m in range(CM):
                yield ("cb", m)
                yield ("ca", m)
            for m in range(4):
                yield ("qk", m)
            yield ("af", 0)
            for name in ("v", "g"):
                for c in range(4):
                    yield (name, c)
            for c in range(2):
                yield ("pw2", c)
            for half in range(2):
                for c in range(4):
                    yield ("out", 4 * half + c)
            for b, _, _ in stream_blocks(s):
                for hp in range(HP):
                    yield ("wq", (b, hp))

        order = [(s, *c) for s in range(2) for c in chunks(s)]
        at_slot = {c: (n % WSLOTS, n) for n, c in enumerate(order)}

        def last_unit(s, name, part):
            b, _, _ = stream_blocks(s)[-1]
            t = STREAMS[s][1] - 1
            return {"cb": ("cb", part, b), "ca": ("ca", part, b), "qk": ("qk", part, b), "af": ("af", b),
                    "v": ("v", t), "g": ("g", t), "pw2": ("pw2", CM - 1, b),
                    "out": ("out", part // 4 if name == "out" else 0, t),
                    "wq": ("qf", *part) if name == "wq" else None}[name]

        def chunk_source(name, part):
            if name in ("cb", "ca", "qk"):
                m = {"qk": 0, "ca": 4, "cb": 8}[name] + part
                return a["w_cols"][m], D
            if name == "af":
                return a["w_af"], KD * 2 * RANK
            if name in ("v", "g"):
                return a["w_vg"][4 * (name == "g") + part], D
            if name == "pw2":
                return a["w_pw2"][part], D
            if name == "out":
                return a["w_out"][part], D
            return a["w_q"][part[1]], D

        def weights_ready(pe, s, name, part):
            slot, _ = at_slot[(s, name, part)]
            pe.wait_ge(*w_in[slot].at((s, name, part)))
            return W[slot]

        BY_DVE = {"xT1", "hT1", "ca", "ln1", "scf", "out", "sc", "mod"}

        def emptied(key):
            if key[0] == "st":
                return S["st_next"].at(key[1:])
            if key[0] == "o":
                return S["og"].at(key[1])
            return S["bank_dve" if key[0] in BY_DVE else "bank_act"].at(key)

        def sct(c):
            return junk[:, (c % 2) * 512:(c % 2 + 1) * 512]

        def by_head(r, odd):
            return r.rearrange("p (a o n) -> p a o n", o=2, n=P)[:, :, odd, :]

        hooks, at_hook = {}, 0
        for phase, n in (("norm", 8), ("conv", 16), ("qk", 8), ("vg", 16), ("ln", 8), ("gates", 8), ("states", 14),
                         ("attn", 10), ("out", 16), ("qf0", 20), ("qf1", 20)):
            hooks[phase] = at_hook
            at_hook += n
        assert at_hook > EARLY

        def hook(s, phase, n):
            return hooks[phase] + n if s == 1 and hooks[phase] + n <= EARLY else -1

        def unit_banks():
            keys = counts["bank_full"]
            return {k: banks[(v - 1) % 4] for k, v in keys.items()}

        def former(d, pair):
            n = PAIRS * d + pair - 1
            return n // PAIRS, n % PAIRS

        block = ctx.enter_context(nc.Block())

        def store_scores(sp, b, tb, n, quad):
            sp.wait_ge(*S["bank_dve"].at(("sc", b, 4 * quad + 3)))
            for j in range(n):
                out = sc_d[(tb + j) * P:(tb + j + 1) * P, quad * 512:(quad + 1) * 512]
                src = scb[quad % 2][:, j, :, :].rearrange("p h n -> p (h n)")
                sp.dma_start(out, src).then_inc(*S[f"sc_out{quad % 2}"].mark((b, quad), 16))
                if tb + j == 0:
                    sp.dma_start(sc_d[NT * P:, quad * 512:(quad + 1) * 512], src
                                 ).then_inc(*S[f"sc_out{quad % 2}"].mark((b, quad), 16))

        @block.sync
        def _(sp):
            n_small = 0
            sp.dma_start(cvec[:], a["c2"]).then_inc(*S["small_in"].mark("c", 16))
            sp.wait_ge(*S["small_in"].at("c"))
            for i in range(2):
                sp.dma_start(bmod[i:i + 1, :], a["b_mod"]).then_inc(*S["small_in"].mark(("b", i), 16))
                sp.dma_start(grow[i:i + 1, 0, :], a["norm1_g"]).then_inc(*S["small_in"].mark(("g1", i), 16))
                sp.dma_start(grow[i:i + 1, 1, :], a["norm2_g"]).then_inc(*S["small_in"].mark(("g2", i), 16))
            for dst, name in ((wup[:], "w_up"), (bup[:], "b_up"), (cw[:], "conv_w"), (cvv[:], "conv_v"),
                              (gnb[:], "gla_g")):
                src = a[name].partition_broadcast(P) if name == "gla_g" else a[name]
                sp.dma_start(dst, src).then_inc(*S["small_in"].mark("all", 16))
            for n in range(12):
                if n >= 2:
                    sp.wait_ge(*S["bank_full"].at(("mod", n - 2)))
                sp.dma_start(wmod[n % 2], a["w_mod"][n]).then_inc(*S[f"wmod_in{n % 2}"].mark(n, 16))
            sp.wait_ge(*S["mod_rows"].at("a2"))
            sp.dma_start(mod_d, modrow).then_inc(*S["mod_out"].mark("rows", 16))
            sp.wait_ge(*S["mod_out"].at("rows"))
            sp.dma_start(gate2_d[0:1, :], mod_d[0:1, 5 * D:6 * D]).then_inc(*S["mod_out"].mark("gate2", 16))
            sp.dma_start(gate2_d[1:NT // 2, :], mod_d[1, 5 * D:6 * D].partition_broadcast(NT // 2 - 1)
                         ).then_inc(*S["mod_out"].mark("gate2", 16))

            for s, (t0, t1) in enumerate(STREAMS):
                queue = [c for c in order if c[0] == s]

                def load_weights(upto):
                    while queue:
                        c = queue.pop(0)
                        slot, n = at_slot[c]
                        if n >= WSLOTS:
                            sp.wait_ge(*S["bank_full"].at(last_unit(*order[n - WSLOTS])))
                        src, words = chunk_source(*c[1:])
                        sp.dma_start(W[slot][:, 0:words], src).then_inc(*w_in[slot].mark(c, 16))
                        if c[1:] == upto:
                            return

                if s == 0:
                    sp.wait_ge(*S["modT_ready"].at(0))
                for t in range(t0, t1):
                    if t >= 2:
                        sp.wait_ge(*S["bank_full"].at(("xT1" if t >= t0 + 2 else "hT1", t - 2)))
                        if t < t0 + 2:
                            sp.wait_ge(*S[f"h2_out{t % 2}"].at(t - 2))
                    sp.dma_start(xb[t % 2], a["x"][t * P:(t + 1) * P, :]).then_inc(*S[f"x_in{t % 2}"].mark(t, 16))
                    if t == t0 + 1:
                        load_weights(("cb", 1))
                load_weights(("pw2", 1))
                if s == 1:
                    sp.wait_ge(*S["bank_full"].at(("xT1", t1 - 1)))
                    for d, name in enumerate(("state_f", "state_b")):
                        for pair in range(PAIRS):
                            sp.dma_start(Scur[2 * d + pair], a[name][pair * P:(pair + 1) * P, :]
                                         ).then_inc(*S["state_in"].mark(s, 16))
                load_weights(("out", 0))
                if s == 0:
                    for d, name in enumerate(("new_f", "new_b")):
                        for pair in range(PAIRS):
                            sp.wait_ge(*S["st_next"].at((s, t1 - t0 - 1, 2 * d + pair)))
                            sp.dma_start(a[name][pair * P:(pair + 1) * P, :], Scur[2 * d + pair]
                                         ).then_inc(*S["state_out"].mark(s, 16))
                load_weights(("out", 3))
                for t in range(t0, t1):
                    sp.wait_ge(*S["bank_full"].at(("o", t1 - 1)))
                    sp.dma_start(X1[:, t - t0, :], a["x"][t * P:(t + 1) * P, :]).then_inc(*S["x1_in"].mark(s, 16))
                for dst, row in ((gate1b, 2), (shift2b, 3), (a2b, 4)):
                    sp.dma_start(dst, mod_d[s, row * D:(row + 1) * D].partition_broadcast(P)
                                 ).then_inc(*S["bc_in"].mark(s, 16))
                load_weights(("out", 7))
                sp.wait_ge(*S["bank_full"].at(("out", 1, t1 - 1)))
                sp.dma_start(skT, a["sk"]).then_inc(*S["sk_in"].mark(s, 16))
                for b, tb, n in stream_blocks(s):
                    load_weights(("wq", (b, 0)))
                    for t in range(tb, tb + n):
                        sp.wait_ge(*S["x1_ready"].at((1, t)))
                        sp.dma_start(x1_d[t * P:(t + 1) * P, :], X1[:, t - t0, :]).then_inc(*S["front_done"].mark("x1", 16))
                        sp.wait_ge(*S["h2_ready"].at(t))
                        sp.dma_start(h2_d[t * P:(t + 1) * P, :], xb[t % 2]).then_inc(*S[f"h2_out{t % 2}"].mark(t, 16))
                    for hp in range(HP):
                        if hp:
                            load_weights(("wq", (b, hp)))
                        if hp >= 4 and hp % 4 == 1:
                            store_scores(sp, b, tb, n, hp // 4 - 1)
                    store_scores(sp, b, tb, n, 3)
                    if b < 2:
                        for i in range(2):
                            sp.wait_ge(*S[f"sc_out{i}"].at((b, i + 2)))
                        if b == 1:
                            sp.wait_ge(S["idx_ready"].sem, 2)
                        sp.dma_start(pick_at[b][0], sc_d[tb * P:(tb + 1) * P, :]).then_inc(*S["scr_in"].mark(2 * b, 16))

            for i in range(2):
                sp.wait_ge(*S[f"h2_out{i}"].at(NT - 2 + i))
                sp.wait_ge(*S[f"sc_out{i}"].at((2, i + 2)))
            sp.wait_ge(*S["front_done"].at("x1"))
            sp.wait_ge(*S["mod_out"].at("gate2"))
            sp.wait_ge(*S["bank_dve"].at(("sc", 2, HP - 1)))
            sp.wait_ge(S["idx_ready"].sem, 3)
            sp.dma_start(finalb, a["final_g"].partition_broadcast(P)).then_inc(*S["final_in"].mark(0, 16))

            def load_tile(p, row, pair):
                sp.dma_start(h2b[p], h2_d[bass.ds(row, P), :]).then_inc(S[f"tile_in{p}"].sem, 16)
                sp.dma_start(x1b[p], x1_d[bass.ds(row, P), :]).then_inc(S[f"tile_in{p}"].sem, 16)
                sp.dma_start(gate2b[p], gate2_d[bass.ds(pair, 1), :].rearrange("a n -> (a n)").partition_broadcast(P)
                             ).then_inc(S[f"tile_in{p}"].sem, 16)

            for t in range(2):
                load_tile(t, t * P, 0)
                S[f"tile_in{t}"].mark(t, 48)
            with sp.Fori(0, NT // 2 - 1) as i:
                for p in range(2):
                    row = i * (2 * P) + (p + 2) * P
                    sp.wait_ge(S[f"y_out{p}"].sem, i * 16 + 16)
                    sp.sem_inc(S["sp_pace"].sem)
                    load_tile(p, row, i + 1)
                    sp.wait_ge(S["idx_ready"].sem, i * 2 + p + 3)
                    sp.sem_inc(S["sp_pace"].sem)
                    sp.dma_start(pick_at[2][0], sc_d[bass.ds(row + P, P), :]).then_inc(S["scr_in"].sem, 16)
            for p in range(2):
                sp.wait_ge(S[f"y_out{p}"].sem, 16 * NT // 2)
            sp.wait_ge(*S["state_out"].at(0))

        @block.gpsimd
        def _(pool):
            consts = S["consts"]
            pool.memset(ident[:], 0.0).then_inc(*consts.mark("z"))
            pool.memset(twice_d[:], 1.0).then_inc(*consts.mark("z"))
            pool.memset(keep_f[:], 1).then_inc(*consts.mark("z"))
            pool.memset(one[:], 1.0).then_inc(*consts.mark("z"))
            pool.memset(ones[:], 1.0 / CH).then_inc(*consts.mark("z"))
            pool.memset(eps[:], EPS).then_inc(*consts.mark("z"))
            pool.iota(iota16[:], [[1, TOPK]], base=0, channel_multiplier=0,
                      allow_small_or_imprecise_dtypes=True).then_inc(*consts.mark("z"))
            pool.wait_ge(*consts.at("z"))
            pool.affine_select(out=ident[:], in_=ident[:], compare_op=ALU.not_equal, fill=1.0, base=0,
                               pattern=[[-1, P]], channel_multiplier=1).then_inc(*consts.mark("all"))
            pool.affine_select(out=twice_d[:], in_=twice_d[:], compare_op=ALU.not_equal, fill=2.0, base=0,
                               pattern=[[0, HEADS], [-1, P]], channel_multiplier=1).then_inc(*consts.mark("all"))
            kf = keep_f[:].bitcast(mybir.dt.int32)
            pool.affine_select(out=kf, in_=kf, compare_op=ALU.is_ge, fill=0, base=0,
                               pattern=[[0, PAIRS], [1, P]], channel_multiplier=-1).then_inc(*consts.mark("all"))

            pool.wait_ge(*S["h2_out0"].at(0))
            pool.wait_ge(*S["h2_out1"].at(1))
            for t in range(2):
                pool.dma_start(h2e[t], h2_d[t * P:(t + 1) * P, :]).then_inc(*S["h2e_in"].mark(0, 16))
            pool.wait_ge(S["idx_ready"].sem, 1)
            for k in range(2 * SLOTS):
                if k == SLOTS:
                    pool.wait_ge(S["idx_ready"].sem, 2)
                if k >= ERING:
                    pool.wait_ge(*S["used_e"].at(k - ERING))
                pool.indirect_dma_start(
                    out=ring_e[k % ERING], out_offset=None, in_=a["uv"],
                    in_offset=bass.IndirectOffsetOnAxis(ap=idx[k // SLOTS][:, k % SLOTS:k % SLOTS + 1], axis=0)
                ).then_inc(*landed_e[k % ERING].mark(k, 16))
                if k == 1:
                    pool.dma_start(pick_at[0][0], sc_d[P:2 * P, :]).then_inc(*S["scr1_in"].mark(1, 16))

            pool.wait_ge(*S["bank_dve"].at(("sc", 2, HP - 1)))
            for i in range(2):
                pool.wait_ge(*S[f"h2_out{i}"].at(NT - 2 + i))
                pool.wait_ge(*S[f"sc_out{i}"].at((2, i + 2)))
            pool.wait_ge(*S["front_done"].at("x1"))
            with pool.Fori(0, NT // 2 - 1) as i:
                for p in range(2):
                    pool.wait_ge(S["idx_ready"].sem, i * 2 + p + 3)
                    pool.sem_inc(S["slot_ok"].sem)
                    for k in range(SLOTS):
                        pool.wait_ge(S["slot_used"].sem, i * (2 * SLOTS) + p * SLOTS + k + 1)
                        pool.sem_inc(S["slot_ok"].sem)
                        pool.indirect_dma_start(
                            out=ring[k % RING], out_offset=None, in_=a["uv"],
                            in_offset=bass.IndirectOffsetOnAxis(ap=idx[p][:, k:k + 1], axis=0)
                        ).then_inc(landed[k % RING], 16)

        @block.tensor
        def _(pe):
            units = []

            def bank(key):
                n = len(units)
                if n >= 4:
                    pe.wait_ge(*emptied(units[n - 4]))
                units.append(key)
                return banks[n % 4]

            def full(ins, key):
                ins.then_inc(*S["bank_full"].mark(key))

            def turn_tile(name, t):
                for half in range(2):
                    bk = bank((f"{name}{half}", t))
                    for k in range(4):
                        c0 = half * 512 + k * P
                        ins = pe.transpose(bk[:, k * P:(k + 1) * P], xb[t % 2][:, c0:c0 + P], ident[:])
                    full(ins, (f"{name}{half}", t))

            def early(s, phase, n):
                c = hook(s, phase, n) - 1
                if not 0 <= c < EARLY:
                    return
                for k in range(EC * c, EC * c + EC):
                    pe.wait_ge(*S["diag_e"].at(k))
                    for h in range(2):
                        ins = pe.matmul(wide[k // SLOTS][:, h * 512:(h + 1) * 512], lhsT=diag_e[k % ERING],
                                        rhs=ring_e[k % ERING][:, D + h * 512:D + (h + 1) * 512],
                                        start=(k % SLOTS == 0), stop=(k % SLOTS == SLOTS - 1), skip_group_check=True)
                    ins.then_inc(*S["used_e"].mark(k))

            pe.wait_ge(*S["consts"].at("all"))
            pe.wait_ge(*S["cs_ready"].at(0))
            for n in range(12):
                bk = bank(("mod", n))
                pe.wait_ge(*S[f"wmod_in{n % 2}"].at(n))
                for k in range(KD):
                    ins = pe.matmul(bk[0:2, :], lhsT=csil[:, k, :], rhs=wmod[n % 2][:, k, :],
                                    start=(k == 0), stop=(k == KD - 1))
                full(ins, ("mod", n))
            pe.wait_ge(*S["mod_rows"].at("a2"))
            for which in range(2):
                for k in range(KD):
                    ins = pe.transpose(wide[0][:, (which * KD + k) * 2:(which * KD + k) * 2 + 2],
                                       modrow[:, which * D + k * P:which * D + (k + 1) * P], ident[0:2, 0:2])
            ins.then_inc(*S["mod_cols"].mark(0))
            pe.wait_ge(*S["modT_ready"].at(0))

            for s, (t0, t1) in enumerate(STREAMS):
                blocks = stream_blocks(s)
                for t in range(t0, t1):
                    pe.wait_ge(*S["xn_ready"].at(t))
                    turn_tile("xT", t)
                    early(s, "norm", t - t0)
                pe.wait_ge(*S["bank_act"].at(("xT0", t1 - 1)))
                pe.wait_ge(*S["bank_dve"].at(("xT1", t1 - 1)))

                def project(name, m, b, tb, n):
                    w = weights_ready(pe, s, name, m)
                    cols_ = slice((tb - t0) * P, (tb - t0 + n) * P)
                    key = (name, m, b) if name != "af" else ("af", b)
                    bk = bank(key)
                    M = P if name != "af" else 2 * RANK
                    for k in range(KD):
                        ins = pe.matmul(bk[0:M, 0:n * P], lhsT=w[:, k * M:(k + 1) * M], rhs=hT[:, k, cols_],
                                        start=(k == 0), stop=(k == KD - 1))
                    full(ins, key)

                for m in range(CM):
                    for j, blk in enumerate(blocks):
                        project("cb", m, *blk)
                        early(s, "conv", 4 * m + 2 * j)
                        project("ca", m, *blk)
                        early(s, "conv", 4 * m + 2 * j + 1)
                for m in range(4):
                    for j, blk in enumerate(blocks):
                        project("qk", m, *blk)
                        early(s, "qk", 2 * m + j)
                for blk in blocks:
                    project("af", 0, *blk)
                for name in ("v", "g"):
                    for t in range(t0, t1):
                        bk = bank((name, t))
                        for k in range(KD):
                            w = weights_ready(pe, s, name, k // 2)
                            ins = pe.matmul(bk[:], lhsT=hT[:, k, (t - t0) * P:(t - t0 + 1) * P],
                                            rhs=w[:, (k % 2) * 512:(k % 2 + 1) * 512], start=(k == 0), stop=(k == KD - 1))
                        full(ins, (name, t))
                        early(s, "vg", t - t0 + 8 * (name == "g"))
                for j, (b, tb, n) in enumerate(blocks):
                    cols_ = slice((tb - t0) * P, (tb - t0 + n) * P)
                    if b == blocks[0][0]:
                        for m in range(CM):
                            pe.wait_ge(*S["tap_done"].at((s, m, TAPS - 1)))
                    bk = bank(("ln1", b))
                    for m in range(CM):
                        ins = pe.matmul(bk[:, 0:n * P], lhsT=ones[:], rhs=C[:, m, cols_], start=(m == 0), stop=(m == CM - 1))
                    full(ins, ("ln1", b))
                    early(s, "ln", 4 * j)
                    pe.wait_ge(*S["squared"].at(b))
                    bk = bank(("ln2", b))
                    for m in range(CM):
                        ins = pe.matmul(bk[:, 0:n * P], lhsT=ones[:], rhs=U[:, m, cols_], start=(m == 0), stop=(m == CM - 1))
                    full(ins, ("ln2", b))
                    early(s, "ln", 4 * j + 1)
                    pe.wait_ge(*S["conv_act"].at(b))
                    for m in range(CM):
                        bk = bank(("pw2", m, b))
                        for k in range(CM):
                            w = weights_ready(pe, s, "pw2", k // 2)
                            c0 = (k % 2) * 512 + m * P
                            ins = pe.matmul(bk[:, 0:n * P], lhsT=w[:, c0:c0 + P], rhs=C[:, k, cols_],
                                            start=(k == 0), stop=(k == CM - 1))
                        full(ins, ("pw2", m, b))
                        if m % 2:
                            early(s, "ln", 4 * j + 2 + m // 2)
                pe.wait_ge(*S["bank_act"].at(("af", blocks[-1][0])))
                for d in range(2):
                    for pair in range(PAIRS):
                        for b, tb, n in blocks:
                            bk = bank(("gz", d, pair, b))
                            ins = pe.matmul(bk[:, 0:n * P], lhsT=wup[:, d, pair * P:(pair + 1) * P],
                                            rhs=afT[0:2 * RANK, (tb - t0) * P:(tb - t0 + n) * P], start=True, stop=True)
                            full(ins, ("gz", d, pair, b))
                        for j in range(2):
                            early(s, "gates", 4 * d + 2 * pair + j)
                pe.wait_ge(*S["qk_scaled"].at((s, 1, PAIRS - 1, 1)))
                steps = t1 - t0
                last = steps if s == 0 else steps - 1
                for i in range(last):
                    for dp in range(4):
                        d, pair = dp // 2, dp % 2
                        c = i if d == 0 else steps - 1 - i
                        K_ = KF[:, pair, :] if d == 0 else QK[:, 2 + pair, :]
                        bk = bank(("kt", s, i, dp))
                        full(pe.transpose(bk[:, 0:P], K_[:, c * P:(c + 1) * P], ident[:]), ("kt", s, i, dp))
                    early(s, "states", 2 * i)
                    for dp in range(4):
                        d, pair = dp // 2, dp % 2
                        c = i if d == 0 else steps - 1 - i
                        pe.wait_ge(*S["bank_act"].at(("kt", s, i, dp)))
                        bk = bank(("st", s, i, dp))
                        full(pe.matmul(bk[:, 0:2 * HV], lhsT=kT[dp], rhs=V[:, c, pair * 2 * HV:(pair + 1) * 2 * HV],
                                       start=True, stop=True), ("st", s, i, dp))
                    early(s, "states", 2 * i + 1)
                pe.wait_ge(*S["st_kept"].at((s, steps - 1, 3)))

                def out_chunk(c):
                    t = t0 + c
                    pe.wait_ge(*S["scT"].at(t))
                    bk = bank(("o", t))
                    cc = slice(c * P, (c + 1) * P)
                    for h in range(HEADS):
                        pe.matmul(bk[:, h * HV:(h + 1) * HV], lhsT=sct(c)[:, h * P:(h + 1) * P],
                                  rhs=V[:, c, h * HV:(h + 1) * HV], start=(h == 0), stop=False, skip_group_check=True)
                    for pair in range(PAIRS):
                        o = bk[:, pair * 2 * HV:(pair + 1) * 2 * HV]
                        pe.matmul(o, lhsT=QF[:, pair, cc], rhs=ST[0][:, c, pair, :], start=False, stop=False,
                                  skip_group_check=True)
                        ins = pe.matmul(o, lhsT=QK[:, pair, cc], rhs=ST[1][:, c, pair, :], start=False, stop=True,
                                        skip_group_check=True)
                    full(ins, ("o", t))

                def turn_chunk(c):
                    t = t0 + c
                    pe.wait_ge(*S["og"].at(t))
                    bk = bank(("ot", t))
                    for h in range(HEADS):
                        ins = pe.transpose(bk[:, h * P:(h + 1) * P], SG[:, c, h * P:(h + 1) * P], ident[:])
                    full(ins, ("ot", t))

                for c in range(steps + 2):
                    if c < steps:
                        cc = slice(c * P, (c + 1) * P)
                        for name, k_, q_, o_ in (("scb", QK, QK, 2), ("scf", KF, QF, 0)):
                            for odd in range(2):
                                bk = bank((name, odd, t0 + c))
                                rows = slice(odd * HK, (odd + 1) * HK)
                                for pair in range(PAIRS):
                                    ins = pe.matmul(bk[:, pair * P:(pair + 1) * P], lhsT=k_[rows, o_ + pair, cc],
                                                    rhs=q_[rows, pair, cc], start=True, stop=True)
                                full(ins, (name, odd, t0 + c))
                    if 1 <= c <= steps:
                        out_chunk(c - 1)
                    if c >= 2:
                        turn_chunk(c - 2)
                    early(s, "attn", c)
                pe.wait_ge(*S["bank_act"].at(("ot", t1 - 1)))
                for half in range(2):
                    for t in range(t0, t1):
                        bk = bank(("out", half, t))
                        c = t - t0
                        for k in range(KD):
                            w = weights_ready(pe, s, "out", 4 * half + k // 2)
                            l = V[:, c, k * P:(k + 1) * P] if k < 4 else U[:, k - 4, c * P:(c + 1) * P]
                            ins = pe.matmul(bk[:], lhsT=l, rhs=w[:, (k % 2) * 512:(k % 2 + 1) * 512],
                                            start=(k == 0), stop=(k == KD - 1))
                        full(ins, ("out", half, t))
                        early(s, "out", 8 * half + c)
                for j, (b, tb, n) in enumerate(blocks):
                    for t in range(tb, tb + n):
                        pe.wait_ge(*S["h2_ready"].at(t))
                        turn_tile("hT", t)
                        early(s, f"qf{j}", t - tb)
                    pe.wait_ge(*S["bank_act"].at(("hT0", tb + n - 1)))
                    pe.wait_ge(*S["bank_dve"].at(("hT1", tb + n - 1)))
                    pe.wait_ge(*S["sk_in"].at(s))
                    for hp in range(HP + 1):
                        if hp < HP:
                            w = weights_ready(pe, s, "wq", (b, hp))
                            bk = bank(("qf", b, hp))
                            for k in range(KD):
                                ins = pe.matmul(bk[:, 0:n * P], lhsT=w[:, k * P:(k + 1) * P], rhs=H2T[:, k, 0:n * P],
                                                start=(k == 0), stop=(k == KD - 1))
                            full(ins, ("qf", b, hp))
                        if hp:
                            pe.wait_ge(*S["bank_act"].at(("qf", b, hp - 1)))
                            bk = bank(("sc", b, hp - 1))
                            for q in range(n):
                                ins = pe.matmul(bk[:, q * P:(q + 1) * P], lhsT=qfT[(hp - 1) % 2][:, q * P:(q + 1) * P],
                                                rhs=skT[:, hp - 1, :], start=True, stop=True)
                            full(ins, ("sc", b, hp - 1))
                        if hp < HP:
                            early(s, f"qf{j}", 4 + hp)

            def add_rows(i, p, g, first):
                for r in range(RING):
                    pe.wait_ge(S["diag_ready"].sem, i * (2 * SLOTS) + p * SLOTS + g * RING + r + 1)
                    for c in range(2):
                        ins = pe.matmul(wide[p][:, c * 512:(c + 1) * 512], lhsT=diag[r],
                                        rhs=ring[r][:, D + c * 512:D + (c + 1) * 512],
                                        start=(first and r == 0), stop=(r == RING - 1), skip_group_check=True)
                    ins.then_inc(S["slot_used"].sem, 1)

            pe.sem_inc(S["slot_used"].sem, RING)
            with pe.Fori(0, NT // 2 - 1) as i:
                for p in range(2):
                    pe.wait_ge(S["y_ready"].sem, i * 2 + p + 1)
                    add_rows(i, p, 0, True)
                    with pe.Fori(1, SLOTS // RING) as g:
                        add_rows(i, p, g, False)

        @block.scalar
        def _(act):
            def drained(ins, key):
                ins.then_inc(*S["bank_act"].mark(key))

            bank_of = unit_banks()

            def wait_full(key):
                act.wait_ge(*S["bank_full"].at(key))
                return bank_of[key]

            act.wait_ge(*S["small_in"].at("c"))
            act.activation(csil[:], cvec[:], ACT.Silu).then_inc(*S["cs_ready"].mark(0))
            act.wait_ge(*S["consts"].at("all"))

            def pick_exp(tile):
                act.wait_ge(S["gexp_in"].sem, tile + 1)
                act.activation(ge, ge, ACT.Exp).then_inc(S["gexp"].sem, 1)

            def early(s, phase, n):
                c = hook(s, phase, n)
                if not 0 <= c < EARLY:
                    return
                k0 = EC * c
                r0 = k0 % ERING
                t_, g0 = k0 // SLOTS, k0 % SLOTS
                act.wait_ge(*S["dot_e"].at(k0 + EC - 1))
                act.activation(gel_e[:, r0:r0 + EC], dots_e[:, r0:r0 + EC], ACT.Gelu).then_inc(*S["gelu_e"].mark(c))
                act.wait_ge(*S["gelu_e"].at(c))
                for j in range(EC):
                    act.activation(wts_e[:, r0 + j:r0 + j + 1], gel_e[:, r0 + j:r0 + j + 1], ACT.Copy,
                                   scale=gate[t_][:, g0 + j:g0 + j + 1]).then_inc(*S["weight_e"].mark(k0 + j))
                for j in range(EC):
                    act.wait_ge(*S["weight_e"].at(k0 + j))
                    if k0 + j >= ERING:
                        act.wait_ge(*S["used_e"].at(k0 + j - ERING))
                    act.activation(diag_e[r0 + j], ident[:], ACT.Copy, scale=wts_e[:, r0 + j:r0 + j + 1]
                                   ).then_inc(*S["diag_e"].mark(k0 + j))
                if c == PICK_STEPS - 1:
                    pick_exp(1)

            def mean_square(src, sqname, t, col, stdname):
                act.activation(junk, src, ACT.Square, accum_out=ss[:, col, t:t + 1]).then_inc(*S[sqname].mark(t))
                act.wait_ge(*S[sqname].at(t))
                act.activation(rs[:, col, t:t + 1], ss[:, col, t:t + 1], ACT.Sqrt, bias=eps[:], scale=1.0 / D
                               ).then_inc(*S[stdname].mark(t))

            for s, (t0, t1) in enumerate(STREAMS):
                blocks = stream_blocks(s)
                if s == 0:
                    act.wait_ge(*S["modT_ready"].at(0))
                for t in range(t0, t1 + 1):
                    if t < t1:
                        act.wait_ge(*S[f"x_in{t % 2}"].at(t))
                        mean_square(xb[t % 2], "sumsq", t, 0, "std_ready")
                    if t > t0:
                        u = t - 1
                        bk = wait_full(("xT0", u))
                        for k in range(KD // 2):
                            ins = act.activation(hT[:, k, (u - t0) * P:(u - t0 + 1) * P], bk[:, k * P:(k + 1) * P],
                                                 ACT.Identity, bias=modT[:, 0, k, s:s + 1], scale=modT[:, 1, k, s:s + 1])
                        drained(ins, ("xT0", u))
                        early(s, "norm", u - t0)
                n_, before = 0, []
                for m in range(CM):
                    for b, tb, n in blocks:
                        bk = wait_full(("cb", m, b))
                        if n_ >= 2:
                            act.wait_ge(*S["bank_dve"].at(before[n_ - 2]))
                        before.append(("ca", m, b))
                        drained(act.activation(sgt[n_ % 2][:, 0:n * P], bk[:, 0:n * P], ACT.Sigmoid), ("cb", m, b))
                        early(s, "conv", 2 * n_)
                        early(s, "conv", 2 * n_ + 1)
                        n_ += 1
                for m in range(4):
                    for j, (b, tb, n) in enumerate(blocks):
                        bk = wait_full(("qk", m, b))
                        drained(act.activation(QK[:, m, (tb - t0) * P:(tb - t0 + n) * P], bk[:, 0:n * P], ACT.Copy,
                                               scale=HK ** -0.5 if m < 2 else 1.0), ("qk", m, b))
                        early(s, "qk", 2 * m + j)
                for b, tb, n in blocks:
                    bk = wait_full(("af", b))
                    drained(act.activation(afT[0:2 * RANK, (tb - t0) * P:(tb - t0 + n) * P], bk[0:2 * RANK, 0:n * P],
                                           ACT.Copy), ("af", b))
                for t in range(t0, t1):
                    bk = wait_full(("v", t))
                    drained(act.activation(V[:, t - t0, :], bk[:], ACT.Copy), ("v", t))
                    early(s, "vg", t - t0)
                for t in range(t0, t1):
                    bk = wait_full(("g", t))
                    drained(act.activation(SG[:, t - t0, :], bk[:], ACT.Silu), ("g", t))
                    early(s, "vg", 8 + t - t0)
                for j, (b, tb, n) in enumerate(blocks):
                    cols_ = slice((tb - t0) * P, (tb - t0 + n) * P)
                    act.wait_ge(*S["bank_dve"].at(("ln1", b)))
                    for m in range(CM):
                        ins = act.activation(U[:, m, cols_], C[:, m, cols_], ACT.Square)
                    ins.then_inc(*S["squared"].mark(b))
                    early(s, "ln", 4 * j)
                    bk = wait_full(("ln2", b))
                    drained(act.activation(rsb[:, 0:n * P], bk[:, 0:n * P], ACT.Sqrt, bias=eps[:]), ("ln2", b))
                    act.wait_ge(*S["ln_scaled"].at(b))
                    for m in range(CM):
                        ins = act.activation(C[:, m, cols_], C[:, m, cols_], ACT.Silu, bias=cvv[:, 2, m:m + 1],
                                             scale=cvv[:, 1, m:m + 1])
                    ins.then_inc(*S["conv_act"].mark(b))
                    early(s, "ln", 4 * j + 1)
                    for m in range(CM):
                        bk = wait_full(("pw2", m, b))
                        drained(act.activation(U[:, m, cols_], bk[:, 0:n * P], ACT.Copy), ("pw2", m, b))
                        if m % 2:
                            early(s, "ln", 4 * j + 2 + m // 2)
                for d in range(2):
                    for pair in range(PAIRS):
                        key = (s, d, pair)
                        L = (t1 - t0) * P
                        for b, tb, n in blocks:
                            cols_ = slice((tb - t0) * P, (tb - t0 + n) * P)
                            bk = wait_full(("gz", d, pair, b))
                            if (d, pair) == (0, 0):
                                act.wait_ge(*S["bank_full"].at(("pw2", CM - 1, blocks[-1][0])))
                            else:
                                act.wait_ge(*S["qk_scaled"].at((s, *former(d, pair), 1)))
                            act.activation(TMP[:, 1, cols_], bk[:, 0:n * P], ACT.Abs, bias=bup[:, d, pair:pair + 1]
                                           ).then_inc(*S["az"].mark((*key, b)))
                            drained(act.activation(TMP[:, 0, cols_], bk[:, 0:n * P], ACT.Identity,
                                                   bias=bup[:, d, pair:pair + 1]), ("gz", d, pair, b))
                        act.wait_ge(*S["az"].at((*key, blocks[-1][0])))
                        act.activation(TMP[:, 1, 0:L], TMP[:, 1, 0:L], ACT.Exp, scale=-1.0).then_inc(*S["softplus"].mark((*key, 0)))
                        act.wait_ge(*S["softplus"].at((*key, 0)))
                        act.activation(TMP[:, 1, 0:L], TMP[:, 1, 0:L], ACT.Ln, bias=1.0).then_inc(*S["softplus"].mark((*key, 1)))
                        early(s, "gates", 4 * d + 2 * pair)
                        act.wait_ge(*S["cols_in"].at(key))
                        dp = 2 * d + pair
                        act.activation(cols[:, dp, :, 0:t1 - t0], colsin[:, dp, :, 0:t1 - t0], ACT.Exp, scale=1.0 / RANK
                                       ).then_inc(*S["cols_ready"].mark(key))
                        act.activation(TMP[:, 3, 0:L], TMP[:, 2, 0:L], ACT.Exp, scale=-1.0 / RANK).then_inc(*S["exps"].mark((*key, 0)))
                        act.activation(TMP[:, 2, 0:L], TMP[:, 2, 0:L], ACT.Exp, scale=1.0 / RANK).then_inc(*S["exps"].mark((*key, 1)))
                        early(s, "gates", 4 * d + 2 * pair + 1)
                steps = t1 - t0
                last = steps if s == 0 else steps - 1
                act.wait_ge(*S["ln_scaled"].at(blocks[-1][0]))
                for i in range(last):
                    for dp in range(4):
                        bk = wait_full(("kt", s, i, dp))
                        if i:
                            act.wait_ge(*S["bank_full"].at(("st", s, i - 1, dp)))
                        drained(act.activation(kT[dp], bk[:, 0:P], ACT.Copy), ("kt", s, i, dp))
                    for j in range(2):
                        early(s, "states", 2 * i + j)
                def o_stats(c):
                    t = t0 + c
                    bk = wait_full(("o", t))
                    for h in range(HEADS):
                        if h or c:
                            act.wait_ge(*S["osum"].at((t, h - 1) if h else (t - 1, HEADS - 1)))
                        act.activation(xb[0][:, 512:640], bk[:, h * HV:(h + 1) * HV], ACT.Square,
                                       accum_out=oss[:, t, h:h + 1]).then_inc(*S["osum"].mark((t, h)))
                    act.wait_ge(*S["osum"].at((t, HEADS - 1)))
                    act.activation(ors[:, t, :], oss[:, t, :], ACT.Sqrt, bias=eps[:], scale=1.0 / HV
                                   ).then_inc(*S["ostd"].mark(t))

                def turn_out(c):
                    t = t0 + c
                    bk = wait_full(("ot", t))
                    drained(act.activation(V[:, c, :], bk[:], ACT.Copy), ("ot", t))

                for c in range(steps + 2):
                    if c < steps:
                        if c >= 2:
                            act.wait_ge(*S["bank_full"].at(("o", t0 + c - 2)))
                        for odd in range(2):
                            bk = wait_full(("scb", odd, t0 + c))
                            drained(act.activation(by_head(sct(c), odd), bk[:, 0:2 * P].rearrange("p (a n) -> p a n", n=P),
                                                   ACT.Copy), ("scb", odd, t0 + c))
                    if 1 <= c <= steps:
                        o_stats(c - 1)
                    if c >= 2:
                        turn_out(c - 2)
                    early(s, "attn", c)
                for n in range(16):
                    early(s, "out", n)
                for j, (b, tb, n) in enumerate(blocks):
                    for t in range(tb, tb + n + 1):
                        if t < tb + n:
                            act.wait_ge(*S["x1_ready"].at((1, t)))
                            mean_square(X1[:, t - t0, :], "sumsq2", t, 1, "std2")
                        if t > tb:
                            u = t - 1
                            bk = wait_full(("hT0", u))
                            if b > blocks[0][0]:
                                act.wait_ge(*S["bank_full"].at(("qf", b - 1, HP - 1)))
                            cc = slice((u - tb) * P, (u - tb + 1) * P)
                            drained(act.activation(H2T[:, 0:4, cc], bk[:].rearrange("p (k n) -> p k n", k=4), ACT.Copy),
                                    ("hT0", u))
                            early(s, f"qf{j}", u - tb)
                    for hp in range(HP):
                        bk = wait_full(("qf", b, hp))
                        if hp >= 2:
                            act.wait_ge(*S["bank_full"].at(("sc", b, hp - 2)))
                        elif b > blocks[0][0]:
                            act.wait_ge(*S["bank_full"].at(("sc", b - 1, HP - 2 + hp)))
                        drained(act.activation(qfT[hp % 2][:, 0:n * P], bk[:, 0:n * P], ACT.Copy), ("qf", b, hp))
                        early(s, f"qf{j}", 4 + hp)
                if s == 0:
                    pick_exp(0)

            def group(i, p, g):
                for half in range(RING // GROUP):
                    j = half * GROUP
                    act.wait_ge(S["dot"].sem, i * (2 * SLOTS) + p * SLOTS + g * RING + j + GROUP)
                    act.activation(gel[:, j:j + GROUP], dots[:, j:j + GROUP], ACT.Gelu).then_inc(S["gelu"].sem, 1)
                    act.wait_ge(S["weight"].sem, i * (2 * SLOTS // GROUP) + p * (SLOTS // GROUP) + g * (RING // GROUP) + half + 1)
                    for r in range(j, j + GROUP):
                        act.activation(diag[r], ident[:], ACT.Copy, scale=wts[:, r:r + 1]).then_inc(S["diag_ready"].sem, 1)

            def result(p, tile):
                act.wait_ge(S["y_pre"].sem, tile * 2 + 2)
                act.activation(pick_at[2][1][:, 0:D], x1b[p], ACT.Square, accum_out=fss[:, p:p + 1]).then_inc(S["y_sum"].sem, 1)
                act.wait_ge(S["y_sum"].sem, tile + 1)
                act.activation(frs[:, p:p + 1], fss[:, p:p + 1], ACT.Sqrt, bias=eps[:], scale=1.0 / D
                               ).then_inc(S["y_std"].sem, 1)
                act.wait_ge(S["y_ready"].sem, tile + 1)
                act.sem_inc(S["act_pace"].sem)
                act.dma_start(a["y"][bass.ds(tile * P, P), :], x1b[p]).then_inc(S[f"y_out{p}"].sem, 16)

            pick_exp(2)
            for t in range(2):
                result(t, t)
            with act.Fori(0, NT // 2 - 1) as i:
                for p in range(2):
                    tile = i * 2 + p + 2
                    with act.Fori(0, PICK_DONE, 4) as g:
                        for q in range(4):
                            group(i, p, g + q)
                    pick_exp(tile + 1)
                    for g in range(PICK_DONE, SLOTS // RING):
                        group(i, p, g)
                    result(p, tile)

        @block.vector
        def _(dve):
            def drained(ins, key):
                ins.then_inc(*S["bank_dve"].mark(key))

            bank_of = unit_banks()

            def wait_full(key):
                dve.wait_ge(*S["bank_full"].at(key))
                return bank_of[key]

            dve.wait_ge(*S["consts"].at("all"))
            dve.wait_ge(*S["small_in"].at("all"))
            for n in range(12):
                bk = wait_full(("mod", n))
                drained(dve.tensor_tensor(modrow[:, n * 512:(n + 1) * 512], bk[0:2, :], bmod[:, n * 512:(n + 1) * 512],
                                          ALU.add), ("mod", n))
            dve.wait_ge(*S["bank_dve"].at(("mod", 11)))
            for name, at, g in (("a1", 1, 0), ("a2", 4, 1)):
                r = modrow[:, at * D:(at + 1) * D]
                dve.scalar_tensor_tensor(out=r, in0=r, scalar=1.0, in1=grow[:, g, :], op0=ALU.add, op1=ALU.mult
                                         ).then_inc(*S["mod_rows"].mark(name))
            dve.wait_ge(*S["mod_cols"].at(0))
            dve.tensor_copy(modT[:].rearrange("p a k s -> p (a k s)"), wide[0][:, 0:4 * KD]).then_inc(*S["modT_ready"].mark(0))

            chain = S["pick"]

            def pick_step(tile, q, p=None, where=None):
                if p is None:
                    p, where = tile % 2, pick_at[0 if tile < 2 else 1]
                scr, oneh = where
                count = [5 * q if q < HP else 5 * HP + 6 * (q - HP)]

                def after(scan=False):
                    if count[0]:
                        dve.wait_ge(chain.sem, tile * CHAIN + count[0])
                        if scan and not isinstance(tile, int):
                            dve.sem_inc(S["x_pace"].sem)

                def done(ins):
                    count[0] += 1
                    ins.then_inc(chain.sem, 1)

                def top16(src, vals, places):
                    done(dve.max(vals[:, 0:8], src))
                    after(scan=True)
                    done(dve.max_index(places[:, 0:8], vals[:, 0:8], src))
                    after(scan=True)
                    done(dve.match_replace(src, vals[:, 0:8], src, NEG))
                    after(scan=True)
                    done(dve.max(vals[:, 8:16], src))
                    after(scan=True)
                    done(dve.max_index(places[:, 8:16], vals[:, 8:16], src))

                def keys(hp):
                    if hp == 0:
                        if isinstance(tile, int) and tile < 2:
                            dve.wait_ge(S["scr1_in" if tile else "scr_in"].sem, 16)
                        else:
                            dve.wait_ge(S["scr_in"].sem, tile * 16)
                        dve.sem_inc(S["x_pace"].sem)
                    top16(scr[:, hp * NKEYS:(hp + 1) * NKEYS], sv[:, hp * TOPK:(hp + 1) * TOPK],
                          si[:, hp * TOPK:(hp + 1) * TOPK])

                def head(h):
                    after()
                    va, vb = (sv[:, (2 * h + r) * TOPK:(2 * h + r + 1) * TOPK] for r in range(2))
                    cd = cand[h % 2]
                    done(dve.tensor_tensor(cd.rearrange("p (a b) -> p a b", b=TOPK),
                                           va.unsqueeze(2).to_broadcast([P, TOPK, TOPK]),
                                           vb.unsqueeze(1).to_broadcast([P, TOPK, TOPK]), ALU.add))
                    after(scan=True)
                    top16(cd, ts[:, h * TOPK:(h + 1) * TOPK], pos[:, h * TOPK:(h + 1) * TOPK])

                def finish():
                    after()
                    t3 = ts.rearrange("p (h k) -> p h k", k=TOPK)
                    g3 = ge.rearrange("p (h k) -> p h k", k=TOPK)
                    dve.tensor_tensor(g3, t3, t3[:, :, 0:1].to_broadcast([P, PH, TOPK]), ALU.subtract
                                      ).then_inc(S["gexp_in"].sem, 1)
                    done(dve.tensor_copy(sf, si))
                    after()
                    done(dve.tensor_scalar(pab[0], pos, 4, None, ALU.logical_shift_right))
                    done(dve.tensor_scalar(pab[1], pos, 15, None, ALU.bitwise_and))
                    for r in range(2):
                        after()
                        done(dve.tensor_copy(pf[r], pab[r]))
                        after()
                        o3 = oneh.rearrange("p (j a) -> p j a", a=TOPK)
                        done(dve.tensor_tensor(o3, pf[r].unsqueeze(2).to_broadcast([P, SLOTS, TOPK]),
                                               iota16[:].unsqueeze(1).to_broadcast([P, SLOTS, TOPK]), ALU.is_equal))
                        after()
                        o4 = oneh.rearrange("p (h k a) -> p h k a", k=TOPK, a=TOPK)
                        s4 = sf.rearrange("p (h r a) -> p h r a", r=2, a=TOPK)[:, :, r:r + 1, :]
                        done(dve.tensor_tensor(o4, o4, s4.to_broadcast([P, PH, TOPK, TOPK]), ALU.mult))
                        after()
                        done(dve.tensor_reduce(pi[r], o3, AX.X, ALU.add))
                    after()
                    done(dve.scalar_tensor_tensor(out=idx[p][:], in0=pi[0], scalar=float(NKEYS), in1=pi[1],
                                                  op0=ALU.mult, op1=ALU.add))
                    after()
                    dve.wait_ge(S["gexp"].sem, tile + 1)
                    done(dve.tensor_reduce(gsum, g3, AX.X, ALU.add))
                    after()
                    done(dve.reciprocal(gsum, gsum))
                    after()
                    done(dve.tensor_tensor(gate[p].rearrange("p (h k) -> p h k", k=TOPK), g3,
                                           gsum.unsqueeze(2).to_broadcast([P, PH, TOPK]), ALU.mult))
                    after()
                    dve.sem_inc(S["idx_ready"].sem)
                    assert count[0] == CHAIN

                if q < HP:
                    keys(q)
                elif q < HP + PH:
                    head(q - HP)
                else:
                    finish()

            def early(s, phase, n):
                c = hook(s, phase, n)
                if not 0 <= c < EARLY:
                    return
                if c == 0:
                    dve.wait_ge(*S["h2e_in"].at(0))
                for k in range(EC * c, EC * c + EC):
                    r_ = k % ERING
                    dve.wait_ge(*landed_e[r_].at(k))
                    if k >= ERING:
                        dve.wait_ge(*S["gelu_e"].at((k - ERING) // EC))
                    dve.tensor_tensor_reduce(out=ring_e[r_][:, 0:D], in0=ring_e[r_][:, 0:D], in1=h2e[k // SLOTS], scale=1.0,
                                             scalar=0.0, op0=ALU.mult, op1=ALU.add, accum_out=dots_e[:, r_:r_ + 1]
                                             ).then_inc(*S["dot_e"].mark(k))
                if c < PICK_STEPS:
                    pick_step(1, c)

            for s, (t0, t1) in enumerate(STREAMS):
                blocks = stream_blocks(s)
                L = (t1 - t0) * P
                for t in range(t0, t1 + 1):
                    if t < t1:
                        dve.wait_ge(*S["std_ready"].at(t))
                        dve.reciprocal(rs[:, 0, t:t + 1], rs[:, 0, t:t + 1]).then_inc(*S["rstd"].mark(t))
                        dve.wait_ge(*S["rstd"].at(t))
                        dve.tensor_scalar(xb[t % 2], xb[t % 2], rs[:, 0, t:t + 1], None, ALU.mult).then_inc(*S["xn_ready"].mark(t))
                    if t > t0:
                        u = t - 1
                        bk = wait_full(("xT1", u))
                        if u == 0:
                            dve.wait_ge(*S["modT_ready"].at(0))
                        for k in range(4, KD):
                            ins = dve.tensor_scalar(hT[:, k, (u - t0) * P:(u - t0 + 1) * P], bk[:, (k - 4) * P:(k - 3) * P],
                                                    modT[:, 1, k, s:s + 1], modT[:, 0, k, s:s + 1], ALU.mult, ALU.add)
                        drained(ins, ("xT1", u))
                        early(s, "norm", u - t0)
                n_ = 0
                for m in range(CM):
                    for b, tb, n in blocks:
                        early(s, "conv", 2 * n_)
                        bk = wait_full(("ca", m, b))
                        dve.wait_ge(*S["bank_act"].at(("cb", m, b)))
                        drained(dve.tensor_tensor(U[:, m, (tb - t0) * P:(tb - t0 + n) * P], bk[:, 0:n * P],
                                                  sgt[n_ % 2][:, 0:n * P], ALU.mult), ("ca", m, b))
                        early(s, "conv", 2 * n_ + 1)
                        n_ += 1
                dve.wait_ge(*S["bank_dve"].at(("ca", CM - 1, blocks[-1][0])))
                offsets = [0] + [d for k in range(1, PAD + 1) for d in (-k, k)]
                for j, d in enumerate(offsets):
                    for m in range(CM):
                        w = cw[:, m, d + PAD:d + PAD + 1]
                        if j:
                            dve.wait_ge(*S["tap_done"].at((s, m, j - 1)))
                        if s == 0:
                            lo, hi = max(0, -d), min(L, L - d)
                            o, x = C[:, m, lo:hi], U[:, m, lo + d:hi + d]
                        elif m < CM // 2:
                            lo, hi = max(0, -d), min(GRID, GRID - d)
                            g_ = lambda r: r[:, m, 0:L].rearrange("p (r c) -> p r c", c=GRID)
                            o, x = g_(C)[:, :, lo:hi], g_(U)[:, :, lo + d:hi + d]
                        else:
                            lo, hi = max(0, -d) * GRID, min(L, L - d * GRID)
                            o, x = C[:, m, lo:hi], U[:, m, lo + d * GRID:hi + d * GRID]
                        if j == 0:
                            dve.tensor_scalar(o, x, w, cvv[:, 0, m:m + 1], ALU.mult, ALU.add
                                              ).then_inc(*S["tap_done"].mark((s, m, j)))
                        else:
                            dve.scalar_tensor_tensor(out=o, in0=x, scalar=w, in1=o, op0=ALU.mult, op1=ALU.add
                                                     ).then_inc(*S["tap_done"].mark((s, m, j)))
                        taps_done = j * CM + m + 1
                        if taps_done % 5 == 0 and taps_done <= 5 * 24:
                            early(s, "qk", taps_done // 5 - 1)
                for t in range(t0, t1):
                    dve.wait_ge(*S["bank_act"].at(("g", t)))
                    dve.tensor_tensor(SG[:, t - t0, :], SG[:, t - t0, :], gnb[:], ALU.mult).then_inc(*S["sg_ready"].mark(t))
                for j, (b, tb, n) in enumerate(blocks):
                    cols_ = slice((tb - t0) * P, (tb - t0 + n) * P)
                    bk = wait_full(("ln1", b))
                    for m in range(CM):
                        ins = dve.tensor_tensor(C[:, m, cols_], C[:, m, cols_], bk[:, 0:n * P], ALU.subtract)
                    drained(ins, ("ln1", b))
                    early(s, "ln", 4 * j)
                    dve.wait_ge(*S["bank_act"].at(("ln2", b)))
                    dve.reciprocal(rsb[:, 0:n * P], rsb[:, 0:n * P]).then_inc(*S["ln_rstd"].mark(b))
                    dve.wait_ge(*S["ln_rstd"].at(b))
                    for m in range(CM):
                        ins = dve.tensor_tensor(C[:, m, cols_], C[:, m, cols_], rsb[:, 0:n * P], ALU.mult)
                    ins.then_inc(*S["ln_scaled"].mark(b))
                    for q in range(1, 4):
                        early(s, "ln", 4 * j + q)
                nt = t1 - t0
                for d in range(2):
                    for pair in range(PAIRS):
                        key, dp = (s, d, pair), 2 * d + pair
                        z, l, x = TMP[:, 0, 0:L], TMP[:, 1, 0:L], TMP[:, 2, 0:L]
                        xc, lc = (r.rearrange("p (c n) -> p c n", n=P) for r in (x, l))
                        ci = colsin[:, dp, :, 0:nt]
                        early(s, "gates", 4 * d + 2 * pair)
                        dve.wait_ge(*S["softplus"].at((*key, 1)))
                        dve.scalar_tensor_tensor(out=z, in0=z, scalar=0.0, in1=l, op0=ALU.min, op1=ALU.subtract
                                                 ).then_inc(*S["g_ready"].mark(key))
                        dve.wait_ge(*S["g_ready"].at(key))
                        for c in range(nt):
                            cc = slice(c * P, (c + 1) * P)
                            ins = dve.tensor_tensor_scan(l[:, cc], one[:], z[:, cc], 0.0, ALU.mult, ALU.add)
                        ins.then_inc(*S["scan"].mark(key))
                        dve.wait_ge(*S["scan"].at(key))
                        if d == 0:
                            mid = lc[:, :, P // 2 - 1:P // 2]
                            end = lc[:, :, P - 1]
                            dve.tensor_copy(ci[:, 0, :], mid.rearrange("p c n -> p (c n)"))
                            dve.tensor_copy(ci[:, 1, :], end)
                            dve.tensor_tensor(ci[:, 2, :], end, mid.rearrange("p c n -> p (c n)"), ALU.subtract)
                            dve.tensor_tensor(xc, lc, mid.to_broadcast([P, nt, P]), ALU.subtract
                                              ).then_inc(*S["cols_in"].mark(key))
                        else:
                            dve.tensor_tensor(z, z, l, ALU.subtract).then_inc(*S["span"].mark(key))
                            dve.wait_ge(*S["span"].at(key))
                            zc = z.rearrange("p (c n) -> p c n", n=P)
                            mid = zc[:, :, P // 2:P // 2 + 1]
                            end = lc[:, :, P - 1]
                            dve.tensor_tensor(ci[:, 0, :], end, mid.rearrange("p c n -> p (c n)"), ALU.add)
                            dve.tensor_copy(ci[:, 1, :], end)
                            dve.tensor_scalar(ci[:, 2, :], mid.rearrange("p c n -> p (c n)"), -1.0, None, ALU.mult)
                            dve.tensor_tensor(xc, zc, mid.to_broadcast([P, nt, P]), ALU.subtract
                                              ).then_inc(*S["cols_in"].mark(key))
                        Q_, K_ = (QF, KF) if d == 0 else (QK, QK[:, 2:4, :])
                        dve.wait_ge(*S["exps"].at((*key, 0)))
                        if d == 0:
                            dve.wait_ge(*S["bank_full"].at(("g", t1 - 1)))
                        dve.tensor_tensor(K_[:, pair, 0:L], QK[:, 2 + pair, 0:L], TMP[:, 3, 0:L], ALU.mult
                                          ).then_inc(*S["qk_scaled"].mark((*key, 0)))
                        dve.wait_ge(*S["exps"].at((*key, 1)))
                        dve.tensor_tensor(Q_[:, pair, 0:L], QK[:, pair, 0:L], TMP[:, 2, 0:L], ALU.mult
                                          ).then_inc(*S["qk_scaled"].mark((*key, 1)))
                        early(s, "gates", 4 * d + 2 * pair + 1)
                if s == 0:
                    dve.wait_ge(*S["bank_full"].at(("xT1", t1 - 1)))
                    for dp in range(4):
                        dve.memset(Scur[dp], 0.0).then_inc(*S["st_next"].mark((s, -1, dp)))
                else:
                    dve.wait_ge(*S["state_in"].at(s))
                last = nt if s == 0 else nt - 1
                dve.wait_ge(*S["cols_ready"].at((s, 1, 1)))
                dve.wait_ge(*S["qk_scaled"].at((s, 1, PAIRS - 1, 1)))
                for d in range(2):
                    dve.memset(ST[d][:, 0:nt].rearrange("p c d n -> p (c d n)"), 0.0).then_inc(*S["st_zero"].mark(s))
                dve.wait_ge(*S["st_zero"].at(s))
                for i in range(nt):
                    for dp in range(4):
                        c = i if dp < 2 else nt - 1 - i
                        T_ = cols[:, dp, 1, c:c + 1]
                        if i or s == 0:
                            dve.wait_ge(*S["st_next"].at((s, i - 1, dp)))
                        for r in range(2):
                            h = slice(r * HK, (r + 1) * HK)
                            ins = dve.tensor_scalar(ST[dp // 2][h, c, dp % 2, r * HV:(r + 1) * HV], Scur[dp][h, :],
                                                    cols[h, dp, 0, c:c + 1], None, ALU.mult)
                        ins.then_inc(*S["st_kept"].mark((s, i, dp)))
                        if i < last:
                            dve.tensor_scalar(Stmp[dp], Scur[dp], T_, None, ALU.mult).then_inc(*S["st_tmp"].mark((s, i, dp)))
                    if i < last:
                        early(s, "states", 2 * i)
                        for dp in range(4):
                            c = i if dp < 2 else nt - 1 - i
                            bk = wait_full(("st", s, i, dp))
                            dve.wait_ge(*S["st_tmp"].at((s, i, dp)))
                            dve.wait_ge(*S["st_kept"].at((s, i, dp)))
                            for r in range(2):
                                h = slice(r * HK, (r + 1) * HK)
                                ins = dve.scalar_tensor_tensor(out=Scur[dp][h, :], in0=bk[h, r * HV:(r + 1) * HV],
                                                               scalar=cols[h, dp, 2, c:c + 1], in1=Stmp[dp][h, :],
                                                               op0=ALU.mult, op1=ALU.add)
                                if r == 0:
                                    ins.then_inc(*S["st_next"].mark((s, i, dp, "half")))
                                else:
                                    ins.then_inc(*S["st_next"].mark((s, i, dp)))
                        early(s, "states", 2 * i + 1)
                def normalise(c):
                    t = t0 + c
                    dve.wait_ge(*S["ostd"].at(t))
                    dve.reciprocal(ors[:, t, :], ors[:, t, :]).then_inc(*S["orstd"].mark(t))
                    dve.wait_ge(*S["orstd"].at(t))
                    dve.wait_ge(*S["sg_ready"].at(t))
                    bk = bank_of[("o", t)]
                    for h in range(HEADS):
                        hc = slice(h * HV, (h + 1) * HV)
                        ins = dve.scalar_tensor_tensor(out=SG[:, c, hc], in0=bk[:, hc], scalar=ors[:, t, h:h + 1],
                                                       in1=SG[:, c, hc], op0=ALU.mult, op1=ALU.mult)
                    ins.then_inc(*S["og"].mark(t))

                for c in range(nt + 1):
                    if c < nt:
                        for odd in range(2):
                            bk = wait_full(("scf", odd, t0 + c))
                            dve.wait_ge(*S["bank_act"].at(("scb", odd, t0 + c)))
                            drained(dve.copy_predicated(by_head(sct(c), odd), keep_f[:, 0:2, :],
                                                        bk[:, 0:2 * P].rearrange("p (a n) -> p a n", n=P)),
                                    ("scf", odd, t0 + c))
                        dve.wait_ge(*S["bank_dve"].at(("scf", 1, t0 + c)))
                        dve.tensor_tensor(sct(c), sct(c), twice_d[:].rearrange("p h n -> p (h n)"), ALU.mult
                                          ).then_inc(*S["scT"].mark(t0 + c))
                    if c:
                        normalise(c - 1)
                    early(s, "attn", c)
                early(s, "attn", nt + 1)
                dve.wait_ge(*S["bc_in"].at(s))
                dve.wait_ge(*S["x1_in"].at(s))
                n_ = 0
                for half in range(2):
                    hc = slice(half * 512, (half + 1) * 512)
                    for t in range(t0, t1):
                        bk = wait_full(("out", half, t))
                        tmp = TMP[:, n_ % 2, 0:512]
                        drained(dve.tensor_tensor(tmp, bk[:], gate1b[:, hc], ALU.mult), ("out", half, t))
                        dve.wait_ge(*S["bank_dve"].at(("out", half, t)))
                        dve.tensor_tensor(X1[:, t - t0, hc], X1[:, t - t0, hc], tmp, ALU.add).then_inc(*S["x1_ready"].mark((half, t)))
                        early(s, "out", n_)
                        n_ += 1
                for j, (b, tb, n) in enumerate(blocks):
                    for t in range(tb, tb + n + 1):
                        if t < tb + n:
                            dve.wait_ge(*S["std2"].at(t))
                            dve.reciprocal(rs[:, 1, t:t + 1], rs[:, 1, t:t + 1]).then_inc(*S["rstd2"].mark(t))
                            dve.wait_ge(*S["rstd2"].at(t))
                            if t >= t0 + 2:
                                dve.wait_ge(*S["bank_full"].at(("hT1", t - 2)))
                                dve.wait_ge(*S[f"h2_out{t % 2}"].at(t - 2))
                            elif s == 0:
                                dve.wait_ge(*S["state_out"].at(s))
                            dve.scalar_tensor_tensor(out=xb[t % 2], in0=X1[:, t - t0, :], scalar=rs[:, 1, t:t + 1],
                                                     in1=a2b, op0=ALU.mult, op1=ALU.mult).then_inc(*S["h2_pre"].mark(t))
                            dve.wait_ge(*S["h2_pre"].at(t))
                            dve.tensor_tensor(xb[t % 2], xb[t % 2], shift2b, ALU.add).then_inc(*S["h2_ready"].mark(t))
                        if t > tb:
                            u = t - 1
                            bk = wait_full(("hT1", u))
                            if b > blocks[0][0]:
                                dve.wait_ge(*S["bank_full"].at(("qf", b - 1, HP - 1)))
                            cc = slice((u - tb) * P, (u - tb + 1) * P)
                            drained(dve.tensor_copy(H2T[:, 4:8, cc], bk[:].rearrange("p (k n) -> p k n", k=4)), ("hT1", u))
                            early(s, f"qf{j}", u - tb)
                    for hp in range(HP):
                        bk = wait_full(("sc", b, hp))
                        quad = hp // 4
                        if hp % 4 == 0:
                            if quad >= 2:
                                dve.wait_ge(*S[f"sc_out{quad % 2}"].at((b, quad - 2)))
                            elif b > 0:
                                dve.wait_ge(*S[f"sc_out{quad % 2}"].at((b - 1, quad + 2)))
                        drained(dve.tensor_copy(scb[quad % 2][:, 0:n, hp % 4, :],
                                                bk[:, 0:n * P].rearrange("p (t n) -> p t n", n=NKEYS)), ("sc", b, hp))
                        early(s, f"qf{j}", 4 + hp)
                        if b == 2:
                            for q in range(hp * 24 // HP, (hp + 1) * 24 // HP):
                                pick_step(2, q)
                if s == 0:
                    for q in range(PICK_STEPS):
                        pick_step(0, q)
                else:
                    pick_step(2, PICK_STEPS - 1)

            def result(p, tile, base):
                dve.tensor_tensor(h2b[p], wide[p][:], gate2b[p], ALU.mult).then_inc(S["y_pre"].sem, 1)
                dve.wait_ge(S["y_pre"].sem, tile * 2 + 1)
                dve.tensor_tensor(x1b[p], x1b[p], h2b[p], ALU.add).then_inc(S["y_pre"].sem, 1)
                dve.wait_ge(S["y_std"].sem, tile + 1)
                dve.reciprocal(frs[:, p:p + 1], frs[:, p:p + 1]).then_inc(S["y_std_done"].sem, 1)
                dve.wait_ge(S["y_std_done"].sem, tile + 1)
                dve.scalar_tensor_tensor(out=x1b[p], in0=x1b[p], scalar=frs[:, p:p + 1], in1=finalb,
                                         op0=ALU.mult, op1=ALU.mult).then_inc(S["y_ready"].sem, 1)

            dve.wait_ge(*S["final_in"].at(0))
            for t in range(2):
                dve.wait_ge(*S["used_e"].at(2 * SLOTS - 1))
                dve.wait_ge(*S[f"tile_in{t}"].at(t))
                result(t, t, 0)
            with dve.Fori(0, NT // 2 - 1) as i:
                for p in range(2):
                    tile = i * 2 + p + 2
                    dve.wait_ge(S[f"tile_in{p}"].sem, i * 48 + 96)
                    dve.sem_inc(S["x_pace"].sem)
                    for g in range(SLOTS // RING):
                        for half in range(RING // GROUP):
                            for r in range(half * GROUP, (half + 1) * GROUP):
                                dve.wait_ge(landed[r], i * (32 * SLOTS // RING) + (p * SLOTS // RING + g + 1) * 16)
                                dve.tensor_tensor_reduce(out=ring[r][:, 0:D], in0=ring[r][:, 0:D], in1=h2b[p], scale=1.0,
                                                         scalar=0.0, op0=ALU.mult, op1=ALU.add, accum_out=dots[:, r:r + 1]
                                                         ).then_inc(S["dot"].sem, 1)
                            if half == 0:
                                steps = range(4 * g, 4 * g + 4) if g < 4 else range(HP + g - 4, HP + g - 3)
                                for q in steps:
                                    if q < PICK_STEPS:
                                        pick_step(tile + 1, q, 1 - p, pick_at[2])
                            n = p * (SLOTS // GROUP) + g * (RING // GROUP) + half + 1
                            j = half * GROUP
                            dve.wait_ge(S["gelu"].sem, i * (2 * SLOTS // GROUP) + n)
                            dve.tensor_tensor(wts[:, j:j + GROUP], gel[:, j:j + GROUP],
                                              gate[p][:, g * RING + j:g * RING + j + GROUP], ALU.mult
                                              ).then_inc(S["weight"].sem, 1)
                    dve.wait_ge(S["slot_used"].sem, i * (2 * SLOTS) + (p + 1) * SLOTS + RING)
                    result(p, tile, None)


CHAIN = 5 * HP + 6 * PH + 15
PICK_STEPS = HP + PH + 1
PICK_DONE = 12


def kernel(**inputs):
    import numpy as np
    import concourse.bacc as _bacc
    from concourse.bass_utils import run_bass_kernel_spmd as _run

    f = {k: np.asarray(v) for k, v in inputs.items()}

    def by_partition(w, parts):
        return w.reshape(parts, P, -1).transpose(1, 0, 2)

    w_in = by_partition(f["w_in"][0], KD)
    col_at = [0, DK, 2 * DK, 2 * DK + DV, 2 * DK + 2 * DV, 2 * DK + 2 * DV + 2 * RANK]
    ca0 = col_at[5]
    cb0 = ca0 + CH
    starts = [0, P, DK, DK + P] + [ca0 + m * P for m in range(CM)] + [cb0 + m * P for m in range(CM)]
    w_vg = []
    for c0 in (2 * DK, 2 * DK + DV):
        for c in range(4):
            w_vg.append(w_in[:, 2 * c:2 * c + 2, c0:c0 + DV].reshape(P, D))
    w_up = np.zeros((2 * RANK, 2, DK), np.float32)
    w_up[0:RANK, 0] = f["w_af_up"][0]
    w_up[RANK:, 1] = f["w_ab_up"][0]
    pw2 = by_partition(f["conv_pw2"][0], CM)
    w_out = by_partition(f["w_out"][0], KD)
    wq = by_partition(f["peer_wq"][0], KD)
    ins = {
        "x": np.concatenate([f["x_prompt"][0], f["x_sample"][0]], axis=0),
        "c2": np.stack([f["c_ctx"], f["c"][0]], axis=1).reshape(KD, P, 2).transpose(1, 0, 2),
        "w_mod": by_partition(f["w_mod"][0], KD).reshape(P, KD, 12, 512).transpose(2, 0, 1, 3),
        "b_mod": f["b_mod"],
        "norm1_g": f["norm1_g"], "norm2_g": f["norm2_g"],
        "w_cols": np.stack([w_in[:, :, c:c + P].reshape(P, D) for c in starts]),
        "w_af": w_in[:, :, col_at[4]:col_at[4] + 2 * RANK].reshape(P, KD * 2 * RANK),
        "w_vg": np.stack(w_vg),
        "w_up": w_up,
        "b_up": np.stack([f["b_af"][0], f["b_ab"][0]]).reshape(2, PAIRS, P).transpose(2, 0, 1),
        "gla_g": f["gla_norm_g"][0],
        "conv_w": f["conv_dw_w"][0].T.reshape(CM, P, TAPS).transpose(1, 0, 2),
        "conv_v": np.stack([f["conv_dw_b"][0], f["conv_ln_g"][0], f["conv_ln_b"][0]]).reshape(3, CM, P).transpose(2, 0, 1),
        "w_pw2": np.stack([pw2[:, 2 * c:2 * c + 2].reshape(P, D) for c in range(2)]),
        "w_out": np.stack([w_out[:, 2 * c:2 * c + 2, h * 512:(h + 1) * 512].reshape(P, D) for h in range(2) for c in range(4)]),
        "w_q": np.stack([wq[:, :, m * P:(m + 1) * P].reshape(P, D) for m in range(HP)]),
        "sk": f["peer_subkeys"][0].reshape(HP, NKEYS, P).transpose(2, 0, 1),
        "uv": np.concatenate([f["peer_u"][0], f["peer_v"][0]], axis=1),
        "final_g": f["final_norm_g"],
        "state_f": f["state_gla_fwd"].reshape(DK, HV),
        "state_b": f["state_gla_bwd"].reshape(DK, HV),
    }
    ins = {k: np.ascontiguousarray(v) for k, v in ins.items()}

    def program(counts):
        nc = _bacc.Bacc("TRN2", target_bir_lowering=False, num_devices=1)
        a = {k: nc.dram_tensor(f"in_{k}", v.shape, F32, kind="ExternalInput").ap() for k, v in ins.items()}
        for k, shape in (("y", (NT * P, D)), ("new_f", (DK, HV)), ("new_b", (DK, HV))):
            a[k] = nc.dram_tensor(f"out_{k}", shape, F32, kind="ExternalOutput").ap()
        build(nc, a, counts)
        return nc

    counts = {}
    program(counts)
    nc = program(counts)
    r = _run(nc, [{f"in_{k}": v for k, v in ins.items()}], core_ids=[0]).results[0]
    y = r["out_y"]
    state = (1, 1, HEADS, HK, HV)
    n0 = STREAMS[0][1] * P
    return (y[None, :n0], y[None, n0:], r["out_new_f"].reshape(state), r["out_new_b"].reshape(state))
```

```python
from contextlib import ExitStack

import concourse.bass as bass
from concourse import mybir

F32 = mybir.dt.float32
U32 = mybir.dt.uint32
ALU = mybir.AluOpType
ACT = mybir.ActivationFunctionType
AX = mybir.AxisListType

P = 128
D = 1024
KD = D // P
EPS = 1e-6
HEADS, HK, HV = 4, 64, 128
PAIRS = HEADS // 2
DK, DV = HEADS * HK, HEADS * HV
RANK = 16
CH = 512
CM = CH // P
TAPS = 31
PAD = TAPS // 2
GRID = 64
PH, NKEYS, TOPK = 8, 128, 16
HP = 2 * PH
SLOTS = PH * TOPK
NEG = -3.0e38
STREAMS = ((0, 2), (2, 10))
NT = STREAMS[1][1]
MAXL = P * (STREAMS[1][1] - STREAMS[1][0])
WSLOTS = 4
RING = 16
GROUP = 4
ERING = 4
EC = 2
EARLY = 2 * SLOTS // EC


class Signal:

    def __init__(self, sem, counts):
        self.sem, self.counts, self.n = sem, counts, 0
        self.known = bool(counts)

    def mark(self, key, by=1):
        self.n += by
        self.counts[key] = self.n
        return self.sem, by

    def at(self, key):
        return self.sem, self.counts[key] if self.known else 1


def stream_blocks(s):
    t0, t1 = STREAMS[s]
    n = min(4, t1 - t0)
    return [(s + i, t0 + i * n, n) for i in range((t1 - t0) // n)]


def build(nc, a, counts):
    with ExitStack() as ctx:
        def sb(name, shape, dt=F32):
            return ctx.enter_context(nc.sbuf_tensor(name, shape, dt))

        def scratch(name, shape):
            return nc.dram_tensor(name, shape, F32, kind="Internal").ap()

        def signal(name):
            return Signal(ctx.enter_context(nc.semaphore(name)), counts.setdefault(name, {}))

        mod_d = scratch("mod_d", (2, 6 * D))
        gate2_d = scratch("gate2_d", (NT // 2, D))
        x1_d = scratch("x1_d", (NT * P, D))
        h2_d = scratch("h2_d", ((NT + 1) * P, D))
        sc_d = scratch("sc_d", ((NT + 1) * P, HP * NKEYS))

        ident = sb("ident", [P, P])
        ones = sb("ones", [P, P])
        keep_f = sb("keep_f", [P, PAIRS, P], U32)
        twice_d = sb("twice_d", [P, HEADS, P])
        one = sb("one", [P, P])
        iota16 = sb("iota16", [P, TOPK])
        eps = sb("eps", [P, 1])
        cvec = sb("cvec", [P, KD, 2])
        csil = sb("csil", [P, KD, 2])
        modT = sb("modT", [P, 2, KD, 2])
        wup = sb("wup", [2 * RANK, 2, DK])
        bup = sb("bup", [P, 2, PAIRS])
        cw = sb("cw", [P, CM, TAPS])
        cvv = sb("cvv", [P, 3, CM])
        gnb = sb("gnb", [P, DV])
        ss = sb("ss", [P, 2, NT])
        rs = sb("rs", [P, 2, NT])
        oss = sb("oss", [P, NT, HEADS])
        ors = sb("ors", [P, NT, HEADS])
        colsin = sb("colsin", [P, 4, 3, MAXL // P])
        cols = sb("cols", [P, 4, 3, MAXL // P])
        WORDS = 35 * 1024
        arena = sb("arena", [P, WORDS])
        top = [0]

        def take(words):
            top[0] += words
            assert top[0] <= WORDS, top[0]
            return arena[:, top[0] - words:top[0]]

        xb = [take(D) for _ in range(2)]
        junk = take(D)
        hreg = take(KD * MAXL)
        hT = hreg.rearrange("p (k n) -> p k n", k=KD)
        ureg = take(CM * MAXL)
        U = ureg.rearrange("p (m n) -> p m n", m=CM)
        creg = take(CM * MAXL)
        C = creg.rearrange("p (m n) -> p m n", m=CM)
        qkreg = take(4 * MAXL)
        QK = qkreg.rearrange("p (m n) -> p m n", m=4)
        vreg = take(8 * DV)
        V = vreg.rearrange("p (t n) -> p t n", n=DV)
        greg = take(8 * DV)
        SG = greg.rearrange("p (t n) -> p t n", n=DV)
        W = [take(D) for _ in range(WSLOTS)]
        QF = hreg[:, 0:2 * MAXL].rearrange("p (m n) -> p m n", m=PAIRS)
        KF = hreg[:, 2 * MAXL:4 * MAXL].rearrange("p (m n) -> p m n", m=PAIRS)
        ST = [r.rearrange("p (c d n) -> p c d n", d=PAIRS, n=2 * HV) for r in (hreg[:, 4 * MAXL:8 * MAXL], creg)]
        X1 = hreg.rearrange("p (t n) -> p t n", n=D)
        TMP = creg.rearrange("p (b n) -> p b n", b=4)
        gate1b, a2b, shift2b = (qkreg[:, i * D:(i + 1) * D] for i in range(3))
        afT = junk
        sgt = [junk[:, 0:512], junk[:, 512:1024]]
        rsb = xb[0][:, 0:512]
        kT = [xb[0][:, i * P:(i + 1) * P] for i in range(4)]
        Scur = [xb[1][:, i * P:(i + 1) * P] for i in range(4)]
        Stmp = [xb[1][:, (4 + i) * P:(5 + i) * P] for i in range(4)]
        H2T = greg.rearrange("p (k n) -> p k n", k=KD)
        qfT = [vreg[:, 0:512], vreg[:, 512:1024]]
        hb = [*xb, junk, qkreg[:, 3 * D:4 * D]]
        squares = creg[:, 3 * D:4 * D]
        HB = len(hb)
        skT = vreg[:, 2048:4096].rearrange("p (h n) -> p h n", h=HP)
        scb = [creg[:, i * 2048:(i + 1) * 2048].rearrange("p (t h n) -> p t h n", t=4, h=4) for i in range(2)]
        wmod = [hreg[:, i * 4096:(i + 1) * 4096].rearrange("p (k n) -> p k n", k=KD) for i in range(2)]
        modrow = arena[0:2, 3 * D + 8 * MAXL + 8 * MAXL + 4 * MAXL:3 * D + 20 * MAXL + 6 * D]
        assert 6 * D <= 16 * DV
        bmod = arena[0:2, 3 * D + 8 * MAXL:3 * D + 8 * MAXL + 6 * D]
        grow = arena[0:2, 3 * D + 14 * MAXL:3 * D + 16 * MAXL].rearrange("p (a n) -> p a n", a=2)

        ring_e = [sb(f"ring_e{i}", [P, 2 * D])[:] for i in range(ERING)]
        h2e = [sb(f"h2e{i}", [P, D])[:] for i in range(2)]
        spots = [r[:, i:i + 2 * D] for r in (hreg, creg, greg, vreg, arena[:, WORDS - WSLOTS * D:WORDS])
                 for i in range(0, r.shape[1], 2 * D)]
        ring = spots[0:4] + ring_e + spots[4:]
        assert len(ring) == RING
        h2b = h2e
        x1b = [qkreg[:, i * D:(i + 1) * D] for i in range(2)]
        gate2b = [qkreg[:, (2 + i) * D:(3 + i) * D] for i in range(2)]
        diag = [xb[i // KD][:, (i % KD) * P:(i % KD + 1) * P] for i in range(RING)]
        finalb = junk
        pick_at = [(r[:, 0:2048], r[:, 2048:4096]) for r in (vreg, ureg)]
        small = sb("small", [P, 3 * RING + 4 + PH])
        dots, gel, wts = (small[:, i * RING:(i + 1) * RING] for i in range(3))
        fss, frs, gsum = (small[:, 3 * RING + i:3 * RING + j] for i, j in ((0, 2), (2, 4), (4, 4 + PH)))
        cand = [sb(f"cand{i}", [P, TOPK * TOPK])[:] for i in range(2)]
        sv, sf = (sb(n, [P, HP * TOPK])[:] for n in ("sv", "sf"))
        si = sb("si", [P, HP * TOPK], U32)[:]
        ts, ge = (sb(n, [P, SLOTS])[:] for n in ("ts", "ge"))
        pos = sb("pos", [P, SLOTS], U32)[:]
        pab = [sb(f"pab{i}", [P, SLOTS], U32)[:] for i in range(2)]
        pf = [sb(f"pf{i}", [P, SLOTS])[:] for i in range(2)]
        pi = [sb(f"pi{i}", [P, SLOTS])[:] for i in range(2)]
        gate = [sb(f"gate{i}", [P, SLOTS])[:] for i in range(2)]
        idx = [sb(f"idx{i}", [P, SLOTS], U32) for i in range(2)]
        diag_e = [sb(f"diag_e{i}", [P, P])[:] for i in range(ERING)]
        dots_e, gel_e, wts_e = (sb(n, [P, ERING])[:] for n in ("dots_e", "gel_e", "wts_e"))

        banks = [ctx.enter_context(nc.psum_tensor(f"bank{i}", [P, 512], F32)) for i in range(4)]
        wide = [ctx.enter_context(nc.psum_tensor(f"wide{i}", [P, 2 * 512], F32)) for i in range(2)]

        S = {n: signal(n) for n in (
            "consts", "small_in", "cs_ready", "wmod_in0", "wmod_in1", "mod_rows", "mod_cols", "mod_out",
            "modT_ready", "x_in0", "x_in1", "sumsq", "std_ready", "rstd", "xn_ready", "bank_full", "bank_act",
            "bank_dve", "tap_done", "squared", "ln_rstd", "ln_scaled", "conv_act", "az", "softplus", "g_ready",
            "scan", "span", "cols_in", "exps", "cols_ready", "qk_scaled", "st_zero", "st_tmp", "st_kept", "st_next",
            "state_in", "state_out", "scT", "osum", "ostd", "orstd", "og", "sg_ready", "x1_in", "x1_ready", "sumsq2",
            "std2", "rstd2", "h2_pre", "h2_ready", "h2_out0", "h2_out1", "h2_out2", "h2_out3", "own_scores",
            "h2_in0", "h2_in1", "sc_out0", "sc_out1", "bc_in", "sk_in", "front_done", "scr_in", "scr1_in",
            "final_in", "tile_in0", "tile_in1", "h2e_in", "dot_e", "gelu_e", "weight_e", "diag_e", "used_e",
            "used_v", "y_std_done", "pick", "gexp_in", "gexp", "idx_ready", "slot_ok", "dot", "gelu", "weight",
            "diag_ready", "slot_used", "y_pre", "y_sum", "y_std", "y_ready", "y_out0", "y_out1", "x_pace", "sp_pace",
            "act_pace")}
        w_in = [signal(f"w_in{i}") for i in range(WSLOTS)]
        landed_e = [signal(f"landed_e{i}") for i in range(ERING)]
        landed = [ctx.enter_context(nc.semaphore(f"landed{i}")) for i in range(RING)]

        def chunks(s):
            for m in range(CM):
                yield ("cb", m)
                yield ("ca", m)
            for m in range(4):
                yield ("qk", m)
            yield ("af", 0)
            for name in ("v", "g"):
                for c in range(4):
                    yield (name, c)
            for c in range(2):
                yield ("pw2", c)
            for half in range(2):
                for c in range(4):
                    yield ("out", 4 * half + c)
            for b, _, _ in stream_blocks(s):
                for hp in range(HP):
                    yield ("wq", (b, hp))

        order = [(s, *c) for s in range(2) for c in chunks(s)]
        at_slot = {c: (n % WSLOTS, n) for n, c in enumerate(order)}

        def last_unit(s, name, part):
            b, _, _ = stream_blocks(s)[-1]
            t = STREAMS[s][1] - 1
            return {"cb": ("cb", part, b), "ca": ("ca", part, b), "qk": ("qk", part, b), "af": ("af", b),
                    "v": ("v", t), "g": ("g", t), "pw2": ("pw2", CM - 1, b),
                    "out": ("out", part // 4 if name == "out" else 0, t),
                    "wq": ("qf", *part) if name == "wq" else None}[name]

        def chunk_source(name, part):
            if name in ("cb", "ca", "qk"):
                m = {"qk": 0, "ca": 4, "cb": 8}[name] + part
                return a["w_cols"][m], D
            if name == "af":
                return a["w_af"], KD * 2 * RANK
            if name in ("v", "g"):
                return a["w_vg"][4 * (name == "g") + part], D
            if name == "pw2":
                return a["w_pw2"][part], D
            if name == "out":
                return a["w_out"][part], D
            return a["w_q"][part[1]], D

        def weights_ready(pe, s, name, part):
            slot, _ = at_slot[(s, name, part)]
            pe.wait_ge(*w_in[slot].at((s, name, part)))
            return W[slot]

        BY_DVE = {"xT1", "hT1", "ca", "ln1", "scf", "out", "sc", "mod"}

        def emptied(key):
            if key[0] == "st":
                return S["st_next"].at(key[1:])
            if key[0] == "o":
                return S["og"].at(key[1])
            return S["bank_dve" if key[0] in BY_DVE else "bank_act"].at(key)

        def sct(c):
            return junk[:, (c % 2) * 512:(c % 2 + 1) * 512]

        def by_head(r, odd):
            return r.rearrange("p (a o n) -> p a o n", o=2, n=P)[:, :, odd, :]

        hooks, by_vector, at_hook = {}, [], 0
        for phase, n, vector in (("conv", 16, (False, True)), ("qk", 9, (False,)), ("vg", 16, (False, True)),
                                 ("ln", 8, (False,)), ("gates", 8, (False,)), ("states", 14, (False,)),
                                 ("attn", 10, (False,)), ("out", 16, (True,)), ("qf0", 16, (True,)), ("qf1", 16, (True,))):
            hooks[phase] = at_hook
            by_vector += (vector * n)[:n]
            at_hook += n
        assert at_hook > EARLY

        def vector_sums(k):
            return k % SLOTS >= EC and by_vector[k // EC]

        def used_e(k):
            return S["used_v" if vector_sums(k) else "used_e"].at(k)

        def hook(s, phase, n):
            return hooks[phase] + n if s == 1 and hooks[phase] + n <= EARLY else -1

        def unit_banks():
            keys = counts["bank_full"]
            return {k: banks[(v - 1) % 4] for k, v in keys.items()}

        def former(d, pair):
            n = PAIRS * d + pair - 1
            return n // PAIRS, n % PAIRS

        block = ctx.enter_context(nc.Block())

        def store_scores(sp, b, tb, n, quad):
            sp.wait_ge(*S["bank_dve"].at(("sc", b, 4 * quad + 3)))
            for j in range(n):
                if tb + j == 2:
                    continue
                row = (tb + j or NT) * P
                out = sc_d[row:row + P, quad * 512:(quad + 1) * 512]
                src = scb[quad % 2][:, j, :, :].rearrange("p h n -> p (h n)")
                sp.dma_start(out, src).then_inc(*S[f"sc_out{quad % 2}"].mark((b, quad), 16))

        @block.sync
        def _(sp):
            sp.dma_start(cvec[:], a["c2"]).then_inc(*S["small_in"].mark("c", 16))
            sp.wait_ge(*S["small_in"].at("c"))
            for i in range(2):
                sp.dma_start(bmod[i:i + 1, :], a["b_mod"]).then_inc(*S["small_in"].mark(("b", i), 16))
                sp.dma_start(grow[i:i + 1, 0, :], a["norm1_g"]).then_inc(*S["small_in"].mark(("g1", i), 16))
                sp.dma_start(grow[i:i + 1, 1, :], a["norm2_g"]).then_inc(*S["small_in"].mark(("g2", i), 16))
            for dst, name in ((wup[:], "w_up"), (bup[:], "b_up"), (cw[:], "conv_w"), (cvv[:], "conv_v"),
                              (gnb[:], "gla_g")):
                src = a[name].partition_broadcast(P) if name == "gla_g" else a[name]
                sp.dma_start(dst, src).then_inc(*S["small_in"].mark("all", 16))
            for n in range(12):
                if n >= 2:
                    sp.wait_ge(*S["bank_full"].at(("mod", n - 2)))
                sp.dma_start(wmod[n % 2], a["w_mod"][n]).then_inc(*S[f"wmod_in{n % 2}"].mark(n, 16))
            sp.wait_ge(*S["mod_rows"].at("a2"))
            sp.dma_start(mod_d, modrow).then_inc(*S["mod_out"].mark("rows", 16))
            sp.wait_ge(*S["mod_out"].at("rows"))
            sp.dma_start(gate2_d[0:1, :], mod_d[0:1, 5 * D:6 * D]).then_inc(*S["mod_out"].mark("gate2", 16))
            sp.dma_start(gate2_d[1:NT // 2, :], mod_d[1, 5 * D:6 * D].partition_broadcast(NT // 2 - 1)
                         ).then_inc(*S["mod_out"].mark("gate2", 16))

            def load_result_rows(p, row, pair):
                sp.dma_start(x1b[p], x1_d[bass.ds(row, P), :]).then_inc(S[f"tile_in{p}"].sem, 16)
                sp.dma_start(gate2b[p], gate2_d[bass.ds(pair, 1), :].rearrange("a n -> (a n)").partition_broadcast(P)
                             ).then_inc(S[f"tile_in{p}"].sem, 16)

            for s, (t0, t1) in enumerate(STREAMS):
                queue = [c for c in order if c[0] == s]

                def load_weights(upto):
                    while queue:
                        c = queue.pop(0)
                        slot, n = at_slot[c]
                        if n >= WSLOTS:
                            sp.wait_ge(*S["bank_full"].at(last_unit(*order[n - WSLOTS])))
                        src, words = chunk_source(*c[1:])
                        sp.dma_start(W[slot][:, 0:words], src).then_inc(*w_in[slot].mark(c, 16))
                        if c[1:] == upto:
                            return

                if s == 0:
                    sp.wait_ge(*S["modT_ready"].at(0))
                for t in range(t0, t1):
                    if t >= 2:
                        sp.wait_ge(*S["bank_full"].at(("xT1" if t >= t0 + 2 else "hT1", t - 2)))
                        if t < t0 + 2:
                            sp.wait_ge(*S[f"h2_out{t % 2}"].at(t - 2))
                    sp.dma_start(xb[t % 2], a["x"][t * P:(t + 1) * P, :]).then_inc(*S[f"x_in{t % 2}"].mark(t, 16))
                    if t == t0 + 1:
                        load_weights(("cb", 1))
                load_weights(("pw2", 1))
                if s == 1:
                    sp.wait_ge(*S["bank_full"].at(("xT1", t1 - 1)))
                    for d, name in enumerate(("state_f", "state_b")):
                        for pair in range(PAIRS):
                            sp.dma_start(Scur[2 * d + pair], a[name][pair * P:(pair + 1) * P, :]
                                         ).then_inc(*S["state_in"].mark(s, 16))
                load_weights(("out", 0))
                if s == 0:
                    for d, name in enumerate(("new_f", "new_b")):
                        for pair in range(PAIRS):
                            sp.wait_ge(*S["st_next"].at((s, t1 - t0 - 1, 2 * d + pair)))
                            sp.dma_start(a[name][pair * P:(pair + 1) * P, :], Scur[2 * d + pair]
                                         ).then_inc(*S["state_out"].mark(s, 16))
                load_weights(("out", 3))
                for t in range(t0, t1):
                    sp.wait_ge(*S["bank_full"].at(("o", t1 - 1)))
                    sp.dma_start(X1[:, t - t0, :], a["x"][t * P:(t + 1) * P, :]).then_inc(*S["x1_in"].mark(s, 16))
                for dst, row in ((gate1b, 2), (shift2b, 3), (a2b, 4)):
                    sp.dma_start(dst, mod_d[s, row * D:(row + 1) * D].partition_broadcast(P)
                                 ).then_inc(*S["bc_in"].mark(s, 16))
                load_weights(("out", 7))
                sp.wait_ge(*S["bank_full"].at(("out", 1, t1 - 1)))
                sp.dma_start(skT, a["sk"]).then_inc(*S["sk_in"].mark(s, 16))
                for b, tb, n in stream_blocks(s):
                    load_weights(("wq", (b, WSLOTS - 1)))
                    for t in range(tb, tb + n):
                        sp.wait_ge(*S["x1_ready"].at((1, t)))
                        sp.dma_start(x1_d[t * P:(t + 1) * P, :], X1[:, t - t0, :]).then_inc(*S["front_done"].mark("x1", 16))
                        sp.wait_ge(*S["h2_ready"].at(t))
                        for row in ((0, NT * P) if t == 0 else (t * P,)):
                            sp.dma_start(h2_d[row:row + P, :], hb[t % HB]).then_inc(*S[f"h2_out{t % HB}"].mark(t, 16))
                    if b == 2:
                        sp.wait_ge(*S["front_done"].at("x1"))
                        sp.wait_ge(*S["mod_out"].at("gate2"))
                        sp.wait_ge(*S["bank_full"].at(("hT1", NT - 3)))
                        sp.wait_ge(*S["h2_out2"].at(NT - 4))
                        sp.wait_ge(*S["h2_out3"].at(NT - 3))
                        sp.wait_ge(*S["dot_e"].at(SLOTS - 1))
                        sp.dma_start(h2b[0], h2_d[2 * P:3 * P, :]).then_inc(*S["h2_in0"].mark(2, 16))
                        sp.dma_start(finalb, a["final_g"].partition_broadcast(P)).then_inc(*S["final_in"].mark(0, 16))
                        for t in range(2):
                            load_result_rows(t, t * P, 0)
                            S[f"tile_in{t}"].mark(t, 32)
                    for hp in range(HP):
                        if hp >= WSLOTS:
                            load_weights(("wq", (b, hp)))
                        if hp >= 4 and hp % 4 == 1:
                            store_scores(sp, b, tb, n, hp // 4 - 1)
                    store_scores(sp, b, tb, n, 3)

            for i in range(HB):
                sp.wait_ge(*S[f"h2_out{(NT - 1 - i) % HB}"].at(NT - 1 - i))
            for i in range(2):
                sp.wait_ge(*S[f"sc_out{i}"].at((2, i + 2)))
            with sp.Fori(0, NT // 2 - 1) as i:
                for p in range(2):
                    row = i * (2 * P) + (p + 2) * P
                    sp.wait_ge(S["dot"].sem, i * (2 * SLOTS) + (p + 1) * SLOTS)
                    sp.sem_inc(S["sp_pace"].sem)
                    sp.dma_start(h2b[1 - p], h2_d[bass.ds(row + P, P), :]).then_inc(S[f"h2_in{1 - p}"].sem, 16)
                    sp.wait_ge(S[f"y_out{p}"].sem, i * 16 + 16)
                    sp.sem_inc(S["sp_pace"].sem)
                    load_result_rows(p, row, i + 1)
                    sp.wait_ge(S["idx_ready"].sem, i * 2 + p + 3)
                    sp.sem_inc(S["sp_pace"].sem)
                    sp.dma_start(pick_at[1][0], sc_d[bass.ds(row + P, P), :]).then_inc(S["scr_in"].sem, 16)
            for p in range(2):
                sp.wait_ge(S[f"y_out{p}"].sem, 16 * NT // 2)
            sp.wait_ge(S["h2_in0"].sem, 16 * NT // 2)
            sp.wait_ge(*S["state_out"].at(0))

        @block.gpsimd
        def _(pool):
            consts = S["consts"]
            pool.memset(ident[:], 0.0).then_inc(*consts.mark("z"))
            pool.memset(twice_d[:], 1.0).then_inc(*consts.mark("z"))
            pool.memset(keep_f[:], 1).then_inc(*consts.mark("z"))
            pool.memset(one[:], 1.0).then_inc(*consts.mark("z"))
            pool.memset(ones[:], 1.0 / CH).then_inc(*consts.mark("z"))
            pool.memset(eps[:], EPS).then_inc(*consts.mark("z"))
            pool.iota(iota16[:], [[1, TOPK]], base=0, channel_multiplier=0,
                      allow_small_or_imprecise_dtypes=True).then_inc(*consts.mark("z"))
            pool.wait_ge(*consts.at("z"))
            pool.affine_select(out=ident[:], in_=ident[:], compare_op=ALU.not_equal, fill=1.0, base=0,
                               pattern=[[-1, P]], channel_multiplier=1).then_inc(*consts.mark("all"))
            pool.affine_select(out=twice_d[:], in_=twice_d[:], compare_op=ALU.not_equal, fill=2.0, base=0,
                               pattern=[[0, HEADS], [-1, P]], channel_multiplier=1).then_inc(*consts.mark("all"))
            kf = keep_f[:].bitcast(mybir.dt.int32)
            pool.affine_select(out=kf, in_=kf, compare_op=ALU.is_ge, fill=0, base=0,
                               pattern=[[0, PAIRS], [1, P]], channel_multiplier=-1).then_inc(*consts.mark("all"))

            pool.wait_ge(*S["h2_out0"].at(0))
            pool.wait_ge(*S["h2_out1"].at(1))
            for t in range(2):
                pool.dma_start(h2e[t], h2_d[t * P:(t + 1) * P, :]).then_inc(*S["h2e_in"].mark(0, 16))
            pool.wait_ge(S["idx_ready"].sem, 1)
            for k in range(2 * SLOTS):
                if k == SLOTS:
                    pool.wait_ge(S["idx_ready"].sem, 2)
                if k >= ERING:
                    pool.wait_ge(*used_e(k - ERING))
                pool.indirect_dma_start(
                    out=ring_e[k % ERING], out_offset=None, in_=a["uv"],
                    in_offset=bass.IndirectOffsetOnAxis(ap=idx[k // SLOTS][:, k % SLOTS:k % SLOTS + 1], axis=0)
                ).then_inc(*landed_e[k % ERING].mark(k, 16))
                if k == 1:
                    pool.dma_start(pick_at[0][0], sc_d[P:2 * P, :]).then_inc(*S["scr1_in"].mark(1, 16))

            with pool.Fori(0, NT // 2 - 1) as i:
                for p in range(2):
                    pool.wait_ge(S["idx_ready"].sem, i * 2 + p + 3)
                    pool.sem_inc(S["slot_ok"].sem)
                    for k in range(SLOTS):
                        pool.wait_ge(S["slot_used"].sem, i * (2 * SLOTS) + p * SLOTS + k + 1)
                        pool.sem_inc(S["slot_ok"].sem)
                        pool.indirect_dma_start(
                            out=ring[k % RING], out_offset=None, in_=a["uv"],
                            in_offset=bass.IndirectOffsetOnAxis(ap=idx[p][:, k:k + 1], axis=0)
                        ).then_inc(landed[k % RING], 16)

        @block.tensor
        def _(pe):
            units = []

            def bank(key):
                n = len(units)
                if n >= 4:
                    pe.wait_ge(*emptied(units[n - 4]))
                units.append(key)
                return banks[n % 4]

            def full(ins, key):
                ins.then_inc(*S["bank_full"].mark(key))

            def turn_tile(name, t, src):
                for half in range(2):
                    bk = bank((f"{name}{half}", t))
                    for k in range(4):
                        c0 = half * 512 + k * P
                        ins = pe.transpose(bk[:, k * P:(k + 1) * P], src[:, c0:c0 + P], ident[:])
                    full(ins, (f"{name}{half}", t))

            def early(s, phase, n):
                c = hook(s, phase, n) - 1
                if not 0 <= c < EARLY:
                    return
                for k in range(EC * c, EC * c + EC):
                    if vector_sums(k):
                        continue
                    if k % SLOTS and vector_sums(k - 1):
                        pe.wait_ge(*used_e(k - 1))
                    pe.wait_ge(*S["diag_e"].at(k))
                    for h in range(2):
                        ins = pe.matmul(wide[k // SLOTS][:, h * 512:(h + 1) * 512], lhsT=diag_e[k % ERING],
                                        rhs=ring_e[k % ERING][:, D + h * 512:D + (h + 1) * 512],
                                        start=(k % SLOTS == 0), stop=(k % SLOTS == SLOTS - 1), skip_group_check=True)
                    ins.then_inc(*S["used_e"].mark(k))

            pe.wait_ge(*S["consts"].at("all"))
            pe.wait_ge(*S["cs_ready"].at(0))
            for n in range(12):
                bk = bank(("mod", n))
                pe.wait_ge(*S[f"wmod_in{n % 2}"].at(n))
                for k in range(KD):
                    ins = pe.matmul(bk[0:2, :], lhsT=csil[:, k, :], rhs=wmod[n % 2][:, k, :],
                                    start=(k == 0), stop=(k == KD - 1))
                full(ins, ("mod", n))
            pe.wait_ge(*S["mod_rows"].at("a2"))
            for which in range(2):
                for k in range(KD):
                    ins = pe.transpose(wide[0][:, (which * KD + k) * 2:(which * KD + k) * 2 + 2],
                                       modrow[:, which * D + k * P:which * D + (k + 1) * P], ident[0:2, 0:2])
            ins.then_inc(*S["mod_cols"].mark(0))
            pe.wait_ge(*S["modT_ready"].at(0))

            for s, (t0, t1) in enumerate(STREAMS):
                blocks = stream_blocks(s)
                for t in range(t0, t1):
                    pe.wait_ge(*S["xn_ready"].at(t))
                    turn_tile("xT", t, xb[t % 2])
                pe.wait_ge(*S["bank_act"].at(("xT0", t1 - 1)))
                pe.wait_ge(*S["bank_dve"].at(("xT1", t1 - 1)))

                def project(name, m, b, tb, n):
                    w = weights_ready(pe, s, name, m)
                    cols_ = slice((tb - t0) * P, (tb - t0 + n) * P)
                    key = (name, m, b) if name != "af" else ("af", b)
                    bk = bank(key)
                    M = P if name != "af" else 2 * RANK
                    for k in range(KD):
                        ins = pe.matmul(bk[0:M, 0:n * P], lhsT=w[:, k * M:(k + 1) * M], rhs=hT[:, k, cols_],
                                        start=(k == 0), stop=(k == KD - 1))
                    full(ins, key)

                for m in range(CM):
                    for j, blk in enumerate(blocks):
                        project("cb", m, *blk)
                        early(s, "conv", 4 * m + 2 * j)
                        project("ca", m, *blk)
                        early(s, "conv", 4 * m + 2 * j + 1)
                for m in range(4):
                    for j, blk in enumerate(blocks):
                        project("qk", m, *blk)
                        early(s, "qk", 2 * m + j)
                for blk in blocks:
                    project("af", 0, *blk)
                early(s, "qk", 8)
                for name in ("v", "g"):
                    for t in range(t0, t1):
                        bk = bank((name, t))
                        for k in range(KD):
                            w = weights_ready(pe, s, name, k // 2)
                            ins = pe.matmul(bk[:], lhsT=hT[:, k, (t - t0) * P:(t - t0 + 1) * P],
                                            rhs=w[:, (k % 2) * 512:(k % 2 + 1) * 512], start=(k == 0), stop=(k == KD - 1))
                        full(ins, (name, t))
                        early(s, "vg", t - t0 + 8 * (name == "g"))
                for j, (b, tb, n) in enumerate(blocks):
                    cols_ = slice((tb - t0) * P, (tb - t0 + n) * P)
                    if b == blocks[0][0]:
                        for m in range(CM):
                            pe.wait_ge(*S["tap_done"].at((s, m, TAPS - 1)))
                    bk = bank(("ln1", b))
                    for m in range(CM):
                        ins = pe.matmul(bk[:, 0:n * P], lhsT=ones[:], rhs=C[:, m, cols_], start=(m == 0), stop=(m == CM - 1))
                    full(ins, ("ln1", b))
                    early(s, "ln", 4 * j)
                    pe.wait_ge(*S["squared"].at(b))
                    bk = bank(("ln2", b))
                    for m in range(CM):
                        ins = pe.matmul(bk[:, 0:n * P], lhsT=ones[:], rhs=U[:, m, cols_], start=(m == 0), stop=(m == CM - 1))
                    full(ins, ("ln2", b))
                    early(s, "ln", 4 * j + 1)
                    pe.wait_ge(*S["conv_act"].at(b))
                    for m in range(CM):
                        bk = bank(("pw2", m, b))
                        for k in range(CM):
                            w = weights_ready(pe, s, "pw2", k // 2)
                            c0 = (k % 2) * 512 + m * P
                            ins = pe.matmul(bk[:, 0:n * P], lhsT=w[:, c0:c0 + P], rhs=C[:, k, cols_],
                                            start=(k == 0), stop=(k == CM - 1))
                        full(ins, ("pw2", m, b))
                        if m % 2:
                            early(s, "ln", 4 * j + 2 + m // 2)
                pe.wait_ge(*S["bank_act"].at(("af", blocks[-1][0])))
                for d in range(2):
                    for pair in range(PAIRS):
                        for b, tb, n in blocks:
                            bk = bank(("gz", d, pair, b))
                            ins = pe.matmul(bk[:, 0:n * P], lhsT=wup[:, d, pair * P:(pair + 1) * P],
                                            rhs=afT[0:2 * RANK, (tb - t0) * P:(tb - t0 + n) * P], start=True, stop=True)
                            full(ins, ("gz", d, pair, b))
                        for j in range(2):
                            early(s, "gates", 4 * d + 2 * pair + j)
                pe.wait_ge(*S["qk_scaled"].at((s, 1, PAIRS - 1, 1)))
                steps = t1 - t0
                last = steps if s == 0 else steps - 1
                for i in range(last):
                    for dp in range(4):
                        d, pair = dp // 2, dp % 2
                        c = i if d == 0 else steps - 1 - i
                        K_ = KF[:, pair, :] if d == 0 else QK[:, 2 + pair, :]
                        bk = bank(("kt", s, i, dp))
                        full(pe.transpose(bk[:, 0:P], K_[:, c * P:(c + 1) * P], ident[:]), ("kt", s, i, dp))
                    early(s, "states", 2 * i)
                    for dp in range(4):
                        d, pair = dp // 2, dp % 2
                        c = i if d == 0 else steps - 1 - i
                        pe.wait_ge(*S["bank_act"].at(("kt", s, i, dp)))
                        bk = bank(("st", s, i, dp))
                        full(pe.matmul(bk[:, 0:2 * HV], lhsT=kT[dp], rhs=V[:, c, pair * 2 * HV:(pair + 1) * 2 * HV],
                                       start=True, stop=True), ("st", s, i, dp))
                    early(s, "states", 2 * i + 1)
                pe.wait_ge(*S["st_kept"].at((s, steps - 1, 3)))

                def out_chunk(c):
                    t = t0 + c
                    pe.wait_ge(*S["scT"].at(t))
                    bk = bank(("o", t))
                    cc = slice(c * P, (c + 1) * P)
                    for h in range(HEADS):
                        pe.matmul(bk[:, h * HV:(h + 1) * HV], lhsT=sct(c)[:, h * P:(h + 1) * P],
                                  rhs=V[:, c, h * HV:(h + 1) * HV], start=(h == 0), stop=False, skip_group_check=True)
                    for pair in range(PAIRS):
                        o = bk[:, pair * 2 * HV:(pair + 1) * 2 * HV]
                        pe.matmul(o, lhsT=QF[:, pair, cc], rhs=ST[0][:, c, pair, :], start=False, stop=False,
                                  skip_group_check=True)
                        ins = pe.matmul(o, lhsT=QK[:, pair, cc], rhs=ST[1][:, c, pair, :], start=False, stop=True,
                                        skip_group_check=True)
                    full(ins, ("o", t))

                def turn_chunk(c):
                    t = t0 + c
                    pe.wait_ge(*S["og"].at(t))
                    bk = bank(("ot", t))
                    for h in range(HEADS):
                        ins = pe.transpose(bk[:, h * P:(h + 1) * P], SG[:, c, h * P:(h + 1) * P], ident[:])
                    full(ins, ("ot", t))

                for c in range(steps + 2):
                    if c < steps:
                        cc = slice(c * P, (c + 1) * P)
                        for name, k_, q_, o_ in (("scb", QK, QK, 2), ("scf", KF, QF, 0)):
                            for odd in range(2):
                                bk = bank((name, odd, t0 + c))
                                rows = slice(odd * HK, (odd + 1) * HK)
                                for pair in range(PAIRS):
                                    ins = pe.matmul(bk[:, pair * P:(pair + 1) * P], lhsT=k_[rows, o_ + pair, cc],
                                                    rhs=q_[rows, pair, cc], start=True, stop=True)
                                full(ins, (name, odd, t0 + c))
                    if 1 <= c <= steps:
                        out_chunk(c - 1)
                    if c >= 2:
                        turn_chunk(c - 2)
                    early(s, "attn", c)
                pe.wait_ge(*S["bank_act"].at(("ot", t1 - 1)))
                for half in range(2):
                    for t in range(t0, t1):
                        bk = bank(("out", half, t))
                        c = t - t0
                        for k in range(KD):
                            w = weights_ready(pe, s, "out", 4 * half + k // 2)
                            l = V[:, c, k * P:(k + 1) * P] if k < 4 else U[:, k - 4, c * P:(c + 1) * P]
                            ins = pe.matmul(bk[:], lhsT=l, rhs=w[:, (k % 2) * 512:(k % 2 + 1) * 512],
                                            start=(k == 0), stop=(k == KD - 1))
                        full(ins, ("out", half, t))
                        early(s, "out", 8 * half + c)
                for j, (b, tb, n) in enumerate(blocks):
                    for t in range(tb, tb + n):
                        pe.wait_ge(*S["h2_ready"].at(t))
                        turn_tile("hT", t, hb[t % HB])
                    pe.wait_ge(*S["bank_act"].at(("hT0", tb + n - 1)))
                    pe.wait_ge(*S["bank_dve"].at(("hT1", tb + n - 1)))
                    pe.wait_ge(*S["sk_in"].at(s))
                    for hp in range(HP + 1):
                        if hp < HP:
                            w = weights_ready(pe, s, "wq", (b, hp))
                            bk = bank(("qf", b, hp))
                            for k in range(KD):
                                ins = pe.matmul(bk[:, 0:n * P], lhsT=w[:, k * P:(k + 1) * P], rhs=H2T[:, k, 0:n * P],
                                                start=(k == 0), stop=(k == KD - 1))
                            full(ins, ("qf", b, hp))
                        if hp:
                            pe.wait_ge(*S["bank_act"].at(("qf", b, hp - 1)))
                            bk = bank(("sc", b, hp - 1))
                            for q in range(n):
                                ins = pe.matmul(bk[:, q * P:(q + 1) * P], lhsT=qfT[(hp - 1) % 2][:, q * P:(q + 1) * P],
                                                rhs=skT[:, hp - 1, :], start=True, stop=True)
                            full(ins, ("sc", b, hp - 1))
                        if hp < HP:
                            early(s, f"qf{j}", hp)
                        if b == 2 and hp == HP // 2:
                            pe.wait_ge(*S["front_done"].at("x1"))
                            pe.sem_inc(S["slot_used"].sem, RING // 4)
            pe.wait_ge(*used_e(2 * SLOTS - 1))
            pe.sem_inc(S["slot_used"].sem, RING // 4)

            def add_rows(i, p, g, first):
                for r in range(RING):
                    pe.wait_ge(S["diag_ready"].sem, i * (2 * SLOTS) + p * SLOTS + g * RING + r + 1)
                    for c in range(2):
                        ins = pe.matmul(wide[p][:, c * 512:(c + 1) * 512], lhsT=diag[r],
                                        rhs=ring[r][:, D + c * 512:D + (c + 1) * 512],
                                        start=(first and r == 0), stop=(r == RING - 1), skip_group_check=True)
                    ins.then_inc(S["slot_used"].sem, 1)

            pe.wait_ge(*S["bank_full"].at(("sc", 2, HP - 1)))
            pe.wait_ge(*S["bank_dve"].at(("sc", 2, HP - 1)))
            for i in range(2):
                pe.wait_ge(*S[f"sc_out{i}"].at((2, i + 2)))
            pe.sem_inc(S["slot_used"].sem, RING // 2)
            with pe.Fori(0, NT // 2 - 1) as i:
                for p in range(2):
                    pe.wait_ge(S["y_ready"].sem, i * 2 + p + 1)
                    add_rows(i, p, 0, True)
                    with pe.Fori(1, SLOTS // RING) as g:
                        add_rows(i, p, g, False)

        @block.scalar
        def _(act):
            def drained(ins, key):
                ins.then_inc(*S["bank_act"].mark(key))

            bank_of = unit_banks()

            def wait_full(key):
                act.wait_ge(*S["bank_full"].at(key))
                return bank_of[key]

            act.wait_ge(*S["small_in"].at("c"))
            act.activation(csil[:], cvec[:], ACT.Silu).then_inc(*S["cs_ready"].mark(0))
            act.wait_ge(*S["consts"].at("all"))

            def pick_exp(tile):
                act.wait_ge(S["gexp_in"].sem, tile + 1)
                act.activation(ge, ge, ACT.Exp).then_inc(S["gexp"].sem, 1)

            def early(s, phase, n):
                c = hook(s, phase, n)
                if not 0 <= c < EARLY:
                    return
                k0 = EC * c
                r0 = k0 % ERING
                t_, g0 = k0 // SLOTS, k0 % SLOTS
                act.wait_ge(*S["dot_e"].at(k0 + EC - 1))
                act.activation(gel_e[:, r0:r0 + EC], dots_e[:, r0:r0 + EC], ACT.Gelu).then_inc(*S["gelu_e"].mark(c))
                act.wait_ge(*S["gelu_e"].at(c))
                for j in range(EC):
                    act.activation(wts_e[:, r0 + j:r0 + j + 1], gel_e[:, r0 + j:r0 + j + 1], ACT.Copy,
                                   scale=gate[t_][:, g0 + j:g0 + j + 1]).then_inc(*S["weight_e"].mark(k0 + j))
                for j in range(0 if vector_sums(k0) else EC):
                    act.wait_ge(*S["weight_e"].at(k0 + j))
                    if k0 + j >= ERING:
                        act.wait_ge(*used_e(k0 + j - ERING))
                    act.activation(diag_e[r0 + j], ident[:], ACT.Copy, scale=wts_e[:, r0 + j:r0 + j + 1]
                                   ).then_inc(*S["diag_e"].mark(k0 + j))
                if HP + PH in share(c, 0, SPAN_1):
                    pick_exp(1)

            def mean_square(src, sqname, t, col, stdname):
                act.activation(junk, src, ACT.Square, accum_out=ss[:, col, t:t + 1]).then_inc(*S[sqname].mark(t))
                act.wait_ge(*S[sqname].at(t))
                act.activation(rs[:, col, t:t + 1], ss[:, col, t:t + 1], ACT.Sqrt, bias=eps[:], scale=1.0 / D
                               ).then_inc(*S[stdname].mark(t))

            for s, (t0, t1) in enumerate(STREAMS):
                blocks = stream_blocks(s)
                if s == 0:
                    act.wait_ge(*S["modT_ready"].at(0))
                for t in range(t0, t1 + 1):
                    if t < t1:
                        act.wait_ge(*S[f"x_in{t % 2}"].at(t))
                        mean_square(xb[t % 2], "sumsq", t, 0, "std_ready")
                    if t > t0:
                        u = t - 1
                        bk = wait_full(("xT0", u))
                        for k in range(KD // 2):
                            ins = act.activation(hT[:, k, (u - t0) * P:(u - t0 + 1) * P], bk[:, k * P:(k + 1) * P],
                                                 ACT.Identity, bias=modT[:, 0, k, s:s + 1], scale=modT[:, 1, k, s:s + 1])
                        drained(ins, ("xT0", u))
                if s == 1:
                    pick_exp(0)
                n_, before = 0, []
                for m in range(CM):
                    for b, tb, n in blocks:
                        bk = wait_full(("cb", m, b))
                        if n_ >= 2:
                            act.wait_ge(*S["bank_dve"].at(before[n_ - 2]))
                        before.append(("ca", m, b))
                        drained(act.activation(sgt[n_ % 2][:, 0:n * P], bk[:, 0:n * P], ACT.Sigmoid), ("cb", m, b))
                        early(s, "conv", 2 * n_)
                        early(s, "conv", 2 * n_ + 1)
                        n_ += 1
                for m in range(4):
                    for j, (b, tb, n) in enumerate(blocks):
                        bk = wait_full(("qk", m, b))
                        drained(act.activation(QK[:, m, (tb - t0) * P:(tb - t0 + n) * P], bk[:, 0:n * P], ACT.Copy,
                                               scale=HK ** -0.5 if m < 2 else 1.0), ("qk", m, b))
                        early(s, "qk", 2 * m + j)
                for b, tb, n in blocks:
                    bk = wait_full(("af", b))
                    drained(act.activation(afT[0:2 * RANK, (tb - t0) * P:(tb - t0 + n) * P], bk[0:2 * RANK, 0:n * P],
                                           ACT.Copy), ("af", b))
                early(s, "qk", 8)
                for t in range(t0, t1):
                    bk = wait_full(("v", t))
                    drained(act.activation(V[:, t - t0, :], bk[:], ACT.Copy), ("v", t))
                    early(s, "vg", t - t0)
                for t in range(t0, t1):
                    bk = wait_full(("g", t))
                    drained(act.activation(SG[:, t - t0, :], bk[:], ACT.Silu), ("g", t))
                    early(s, "vg", 8 + t - t0)
                for j, (b, tb, n) in enumerate(blocks):
                    cols_ = slice((tb - t0) * P, (tb - t0 + n) * P)
                    act.wait_ge(*S["bank_dve"].at(("ln1", b)))
                    for m in range(CM):
                        ins = act.activation(U[:, m, cols_], C[:, m, cols_], ACT.Square)
                    ins.then_inc(*S["squared"].mark(b))
                    early(s, "ln", 4 * j)
                    bk = wait_full(("ln2", b))
                    drained(act.activation(rsb[:, 0:n * P], bk[:, 0:n * P], ACT.Sqrt, bias=eps[:]), ("ln2", b))
                    act.wait_ge(*S["ln_scaled"].at(b))
                    for m in range(CM):
                        ins = act.activation(C[:, m, cols_], C[:, m, cols_], ACT.Silu, bias=cvv[:, 2, m:m + 1],
                                             scale=cvv[:, 1, m:m + 1])
                    ins.then_inc(*S["conv_act"].mark(b))
                    early(s, "ln", 4 * j + 1)
                    for m in range(CM):
                        bk = wait_full(("pw2", m, b))
                        drained(act.activation(U[:, m, cols_], bk[:, 0:n * P], ACT.Copy), ("pw2", m, b))
                        if m % 2:
                            early(s, "ln", 4 * j + 2 + m // 2)
                for d in range(2):
                    for pair in range(PAIRS):
                        key = (s, d, pair)
                        L = (t1 - t0) * P
                        for b, tb, n in blocks:
                            cols_ = slice((tb - t0) * P, (tb - t0 + n) * P)
                            bk = wait_full(("gz", d, pair, b))
                            if (d, pair) == (0, 0):
                                act.wait_ge(*S["bank_full"].at(("pw2", CM - 1, blocks[-1][0])))
                            else:
                                act.wait_ge(*S["qk_scaled"].at((s, *former(d, pair), 1)))
                            act.activation(TMP[:, 1, cols_], bk[:, 0:n * P], ACT.Abs, bias=bup[:, d, pair:pair + 1]
                                           ).then_inc(*S["az"].mark((*key, b)))
                            drained(act.activation(TMP[:, 0, cols_], bk[:, 0:n * P], ACT.Identity,
                                                   bias=bup[:, d, pair:pair + 1]), ("gz", d, pair, b))
                        act.wait_ge(*S["az"].at((*key, blocks[-1][0])))
                        act.activation(TMP[:, 1, 0:L], TMP[:, 1, 0:L], ACT.Exp, scale=-1.0).then_inc(*S["softplus"].mark((*key, 0)))
                        act.wait_ge(*S["softplus"].at((*key, 0)))
                        act.activation(TMP[:, 1, 0:L], TMP[:, 1, 0:L], ACT.Ln, bias=1.0).then_inc(*S["softplus"].mark((*key, 1)))
                        early(s, "gates", 4 * d + 2 * pair)
                        act.wait_ge(*S["cols_in"].at(key))
                        dp = 2 * d + pair
                        act.activation(cols[:, dp, :, 0:t1 - t0], colsin[:, dp, :, 0:t1 - t0], ACT.Exp, scale=1.0 / RANK
                                       ).then_inc(*S["cols_ready"].mark(key))
                        act.activation(TMP[:, 3, 0:L], TMP[:, 2, 0:L], ACT.Exp, scale=-1.0 / RANK).then_inc(*S["exps"].mark((*key, 0)))
                        act.activation(TMP[:, 2, 0:L], TMP[:, 2, 0:L], ACT.Exp, scale=1.0 / RANK).then_inc(*S["exps"].mark((*key, 1)))
                        early(s, "gates", 4 * d + 2 * pair + 1)
                steps = t1 - t0
                last = steps if s == 0 else steps - 1
                act.wait_ge(*S["ln_scaled"].at(blocks[-1][0]))
                for i in range(last):
                    for dp in range(4):
                        bk = wait_full(("kt", s, i, dp))
                        if i:
                            act.wait_ge(*S["bank_full"].at(("st", s, i - 1, dp)))
                        drained(act.activation(kT[dp], bk[:, 0:P], ACT.Copy), ("kt", s, i, dp))
                    for j in range(2):
                        early(s, "states", 2 * i + j)
                def o_stats(c):
                    t = t0 + c
                    bk = wait_full(("o", t))
                    for h in range(HEADS):
                        if h or c:
                            act.wait_ge(*S["osum"].at((t, h - 1) if h else (t - 1, HEADS - 1)))
                        act.activation(xb[0][:, 512:640], bk[:, h * HV:(h + 1) * HV], ACT.Square,
                                       accum_out=oss[:, t, h:h + 1]).then_inc(*S["osum"].mark((t, h)))
                    act.wait_ge(*S["osum"].at((t, HEADS - 1)))
                    act.activation(ors[:, t, :], oss[:, t, :], ACT.Sqrt, bias=eps[:], scale=1.0 / HV
                                   ).then_inc(*S["ostd"].mark(t))

                def turn_out(c):
                    t = t0 + c
                    bk = wait_full(("ot", t))
                    drained(act.activation(V[:, c, :], bk[:], ACT.Copy), ("ot", t))

                for c in range(steps + 2):
                    if c < steps:
                        if c >= 2:
                            act.wait_ge(*S["bank_full"].at(("o", t0 + c - 2)))
                        for odd in range(2):
                            bk = wait_full(("scb", odd, t0 + c))
                            drained(act.activation(by_head(sct(c), odd), bk[:, 0:2 * P].rearrange("p (a n) -> p a n", n=P),
                                                   ACT.Copy), ("scb", odd, t0 + c))
                    if 1 <= c <= steps:
                        o_stats(c - 1)
                    if c >= 2:
                        turn_out(c - 2)
                    early(s, "attn", c)
                for half in range(2):
                    for t in range(t0, t1):
                        if half:
                            act.wait_ge(*S["x1_ready"].at((1, t)))
                            act.activation(squares, X1[:, t - t0, :], ACT.Square, accum_out=ss[:, 1, t:t + 1]
                                           ).then_inc(*S["sumsq2"].mark(t))
                            act.wait_ge(*S["sumsq2"].at(t))
                            for b, tb, n in blocks:
                                if t == tb + n - 1:
                                    act.activation(rs[:, 1, tb:tb + n], ss[:, 1, tb:tb + n], ACT.Sqrt, bias=eps[:],
                                                   scale=1.0 / D).then_inc(*S["std2"].mark(b))
                        early(s, "out", 8 * half + t - t0)
                def early_share(j, b, hp):
                    early(s, f"qf{j}", hp)
                    if b == 2 and HP + PH in share(hp, HP, SPAN_2):
                        pick_exp(2)

                for j, (b, tb, n) in enumerate(blocks):
                    for t in range(tb, tb + n):
                        bk = wait_full(("hT0", t))
                        if b > blocks[0][0]:
                            act.wait_ge(*S["bank_full"].at(("qf", b - 1, HP - 1)))
                        cc = slice((t - tb) * P, (t - tb + 1) * P)
                        drained(act.activation(H2T[:, 0:4, cc], bk[:].rearrange("p (k n) -> p k n", k=4), ACT.Copy),
                                ("hT0", t))
                    for hp in range(HP):
                        bk = wait_full(("qf", b, hp))
                        if hp >= 2:
                            act.wait_ge(*S["bank_full"].at(("sc", b, hp - 2)))
                        elif b > blocks[0][0]:
                            act.wait_ge(*S["bank_full"].at(("sc", b - 1, HP - 2 + hp)))
                        drained(act.activation(qfT[hp % 2][:, 0:n * P], bk[:, 0:n * P], ACT.Copy), ("qf", b, hp))
                        if hp:
                            early_share(j, b, hp - 1)
                    early_share(j, b, HP - 1)

            def unit(i, p, g, part):
                j, n = part * GROUP, g * (RING // GROUP) + part + 1
                act.wait_ge(S["dot"].sem, i * (2 * SLOTS) + (p + 1) * SLOTS + g * RING + j + GROUP)
                act.activation(gel[:, j:j + GROUP], dots[:, j:j + GROUP], ACT.Gelu).then_inc(S["gelu"].sem, 1)
                act.wait_ge(S["weight"].sem, i * (2 * SLOTS // GROUP) + p * (SLOTS // GROUP) + n)
                for r in range(j, j + GROUP):
                    act.activation(diag[r], ident[:], ACT.Copy, scale=wts[:, r:r + 1]).then_inc(S["diag_ready"].sem, 1)

            def root(p, tile):
                act.wait_ge(S["y_pre"].sem, tile * 2 + 2)
                act.activation(gate2b[p], x1b[p], ACT.Square, accum_out=fss[:, p:p + 1]).then_inc(S["y_sum"].sem, 1)
                act.wait_ge(S["y_sum"].sem, tile + 1)
                act.activation(frs[:, p:p + 1], fss[:, p:p + 1], ACT.Sqrt, bias=eps[:], scale=1.0 / D
                               ).then_inc(S["y_std"].sem, 1)

            def store(p, tile):
                act.wait_ge(S["y_ready"].sem, tile + 1)
                act.sem_inc(S["act_pace"].sem)
                act.dma_start(a["y"][bass.ds(tile * P, P), :], x1b[p]).then_inc(S[f"y_out{p}"].sem, 16)

            root(0, 0)
            store(0, 0)
            for i in range(2):
                act.wait_ge(*S[f"h2_out{i}"].at(NT - 2 + i))
            act.wait_ge(*S["bank_full"].at(("hT1", NT - 1)))
            with act.Fori(0, NT // 2 - 1) as i:
                for p in range(2):
                    tile = i * 2 + p + 2
                    for part in range(RING // GROUP):
                        unit(i, p, 0, part)
                        if part == ROOT_UNIT:
                            root(1 - p, tile - 1)
                        if part == ROOT_UNIT + 1:
                            store(1 - p, tile - 1)
                    with act.Fori(1, EXP_UNIT // (RING // GROUP)) as g:
                        for part in range(RING // GROUP):
                            unit(i, p, g, part)
                    for part in range(RING // GROUP):
                        unit(i, p, EXP_UNIT // (RING // GROUP), part)
                        if part == EXP_UNIT % (RING // GROUP):
                            pick_exp(tile + 1)
                    with act.Fori(EXP_UNIT // (RING // GROUP) + 1, SLOTS // RING) as g:
                        for part in range(RING // GROUP):
                            unit(i, p, g, part)
            root(1, NT - 1)
            store(1, NT - 1)

        @block.vector
        def _(dve):
            def drained(ins, key):
                ins.then_inc(*S["bank_dve"].mark(key))

            bank_of = unit_banks()

            def wait_full(key):
                dve.wait_ge(*S["bank_full"].at(key))
                return bank_of[key]

            dve.wait_ge(*S["consts"].at("all"))
            dve.wait_ge(*S["small_in"].at("all"))
            for n in range(12):
                bk = wait_full(("mod", n))
                drained(dve.tensor_tensor(modrow[:, n * 512:(n + 1) * 512], bk[0:2, :], bmod[:, n * 512:(n + 1) * 512],
                                          ALU.add), ("mod", n))
            dve.wait_ge(*S["bank_dve"].at(("mod", 11)))
            for name, at, g in (("a1", 1, 0), ("a2", 4, 1)):
                r = modrow[:, at * D:(at + 1) * D]
                dve.scalar_tensor_tensor(out=r, in0=r, scalar=1.0, in1=grow[:, g, :], op0=ALU.add, op1=ALU.mult
                                         ).then_inc(*S["mod_rows"].mark(name))
            dve.wait_ge(*S["mod_cols"].at(0))
            dve.tensor_copy(modT[:].rearrange("p a k s -> p (a k s)"), wide[0][:, 0:4 * KD]).then_inc(*S["modT_ready"].mark(0))

            chain = S["pick"]

            def pick_step(tile, q, p=None, where=None):
                if p is None:
                    p, where = tile % 2, pick_at[0 if tile == 1 else 1]
                scr, oneh = where
                count = [5 * q if q < HP else 5 * HP + 6 * (q - HP) if q < HP + PH else
                         CHAIN - sum(FINISH[q - HP - PH:])]

                def after(scan=False):
                    if count[0]:
                        dve.wait_ge(chain.sem, tile * CHAIN + count[0])
                        if scan and not isinstance(tile, int):
                            dve.sem_inc(S["x_pace"].sem)

                def done(ins):
                    count[0] += 1
                    ins.then_inc(chain.sem, 1)

                def top16(src, vals, places):
                    done(dve.max(vals[:, 0:8], src))
                    after(scan=True)
                    done(dve.max_index(places[:, 0:8], vals[:, 0:8], src))
                    after(scan=True)
                    done(dve.match_replace(src, vals[:, 0:8], src, NEG))
                    after(scan=True)
                    done(dve.max(vals[:, 8:16], src))
                    after(scan=True)
                    done(dve.max_index(places[:, 8:16], vals[:, 8:16], src))

                def keys(hp):
                    if isinstance(tile, int) and tile != 1:
                        dve.wait_ge(*S["own_scores"].at((tile // 2, hp)))
                    elif hp == 0:
                        if isinstance(tile, int) and tile == 1:
                            dve.wait_ge(S["scr1_in"].sem, 16)
                        else:
                            dve.wait_ge(S["scr_in"].sem, (tile - 2) * 16)
                        dve.sem_inc(S["x_pace"].sem)
                    top16(scr[:, hp * NKEYS:(hp + 1) * NKEYS], sv[:, hp * TOPK:(hp + 1) * TOPK],
                          si[:, hp * TOPK:(hp + 1) * TOPK])

                def head(h):
                    after()
                    va, vb = (sv[:, (2 * h + r) * TOPK:(2 * h + r + 1) * TOPK] for r in range(2))
                    cd = cand[h % 2]
                    done(dve.tensor_tensor(cd.rearrange("p (a b) -> p a b", b=TOPK),
                                           va.unsqueeze(2).to_broadcast([P, TOPK, TOPK]),
                                           vb.unsqueeze(1).to_broadcast([P, TOPK, TOPK]), ALU.add))
                    after(scan=True)
                    top16(cd, ts[:, h * TOPK:(h + 1) * TOPK], pos[:, h * TOPK:(h + 1) * TOPK])

                t3 = ts.rearrange("p (h k) -> p h k", k=TOPK)
                g3 = ge.rearrange("p (h k) -> p h k", k=TOPK)
                o3 = oneh.rearrange("p (j a) -> p j a", a=TOPK)
                o4 = oneh.rearrange("p (h k a) -> p h k a", k=TOPK, a=TOPK)

                def mark_place(r):
                    after()
                    done(dve.tensor_tensor(o3, pf[r].unsqueeze(2).to_broadcast([P, SLOTS, TOPK]),
                                           iota16[:].unsqueeze(1).to_broadcast([P, SLOTS, TOPK]), ALU.is_equal))

                def take_key(r):
                    after()
                    s4 = sf.rearrange("p (h r a) -> p h r a", r=2, a=TOPK)[:, :, r:r + 1, :]
                    done(dve.tensor_tensor(o4, o4, s4.to_broadcast([P, PH, TOPK, TOPK]), ALU.mult))

                def sum_key(r):
                    after()
                    done(dve.tensor_reduce(pi[r], o3, AX.X, ALU.add))

                def finish(part):
                    if part == 0:
                        after()
                        dve.tensor_tensor(g3, t3, t3[:, :, 0:1].to_broadcast([P, PH, TOPK]), ALU.subtract
                                          ).then_inc(S["gexp_in"].sem, 1)
                        done(dve.tensor_copy(sf, si))
                        done(dve.tensor_scalar(pab[0], pos, 4, None, ALU.logical_shift_right))
                        done(dve.tensor_scalar(pab[1], pos, 15, None, ALU.bitwise_and))
                        after()
                        for r in range(2):
                            done(dve.tensor_copy(pf[r], pab[r]))
                    elif part == 1:
                        mark_place(0)
                        take_key(0)
                    elif part == 2:
                        sum_key(0)
                        mark_place(1)
                    elif part == 3:
                        take_key(1)
                        sum_key(1)
                    else:
                        after()
                        done(dve.scalar_tensor_tensor(out=idx[p][:], in0=pi[0], scalar=float(NKEYS), in1=pi[1],
                                                      op0=ALU.mult, op1=ALU.add))
                        dve.wait_ge(S["gexp"].sem, tile + 1)
                        done(dve.tensor_reduce(gsum, g3, AX.X, ALU.add))
                        after()
                        done(dve.reciprocal(gsum, gsum))
                        after()
                        done(dve.tensor_tensor(gate[p].rearrange("p (h k) -> p h k", k=TOPK), g3,
                                               gsum.unsqueeze(2).to_broadcast([P, PH, TOPK]), ALU.mult))
                        after()
                        dve.sem_inc(S["idx_ready"].sem)

                n0 = count[0]
                if q < HP:
                    keys(q)
                elif q < HP + PH:
                    head(q - HP)
                else:
                    finish(q - HP - PH)
                assert count[0] - n0 == (5 if q < HP else 6 if q < HP + PH else FINISH[q - HP - PH])

            def early(s, phase, n):
                c = hook(s, phase, n)
                if c >= 0:
                    early_sums(c - 1)
                    early_dots(c)

            def early_sums(c):
                for k in range(EC * c, EC * c + EC):
                    if c < 0 or not vector_sums(k):
                        continue
                    t_, r_ = k // SLOTS, k % ERING
                    dve.wait_ge(*used_e(k - 1))
                    dve.wait_ge(*S["weight_e"].at(k))
                    dve.scalar_tensor_tensor(out=wide[t_][:], in0=ring_e[r_][:, D:2 * D], scalar=wts_e[:, r_:r_ + 1],
                                             in1=wide[t_][:], op0=ALU.mult, op1=ALU.add).then_inc(*S["used_v"].mark(k))

            def early_dots(c):
                if c >= EARLY:
                    return
                if c == 0:
                    dve.wait_ge(*S["h2e_in"].at(0))
                for k in range(EC * c, EC * c + EC):
                    r_ = k % ERING
                    dve.wait_ge(*landed_e[r_].at(k))
                    if k >= ERING:
                        dve.wait_ge(*S["gelu_e"].at((k - ERING) // EC))
                    dve.tensor_tensor_reduce(out=ring_e[r_][:, 0:D], in0=ring_e[r_][:, 0:D], in1=h2e[k // SLOTS], scale=1.0,
                                             scalar=0.0, op0=ALU.mult, op1=ALU.add, accum_out=dots_e[:, r_:r_ + 1]
                                             ).then_inc(*S["dot_e"].mark(k))
                for q in share(c, 0, SPAN_1):
                    pick_step(1, q)

            def norm2(s, t):
                b, tb, n = [k for k in stream_blocks(s) if k[1] <= t][-1]
                if t == tb:
                    dve.wait_ge(*S["std2"].at(b))
                    dve.reciprocal(rs[:, 1, tb:tb + n], rs[:, 1, tb:tb + n]).then_inc(*S["rstd2"].mark(b))
                    dve.wait_ge(*S["rstd2"].at(b))
                h2, first = hb[t % HB], STREAMS[s][0]
                if t >= first + HB:
                    dve.wait_ge(*S["bank_full"].at(("hT1", t - HB)))
                    dve.wait_ge(*S[f"h2_out{t % HB}"].at(t - HB))
                elif s == 0:
                    dve.wait_ge(*S["state_out"].at(s))
                dve.scalar_tensor_tensor(out=h2, in0=X1[:, t - first, :], scalar=rs[:, 1, t:t + 1],
                                         in1=a2b, op0=ALU.mult, op1=ALU.mult).then_inc(*S["h2_pre"].mark(t))
                dve.wait_ge(*S["h2_pre"].at(t))
                dve.tensor_tensor(h2, h2, shift2b, ALU.add).then_inc(*S["h2_ready"].mark(t))

            def residual(p, tile):
                dve.tensor_tensor(gate2b[p], wide[p][:], gate2b[p], ALU.mult).then_inc(S["y_pre"].sem, 1)
                dve.wait_ge(S["y_pre"].sem, tile * 2 + 1)
                dve.tensor_tensor(x1b[p], x1b[p], gate2b[p], ALU.add).then_inc(S["y_pre"].sem, 1)

            def normalised(p, tile):
                dve.wait_ge(S["y_std"].sem, tile + 1)
                dve.reciprocal(frs[:, p:p + 1], frs[:, p:p + 1]).then_inc(S["y_std_done"].sem, 1)
                dve.wait_ge(S["y_std_done"].sem, tile + 1)
                dve.scalar_tensor_tensor(out=x1b[p], in0=x1b[p], scalar=frs[:, p:p + 1], in1=finalb,
                                         op0=ALU.mult, op1=ALU.mult).then_inc(S["y_ready"].sem, 1)

            for s, (t0, t1) in enumerate(STREAMS):
                blocks = stream_blocks(s)
                L = (t1 - t0) * P
                for t in range(t0, t1 + 1):
                    if t < t1:
                        dve.wait_ge(*S["std_ready"].at(t))
                        dve.reciprocal(rs[:, 0, t:t + 1], rs[:, 0, t:t + 1]).then_inc(*S["rstd"].mark(t))
                        dve.wait_ge(*S["rstd"].at(t))
                        dve.tensor_scalar(xb[t % 2], xb[t % 2], rs[:, 0, t:t + 1], None, ALU.mult).then_inc(*S["xn_ready"].mark(t))
                    if t > t0:
                        u = t - 1
                        bk = wait_full(("xT1", u))
                        if u == 0:
                            dve.wait_ge(*S["modT_ready"].at(0))
                        for k in range(4, KD):
                            ins = dve.tensor_scalar(hT[:, k, (u - t0) * P:(u - t0 + 1) * P], bk[:, (k - 4) * P:(k - 3) * P],
                                                    modT[:, 1, k, s:s + 1], modT[:, 0, k, s:s + 1], ALU.mult, ALU.add)
                        drained(ins, ("xT1", u))
                        if s == 1:
                            for q in share(u - t0, HP, t1 - t0):
                                if q < PICK_STEPS - 1:
                                    pick_step(0, q)
                if s == 1:
                    pick_step(0, PICK_STEPS - 1)
                n_ = 0
                for m in range(CM):
                    for b, tb, n in blocks:
                        early(s, "conv", 2 * n_)
                        bk = wait_full(("ca", m, b))
                        dve.wait_ge(*S["bank_act"].at(("cb", m, b)))
                        drained(dve.tensor_tensor(U[:, m, (tb - t0) * P:(tb - t0 + n) * P], bk[:, 0:n * P],
                                                  sgt[n_ % 2][:, 0:n * P], ALU.mult), ("ca", m, b))
                        early(s, "conv", 2 * n_ + 1)
                        n_ += 1
                dve.wait_ge(*S["bank_dve"].at(("ca", CM - 1, blocks[-1][0])))
                offsets = [0] + [d for k in range(1, PAD + 1) for d in (-k, k)]
                for j, d in enumerate(offsets):
                    for m in range(CM):
                        w = cw[:, m, d + PAD:d + PAD + 1]
                        if j:
                            dve.wait_ge(*S["tap_done"].at((s, m, j - 1)))
                        if s == 0:
                            lo, hi = max(0, -d), min(L, L - d)
                            o, x = C[:, m, lo:hi], U[:, m, lo + d:hi + d]
                        elif m < CM // 2:
                            lo, hi = max(0, -d), min(GRID, GRID - d)
                            g_ = lambda r: r[:, m, 0:L].rearrange("p (r c) -> p r c", c=GRID)
                            o, x = g_(C)[:, :, lo:hi], g_(U)[:, :, lo + d:hi + d]
                        else:
                            lo, hi = max(0, -d) * GRID, min(L, L - d * GRID)
                            o, x = C[:, m, lo:hi], U[:, m, lo + d * GRID:hi + d * GRID]
                        if j == 0:
                            dve.tensor_scalar(o, x, w, cvv[:, 0, m:m + 1], ALU.mult, ALU.add
                                              ).then_inc(*S["tap_done"].mark((s, m, j)))
                        else:
                            dve.scalar_tensor_tensor(out=o, in0=x, scalar=w, in1=o, op0=ALU.mult, op1=ALU.add
                                                     ).then_inc(*S["tap_done"].mark((s, m, j)))
                        taps_done = j * CM + m + 1
                        if taps_done * 25 // (TAPS * CM) > (taps_done - 1) * 25 // (TAPS * CM):
                            early(s, "qk", taps_done * 25 // (TAPS * CM) - 1)
                for t in range(t0, t1):
                    dve.wait_ge(*S["bank_act"].at(("g", t)))
                    dve.tensor_tensor(SG[:, t - t0, :], SG[:, t - t0, :], gnb[:], ALU.mult).then_inc(*S["sg_ready"].mark(t))
                for j, (b, tb, n) in enumerate(blocks):
                    cols_ = slice((tb - t0) * P, (tb - t0 + n) * P)
                    bk = wait_full(("ln1", b))
                    for m in range(CM):
                        ins = dve.tensor_tensor(C[:, m, cols_], C[:, m, cols_], bk[:, 0:n * P], ALU.subtract)
                    drained(ins, ("ln1", b))
                    early(s, "ln", 4 * j)
                    dve.wait_ge(*S["bank_act"].at(("ln2", b)))
                    dve.reciprocal(rsb[:, 0:n * P], rsb[:, 0:n * P]).then_inc(*S["ln_rstd"].mark(b))
                    dve.wait_ge(*S["ln_rstd"].at(b))
                    for m in range(CM):
                        ins = dve.tensor_tensor(C[:, m, cols_], C[:, m, cols_], rsb[:, 0:n * P], ALU.mult)
                    ins.then_inc(*S["ln_scaled"].mark(b))
                    for q in range(1, 4):
                        early(s, "ln", 4 * j + q)
                nt = t1 - t0
                for d in range(2):
                    for pair in range(PAIRS):
                        key, dp = (s, d, pair), 2 * d + pair
                        z, l, x = TMP[:, 0, 0:L], TMP[:, 1, 0:L], TMP[:, 2, 0:L]
                        xc, lc = (r.rearrange("p (c n) -> p c n", n=P) for r in (x, l))
                        ci = colsin[:, dp, :, 0:nt]
                        early(s, "gates", 4 * d + 2 * pair)
                        dve.wait_ge(*S["softplus"].at((*key, 1)))
                        dve.scalar_tensor_tensor(out=z, in0=z, scalar=0.0, in1=l, op0=ALU.min, op1=ALU.subtract
                                                 ).then_inc(*S["g_ready"].mark(key))
                        dve.wait_ge(*S["g_ready"].at(key))
                        for c in range(nt):
                            cc = slice(c * P, (c + 1) * P)
                            ins = dve.tensor_tensor_scan(l[:, cc], one[:], z[:, cc], 0.0, ALU.mult, ALU.add)
                        ins.then_inc(*S["scan"].mark(key))
                        dve.wait_ge(*S["scan"].at(key))
                        if d == 0:
                            mid = lc[:, :, P // 2 - 1:P // 2]
                            end = lc[:, :, P - 1]
                            dve.tensor_copy(ci[:, 0, :], mid.rearrange("p c n -> p (c n)"))
                            dve.tensor_copy(ci[:, 1, :], end)
                            dve.tensor_tensor(ci[:, 2, :], end, mid.rearrange("p c n -> p (c n)"), ALU.subtract)
                            dve.tensor_tensor(xc, lc, mid.to_broadcast([P, nt, P]), ALU.subtract
                                              ).then_inc(*S["cols_in"].mark(key))
                        else:
                            dve.tensor_tensor(z, z, l, ALU.subtract).then_inc(*S["span"].mark(key))
                            dve.wait_ge(*S["span"].at(key))
                            zc = z.rearrange("p (c n) -> p c n", n=P)
                            mid = zc[:, :, P // 2:P // 2 + 1]
                            end = lc[:, :, P - 1]
                            dve.tensor_tensor(ci[:, 0, :], end, mid.rearrange("p c n -> p (c n)"), ALU.add)
                            dve.tensor_copy(ci[:, 1, :], end)
                            dve.tensor_scalar(ci[:, 2, :], mid.rearrange("p c n -> p (c n)"), -1.0, None, ALU.mult)
                            dve.tensor_tensor(xc, zc, mid.to_broadcast([P, nt, P]), ALU.subtract
                                              ).then_inc(*S["cols_in"].mark(key))
                        Q_, K_ = (QF, KF) if d == 0 else (QK, QK[:, 2:4, :])
                        dve.wait_ge(*S["exps"].at((*key, 0)))
                        if d == 0:
                            dve.wait_ge(*S["bank_full"].at(("g", t1 - 1)))
                        dve.tensor_tensor(K_[:, pair, 0:L], QK[:, 2 + pair, 0:L], TMP[:, 3, 0:L], ALU.mult
                                          ).then_inc(*S["qk_scaled"].mark((*key, 0)))
                        dve.wait_ge(*S["exps"].at((*key, 1)))
                        dve.tensor_tensor(Q_[:, pair, 0:L], QK[:, pair, 0:L], TMP[:, 2, 0:L], ALU.mult
                                          ).then_inc(*S["qk_scaled"].mark((*key, 1)))
                        early(s, "gates", 4 * d + 2 * pair + 1)
                if s == 0:
                    dve.wait_ge(*S["bank_full"].at(("xT1", t1 - 1)))
                    for dp in range(4):
                        dve.memset(Scur[dp], 0.0).then_inc(*S["st_next"].mark((s, -1, dp)))
                else:
                    dve.wait_ge(*S["state_in"].at(s))
                last = nt if s == 0 else nt - 1
                dve.wait_ge(*S["cols_ready"].at((s, 1, 1)))
                dve.wait_ge(*S["qk_scaled"].at((s, 1, PAIRS - 1, 1)))
                for d in range(2):
                    dve.memset(ST[d][:, 0:nt].rearrange("p c d n -> p (c d n)"), 0.0).then_inc(*S["st_zero"].mark(s))
                dve.wait_ge(*S["st_zero"].at(s))
                for i in range(nt):
                    for dp in range(4):
                        c = i if dp < 2 else nt - 1 - i
                        T_ = cols[:, dp, 1, c:c + 1]
                        if i or s == 0:
                            dve.wait_ge(*S["st_next"].at((s, i - 1, dp)))
                        for r in range(2):
                            h = slice(r * HK, (r + 1) * HK)
                            ins = dve.tensor_scalar(ST[dp // 2][h, c, dp % 2, r * HV:(r + 1) * HV], Scur[dp][h, :],
                                                    cols[h, dp, 0, c:c + 1], None, ALU.mult)
                        ins.then_inc(*S["st_kept"].mark((s, i, dp)))
                        if i < last:
                            dve.tensor_scalar(Stmp[dp], Scur[dp], T_, None, ALU.mult).then_inc(*S["st_tmp"].mark((s, i, dp)))
                    if i < last:
                        early(s, "states", 2 * i)
                        for dp in range(4):
                            c = i if dp < 2 else nt - 1 - i
                            bk = wait_full(("st", s, i, dp))
                            dve.wait_ge(*S["st_tmp"].at((s, i, dp)))
                            dve.wait_ge(*S["st_kept"].at((s, i, dp)))
                            for r in range(2):
                                h = slice(r * HK, (r + 1) * HK)
                                ins = dve.scalar_tensor_tensor(out=Scur[dp][h, :], in0=bk[h, r * HV:(r + 1) * HV],
                                                               scalar=cols[h, dp, 2, c:c + 1], in1=Stmp[dp][h, :],
                                                               op0=ALU.mult, op1=ALU.add)
                                if r == 0:
                                    ins.then_inc(*S["st_next"].mark((s, i, dp, "half")))
                                else:
                                    ins.then_inc(*S["st_next"].mark((s, i, dp)))
                        early(s, "states", 2 * i + 1)
                def normalise(c):
                    t = t0 + c
                    dve.wait_ge(*S["ostd"].at(t))
                    dve.reciprocal(ors[:, t, :], ors[:, t, :]).then_inc(*S["orstd"].mark(t))
                    dve.wait_ge(*S["orstd"].at(t))
                    dve.wait_ge(*S["sg_ready"].at(t))
                    bk = bank_of[("o", t)]
                    for h in range(HEADS):
                        hc = slice(h * HV, (h + 1) * HV)
                        ins = dve.scalar_tensor_tensor(out=SG[:, c, hc], in0=bk[:, hc], scalar=ors[:, t, h:h + 1],
                                                       in1=SG[:, c, hc], op0=ALU.mult, op1=ALU.mult)
                    ins.then_inc(*S["og"].mark(t))

                for c in range(nt + 1):
                    if c < nt:
                        for odd in range(2):
                            bk = wait_full(("scf", odd, t0 + c))
                            dve.wait_ge(*S["bank_act"].at(("scb", odd, t0 + c)))
                            drained(dve.copy_predicated(by_head(sct(c), odd), keep_f[:, 0:2, :],
                                                        bk[:, 0:2 * P].rearrange("p (a n) -> p a n", n=P)),
                                    ("scf", odd, t0 + c))
                        dve.wait_ge(*S["bank_dve"].at(("scf", 1, t0 + c)))
                        dve.tensor_tensor(sct(c), sct(c), twice_d[:].rearrange("p h n -> p (h n)"), ALU.mult
                                          ).then_inc(*S["scT"].mark(t0 + c))
                    if c:
                        normalise(c - 1)
                    early(s, "attn", c)
                early(s, "attn", nt + 1)
                dve.wait_ge(*S["bc_in"].at(s))
                dve.wait_ge(*S["x1_in"].at(s))
                n_ = 0
                for half in range(2):
                    hc = slice(half * 512, (half + 1) * 512)
                    for t in range(t0, t1):
                        bk = wait_full(("out", half, t))
                        tmp = TMP[:, n_ % 2, 0:512]
                        drained(dve.tensor_tensor(tmp, bk[:], gate1b[:, hc], ALU.mult), ("out", half, t))
                        dve.wait_ge(*S["bank_dve"].at(("out", half, t)))
                        dve.tensor_tensor(X1[:, t - t0, hc], X1[:, t - t0, hc], tmp, ALU.add).then_inc(*S["x1_ready"].mark((half, t)))
                        if s == 1 and n_ >= 12:
                            norm2(s, t - 4)
                        early(s, "out", n_)
                        n_ += 1
                for j, (b, tb, n) in enumerate(blocks):
                    if s == 0:
                        for t in range(t0, t1):
                            norm2(s, t)
                    for t in range(tb, tb + n):
                        bk = wait_full(("hT1", t))
                        if b > blocks[0][0]:
                            dve.wait_ge(*S["bank_full"].at(("qf", b - 1, HP - 1)))
                        cc = slice((t - tb) * P, (t - tb + 1) * P)
                        drained(dve.tensor_copy(H2T[:, 4:8, cc], bk[:].rearrange("p (k n) -> p k n", k=4)), ("hT1", t))
                    for hp in range(HP):
                        bk = wait_full(("sc", b, hp))
                        quad = hp // 4
                        if hp % 4 == 0:
                            if quad >= 2:
                                dve.wait_ge(*S[f"sc_out{quad % 2}"].at((b, quad - 2)))
                            elif b > 0:
                                dve.wait_ge(*S[f"sc_out{quad % 2}"].at((b - 1, quad + 2)))
                        drained(dve.tensor_copy(scb[quad % 2][:, 0:n, hp % 4, :],
                                                bk[:, 0:n * P].rearrange("p (t n) -> p t n", n=NKEYS)), ("sc", b, hp))
                        if b < 2:
                            own = scb[quad % 2][:, 0, hp % 4, :]
                            dve.wait_ge(*S["bank_dve"].at(("sc", b, hp)))
                            dve.tensor_copy(pick_at[1][0][:, hp * NKEYS:(hp + 1) * NKEYS], own
                                            ).then_inc(*S["own_scores"].mark((b, hp)))
                            if hp:
                                pick_step(tb, hp - 1)
                        if b == 1 and hp % 3 == 2 and hp < 12:
                            norm2(s, tb + n + hp // 3)
                        early(s, f"qf{j}", hp)
                        if b < 2 and hp == HP - 1:
                            pick_step(tb, hp)
                        if b == 2:
                            for q in share(hp, HP, SPAN_2):
                                pick_step(2, q)
                            if hp == HP - 2:
                                dve.wait_ge(*S["final_in"].at(0))
                                dve.wait_ge(*used_e(SLOTS - 1))
                                dve.wait_ge(*S["tile_in0"].at(0))
                                residual(0, 0)

            dve.wait_ge(*S["dot_e"].at(2 * SLOTS - 1))
            dve.sem_inc(S["dot"].sem, SLOTS)
            normalised(0, 0)
            with dve.Fori(0, NT // 2 - 1) as i:
                for p in range(2):
                    tile = i * 2 + p + 2
                    dve.wait_ge(S[f"h2_in{p}"].sem, i * 16 + 16)
                    dve.sem_inc(S["x_pace"].sem)
                    for n in range(SLOTS // GROUP):
                        g, j = n * GROUP // RING, n * GROUP % RING
                        for r in range(j, j + GROUP):
                            dve.wait_ge(landed[r], i * (32 * SLOTS // RING) + (p * SLOTS // RING + g + 1) * 16)
                            dve.tensor_tensor_reduce(out=ring[r][:, 0:D], in0=ring[r][:, 0:D], in1=h2b[p], scale=1.0,
                                                     scalar=0.0, op0=ALU.mult, op1=ALU.add, accum_out=dots[:, r:r + 1]
                                                     ).then_inc(S["dot"].sem, 1)
                        for q in unit_share(n):
                            pick_step(tile + 1, q, 1 - p, pick_at[1])
                        dve.wait_ge(S["gelu"].sem, i * (2 * SLOTS // GROUP) + p * (SLOTS // GROUP) + n + 1)
                        dve.tensor_tensor(wts[:, j:j + GROUP], gel[:, j:j + GROUP],
                                          gate[p][:, n * GROUP:(n + 1) * GROUP], ALU.mult).then_inc(S["weight"].sem, 1)
                        if n == ROOT_UNIT:
                            dve.wait_ge(S["slot_used"].sem, i * (2 * SLOTS) + p * SLOTS + RING)
                            dve.wait_ge(S[f"tile_in{1 - p}"].sem, i * 32 + (p + 1) * 32)
                            residual(1 - p, tile - 1)
                        if n == ROOT_UNIT + 1:
                            normalised(1 - p, tile - 1)
            dve.wait_ge(S["slot_used"].sem, (NT - 2) * SLOTS + RING)
            dve.wait_ge(S["tile_in1"].sem, 32 * NT // 2)
            residual(1, NT - 1)
            normalised(1, NT - 1)


FINISH = (5, 2, 2, 2, 4)
CHAIN = 5 * HP + 6 * PH + sum(FINISH)
PICK_STEPS = HP + PH + len(FINISH)
SPAN_1 = 16
SPAN_2 = 14
FIRST_UNIT = 2
EXP_UNIT = FIRST_UNIT + HP // 2 + PH
ROOT_UNIT = 0


def share(n, first, span):
    left = PICK_STEPS - first
    return range(first + n * left // span, first + (n + 1) * left // span) if n < span else ()


def unit_share(n):
    n -= FIRST_UNIT
    if n < 0:
        return ()
    if n < HP // 2:
        return range(2 * n, 2 * n + 2)
    return range(n + HP // 2, min(n + HP // 2 + 1, PICK_STEPS))


def kernel(**inputs):
    import numpy as np
    import concourse.bacc as _bacc
    from concourse.bass_utils import run_bass_kernel_spmd as _run

    f = {k: np.asarray(v) for k, v in inputs.items()}

    def by_partition(w, parts):
        return w.reshape(parts, P, -1).transpose(1, 0, 2)

    w_in = by_partition(f["w_in"][0], KD)
    col_at = [0, DK, 2 * DK, 2 * DK + DV, 2 * DK + 2 * DV, 2 * DK + 2 * DV + 2 * RANK]
    ca0 = col_at[5]
    cb0 = ca0 + CH
    starts = [0, P, DK, DK + P] + [ca0 + m * P for m in range(CM)] + [cb0 + m * P for m in range(CM)]
    w_vg = []
    for c0 in (2 * DK, 2 * DK + DV):
        for c in range(4):
            w_vg.append(w_in[:, 2 * c:2 * c + 2, c0:c0 + DV].reshape(P, D))
    w_up = np.zeros((2 * RANK, 2, DK), np.float32)
    w_up[0:RANK, 0] = f["w_af_up"][0]
    w_up[RANK:, 1] = f["w_ab_up"][0]
    pw2 = by_partition(f["conv_pw2"][0], CM)
    w_out = by_partition(f["w_out"][0], KD)
    wq = by_partition(f["peer_wq"][0], KD)
    ins = {
        "x": np.concatenate([f["x_prompt"][0], f["x_sample"][0]], axis=0),
        "c2": np.stack([f["c_ctx"], f["c"][0]], axis=1).reshape(KD, P, 2).transpose(1, 0, 2),
        "w_mod": by_partition(f["w_mod"][0], KD).reshape(P, KD, 12, 512).transpose(2, 0, 1, 3),
        "b_mod": f["b_mod"],
        "norm1_g": f["norm1_g"], "norm2_g": f["norm2_g"],
        "w_cols": np.stack([w_in[:, :, c:c + P].reshape(P, D) for c in starts]),
        "w_af": w_in[:, :, col_at[4]:col_at[4] + 2 * RANK].reshape(P, KD * 2 * RANK),
        "w_vg": np.stack(w_vg),
        "w_up": w_up,
        "b_up": np.stack([f["b_af"][0], f["b_ab"][0]]).reshape(2, PAIRS, P).transpose(2, 0, 1),
        "gla_g": f["gla_norm_g"][0],
        "conv_w": f["conv_dw_w"][0].T.reshape(CM, P, TAPS).transpose(1, 0, 2),
        "conv_v": np.stack([f["conv_dw_b"][0], f["conv_ln_g"][0], f["conv_ln_b"][0]]).reshape(3, CM, P).transpose(2, 0, 1),
        "w_pw2": np.stack([pw2[:, 2 * c:2 * c + 2].reshape(P, D) for c in range(2)]),
        "w_out": np.stack([w_out[:, 2 * c:2 * c + 2, h * 512:(h + 1) * 512].reshape(P, D) for h in range(2) for c in range(4)]),
        "w_q": np.stack([wq[:, :, m * P:(m + 1) * P].reshape(P, D) for m in range(HP)]),
        "sk": f["peer_subkeys"][0].reshape(HP, NKEYS, P).transpose(2, 0, 1),
        "uv": np.concatenate([f["peer_u"][0], f["peer_v"][0]], axis=1),
        "final_g": f["final_norm_g"],
        "state_f": f["state_gla_fwd"].reshape(DK, HV),
        "state_b": f["state_gla_bwd"].reshape(DK, HV),
    }
    ins = {k: np.ascontiguousarray(v) for k, v in ins.items()}

    def program(counts):
        nc = _bacc.Bacc("TRN2", target_bir_lowering=False, num_devices=1)
        a = {k: nc.dram_tensor(f"in_{k}", v.shape, F32, kind="ExternalInput").ap() for k, v in ins.items()}
        for k, shape in (("y", (NT * P, D)), ("new_f", (DK, HV)), ("new_b", (DK, HV))):
            a[k] = nc.dram_tensor(f"out_{k}", shape, F32, kind="ExternalOutput").ap()
        build(nc, a, counts)
        return nc

    counts = {}
    program(counts)
    nc = program(counts)
    r = _run(nc, [{f"in_{k}": v for k, v in ins.items()}], core_ids=[0]).results[0]
    y = r["out_y"]
    state = (1, 1, HEADS, HK, HV)
    n0 = STREAMS[0][1] * P
    return (y[None, :n0], y[None, n0:], r["out_new_f"].reshape(state), r["out_new_b"].reshape(state))
```
